# Optimizing a Trainium2 kernel written in Bass

```python
import jax, jax.numpy as jnp
from jax import lax
import numpy as np

D_MODEL = 1024
BATCH = 1
SEQ = 512
DEPTH = 2
DEC_BATCH = 8
DEC_SEQ = 8
PAST_LEN = 256
PAGE_SIZE = 128

POOL_WIDTH = D_MODEL // 4
POOL_WINDOWS = (2, 4, 8, 16)
POOL_GROUP_W = POOL_WIDTH // len(POOL_WINDOWS)
POOL_KEEP = max(POOL_WINDOWS) - 1
GMLP_WIDTH = D_MODEL // 4
GMLP_GROUPS = 4
GMLP_GROUP_W = GMLP_WIDTH // GMLP_GROUPS
CHUNK = 128
N_HEADS = 8
HEAD_DIM = 64
N_KV_HEADS = 2
GQA = N_HEADS // N_KV_HEADS
NSA_WIDTH = N_HEADS * HEAD_DIM
ROT_DIM = HEAD_DIM // 4
ROPE_THETA = 500000.0
CMP_LEN = 32
CMP_STRIDE = 16
CMP_HIDDEN = 2 * HEAD_DIM
SEL_LEN = 64
SEL_TOPN = 16
WINDOW = 512
Q_BLOCK = 128
N_EXPERTS = 16
N_EXPERT_GROUPS = 4
EXPERTS_PER_GROUP = N_EXPERTS // N_EXPERT_GROUPS
TOP_K = 2
D_EXPERT = D_MODEL // 4
DN_ALPHA = (2 * DEPTH) ** 0.25
DN_BETA = (8 * DEPTH) ** -0.25
LN_EPS = 1e-5
NEG_INF = -1e30
FORCE = 1e9
IN_SPLITS = (POOL_WIDTH, GMLP_WIDTH, GMLP_WIDTH, NSA_WIDTH, 6 * N_KV_HEADS * HEAD_DIM, 3 * N_HEADS, 3 * D_MODEL)
IN_WIDTH = sum(IN_SPLITS)

kernel_name = "hybrid_pool_gmlp_nsa_moe_step"

def split_points():
    pts, acc = [], 0
    for w in IN_SPLITS[:-1]:
        acc += w
        pts.append(acc)
    return pts

def layer_norm(x, g, b):
    xf = x.astype(jnp.float32)
    mu = jnp.mean(xf, -1, keepdims=True)
    var = jnp.mean(jnp.square(xf - mu), -1, keepdims=True)
    y = (xf - mu) * lax.rsqrt(var + LN_EPS) * g.astype(jnp.float32) + b.astype(jnp.float32)
    return y.astype(x.dtype)

def masked_softmax(s, mask):
    s = jnp.where(mask, s.astype(jnp.float32), NEG_INF)
    p = jnp.where(mask, jnp.exp(s - jnp.max(s, -1, keepdims=True)), 0.0)
    d = jnp.sum(p, -1, keepdims=True)
    return p / jnp.where(d > 0, d, 1.0)

def partial_rope(x, pos):
    half = ROT_DIM // 2
    inv = 1.0 / (ROPE_THETA ** (jnp.arange(half, dtype=jnp.float32) / half))
    ang = pos.astype(jnp.float32)[:, None] * inv[None, :]
    cos = jnp.cos(ang)[None, :, None, :]
    sin = jnp.sin(ang)[None, :, None, :]
    xr = x[..., :ROT_DIM].astype(jnp.float32)
    x1, x2 = xr[..., :half], xr[..., half:]
    rot = jnp.concatenate([x1 * cos - x2 * sin, x2 * cos + x1 * sin], -1)
    return jnp.concatenate([rot.astype(x.dtype), x[..., ROT_DIM:]], -1)

def pool_mixer(a, buf, pos0, w, scale):
    n, t_new, _ = a.shape
    ext = a if buf is None else jnp.concatenate([buf.astype(a.dtype), a], 1)
    lb = ext.shape[1] - t_new
    maxw = max(POOL_WINDOWS)
    c = jnp.cumsum(jnp.pad(ext.astype(jnp.float32), ((0, 0), (maxw + 1, 0), (0, 0))), axis=1)
    e0 = maxw + lb + 1
    end = c[:, e0:e0 + t_new]
    pos = (pos0 + jnp.arange(t_new)).astype(jnp.float32)
    af = a.astype(jnp.float32)
    parts = []
    for gi, win in enumerate(POOL_WINDOWS):
        sl = slice(gi * POOL_GROUP_W, (gi + 1) * POOL_GROUP_W)
        total = end[..., sl] - c[:, e0 - win:e0 - win + t_new, sl]
        cnt = jnp.minimum(float(win), pos + 1.0)[None, :, None]
        parts.append(total / cnt - af[..., sl])
    d = jnp.stack(parts, axis=2)
    y = jnp.einsum('ntgc,gcd->ntgd', d, w.astype(jnp.float32)).reshape(n, t_new, POOL_WIDTH)
    y = y * scale.astype(jnp.float32)
    return y.astype(a.dtype), ext[:, -POOL_KEEP:]

def gmlp_mixer(u, v, ln_g, ln_b, ws, bs):
    n, t, _ = u.shape
    cl = min(CHUNK, t)
    nch = t // cl
    vn = layer_norm(v, ln_g, ln_b)
    causal = jnp.tril(jnp.ones((cl, cl), dtype=bool))
    wm = jnp.where(causal[None], ws[:, :cl, :cl], 0.0).astype(vn.dtype)
    vr = vn.reshape(n, nch, cl, GMLP_GROUPS, GMLP_GROUP_W)
    mix = jnp.einsum('gts,ncsgd->nctgd', wm, vr) + bs[:, :cl].T[None, None, :, :, None].astype(vn.dtype)
    return u * mix.reshape(n, t, GMLP_WIDTH), vn

def compress_blocks(x, pe, w1, b1, w2):
    n, l, h, d = x.shape
    nc = (l - CMP_LEN) // CMP_STRIDE + 1
    idx = np.arange(nc)[:, None] * CMP_STRIDE + np.arange(CMP_LEN)[None, :]
    blk = x[:, idx] + pe[None, None, :, None, :]
    blk = jnp.swapaxes(blk, 2, 3).reshape(n, nc, h, CMP_LEN * d)
    hid = jax.nn.gelu(blk @ w1 + b1)
    return hid @ w2

def selection_overlap(nc, nsb):
    i = np.arange(nc)[:, None]
    j = np.arange(nsb)[None, :]
    lo = np.maximum(i * CMP_STRIDE, j * SEL_LEN)
    hi = np.minimum(i * CMP_STRIDE + CMP_LEN, (j + 1) * SEL_LEN)
    return (np.maximum(hi - lo, 0) // CMP_STRIDE).astype(np.float32)

def sel_attention(qg, ks, vs, idx, qpos):
    n, l, h, d = ks.shape
    tq = qg.shape[1]
    nsb = -(-l // SEL_LEN)
    pad = nsb * SEL_LEN - l
    kb = jnp.pad(ks, ((0, 0), (0, pad), (0, 0), (0, 0))).reshape(n, nsb, SEL_LEN, h, d).transpose(0, 3, 1, 2, 4)
    vb = jnp.pad(vs, ((0, 0), (0, pad), (0, 0), (0, 0))).reshape(n, nsb, SEL_LEN, h, d).transpose(0, 3, 1, 2, 4)
    qb = min(Q_BLOCK, tq)
    nqb = tq // qb
    n_sel = idx.shape[-1]
    q_blocks = jnp.swapaxes(qg.reshape(n, nqb, qb, h, GQA, d), 0, 1)
    idx_blocks = idx.reshape(n, h, nqb, qb, n_sel).transpose(2, 0, 1, 3, 4)
    pos_blocks = qpos.reshape(nqb, qb)
    gather = jax.vmap(jax.vmap(lambda tbl, ix: tbl[ix]))

    def one_block(args):
        qq, ix, pp = args
        kg = gather(kb, ix)
        vg = gather(vb, ix)
        kpos = ix[..., None] * SEL_LEN + jnp.arange(SEL_LEN)
        mask = (kpos <= pp[None, None, :, None, None]).reshape(n, h, 1, qb, n_sel * SEL_LEN)
        s = jnp.einsum('nqhgd,nhqjsd->nhgqjs', qq, kg).reshape(n, h, GQA, qb, n_sel * SEL_LEN)
        p = masked_softmax(s, mask)
        return jnp.einsum('nhgqk,nhqkd->nqhgd', p.astype(vg.dtype), vg.reshape(n, h, qb, n_sel * SEL_LEN, d))

    o = lax.map(one_block, (q_blocks, idx_blocks, pos_blocks))
    return jnp.swapaxes(o, 0, 1).reshape(n, tq, h, GQA, d)

def window_banded(qg, kw, vw):
    n, t, h, g, d = qg.shape
    nqb = t // Q_BLOCK
    nw = WINDOW // Q_BLOCK
    kp = jnp.pad(kw, ((0, 0), (WINDOW, 0), (0, 0), (0, 0))).reshape(n, nqb + nw, Q_BLOCK, h, d)
    vp = jnp.pad(vw, ((0, 0), (WINDOW, 0), (0, 0), (0, 0))).reshape(n, nqb + nw, Q_BLOCK, h, d)
    nk = (nw + 1) * Q_BLOCK
    kband = jnp.stack([kp[:, i:i + nqb] for i in range(nw + 1)], axis=2).reshape(n, nqb, nk, h, d)
    vband = jnp.stack([vp[:, i:i + nqb] for i in range(nw + 1)], axis=2).reshape(n, nqb, nk, h, d)
    qb = qg.reshape(n, nqb, Q_BLOCK, h, g, d)
    s = jnp.einsum('nbqhgd,nbkhd->nhgbqk', qb, kband)
    qpos = jnp.arange(t).reshape(nqb, Q_BLOCK)
    kpos = jnp.arange(nqb)[:, None] * Q_BLOCK - WINDOW + jnp.arange(nk)[None, :]
    mask = (kpos[:, None, :] <= qpos[:, :, None]) & (kpos[:, None, :] > qpos[:, :, None] - WINDOW) & (kpos[:, None, :] >= 0)
    p = masked_softmax(s, mask[None, None, None])
    o = jnp.einsum('nhgbqk,nbkhd->nbqhgd', p.astype(vband.dtype), vband)
    return o.reshape(n, t, h, g, d)

def window_dense(qg, kw, vw, pos0):
    tq = qg.shape[1]
    lw = kw.shape[1]
    kpos = pos0 + tq - lw + jnp.arange(lw)
    qpos = pos0 + jnp.arange(tq)
    mask = (kpos[None, :] <= qpos[:, None]) & (kpos[None, :] > qpos[:, None] - WINDOW)
    s = jnp.einsum('nthgd,nkhd->nhgtk', qg, kw)
    p = masked_softmax(s, mask)
    return jnp.einsum('nhgtk,nkhd->nthgd', p.astype(vw.dtype), vw)

def nsa_mixer(q, kv_cmp, kv_sel, kv_win, gate_logits, pos0, pe, w1, b1, w2):
    n, tq = q.shape[:2]
    qpos = pos0 + jnp.arange(tq)
    qg = (q * (HEAD_DIM ** -0.5)).reshape(n, tq, N_KV_HEADS, GQA, HEAD_DIM)
    kc = compress_blocks(kv_cmp[:, :, 0], pe[0], w1[0], b1[0], w2[0])
    vc = compress_blocks(kv_cmp[:, :, 1], pe[1], w1[1], b1[1], w2[1])
    nc = kc.shape[1]
    cend = jnp.arange(nc) * CMP_STRIDE + CMP_LEN - 1
    cmask = cend[None, :] <= qpos[:, None]
    p_cmp = masked_softmax(jnp.einsum('nthgd,nchd->nhgtc', qg, kc), cmask)
    o_cmp = jnp.einsum('nhgtc,nchd->nthgd', p_cmp.astype(vc.dtype), vc)
    l = kv_sel.shape[1]
    nsb = -(-l // SEL_LEN)
    imp = jnp.einsum('nhgtc,cj->nhtj', p_cmp, jnp.asarray(selection_overlap(nc, nsb)))
    blk = jnp.arange(nsb)[None, :]
    cur = (qpos // SEL_LEN)[:, None]
    forced = (blk == 0) | (blk == cur) | (blk == cur - 1)
    score = jnp.where(forced, FORCE, jnp.where(blk <= cur, imp, -FORCE))
    _, idx = lax.top_k(score, min(SEL_TOPN, nsb))
    o_sel = sel_attention(qg, kv_sel[:, :, 0], kv_sel[:, :, 1], idx, qpos)
    if pos0 == 0 and kv_win.shape[1] == tq and tq % Q_BLOCK == 0:
        o_win = window_banded(qg, kv_win[:, :, 0], kv_win[:, :, 1])
    else:
        o_win = window_dense(qg, kv_win[:, :, 0], kv_win[:, :, 1], pos0)
    g = jax.nn.sigmoid(gate_logits.astype(jnp.float32)).reshape(n, tq, N_KV_HEADS, GQA, 3)
    o = g[..., 0:1] * o_cmp + g[..., 1:2] * o_sel + g[..., 2:3] * o_win
    return o.reshape(n, tq, NSA_WIDTH).astype(q.dtype)

def token_mixers(h, pos0, past, lw):
    n, t, _ = h.shape
    z = h @ lw['w_in']
    a, u, v, q, kv, nsa_g, merge_g = jnp.split(z, split_points(), axis=-1)
    pos = pos0 + jnp.arange(t)
    q = partial_rope(q.reshape(n, t, N_HEADS, HEAD_DIM), pos)
    kv = kv.reshape(n, t, 3, 2, N_KV_HEADS, HEAD_DIM)
    k = partial_rope(kv[:, :, :, 0].reshape(n, t, 3 * N_KV_HEADS, HEAD_DIM), pos).reshape(n, t, 3, N_KV_HEADS, HEAD_DIM)
    kv = jnp.stack([k, kv[:, :, :, 1]], axis=3)
    new_cmp, new_sel, new_win = kv[:, :, 0], kv[:, :, 1], kv[:, :, 2]
    if past is None:
        cmp_all, sel_all, win_all = new_cmp, new_sel, new_win
        keep = min(WINDOW, t)
        pool_buf = None
    else:
        cmp_all = jnp.concatenate([past['cmp'].astype(new_cmp.dtype), new_cmp], 1)
        sel_all = jnp.concatenate([past['sel'].astype(new_sel.dtype), new_sel], 1)
        win_all = jnp.concatenate([past['win'].astype(new_win.dtype), new_win], 1)
        keep = past['win'].shape[1]
        pool_buf = past['pool']
    o_nsa = nsa_mixer(q, cmp_all, sel_all, win_all, nsa_g, pos0, lw['cmp_pe'], lw['cmp_w1'], lw['cmp_b1'], lw['cmp_w2'])
    o_pool, pool_state = pool_mixer(a, pool_buf, pos0, lw['pool_w'], lw['pool_scale'])
    o_gmlp, v_rows = gmlp_mixer(u, v, lw['gmlp_ln_g'], lw['gmlp_ln_b'], lw['gmlp_ws'], lw['gmlp_bs'])
    gates = jax.nn.sigmoid(merge_g.astype(jnp.float32)).reshape(n, t, 3, D_MODEL)
    merged = (gates[:, :, 0] * (o_pool @ lw['w_branch_pool'])
              + gates[:, :, 1] * (o_gmlp @ lw['w_branch_gmlp'])
              + gates[:, :, 2] * (o_nsa @ lw['w_branch_nsa']))
    out = merged.astype(h.dtype) @ lw['w_out']
    return out, (new_cmp, new_sel, win_all[:, -keep:], pool_state, v_rows)

def moe_ffn(h, w_router, b_router, w_gate, w_up, w_down):
    n, t, _ = h.shape
    aff = jax.nn.sigmoid(jnp.einsum('ntd,de->nte', h.astype(jnp.float32), w_router.astype(jnp.float32)))
    score = aff + b_router.astype(jnp.float32)
    grp_top = lax.top_k(score.reshape(n, t, N_EXPERT_GROUPS, EXPERTS_PER_GROUP), TOP_K)[0]
    best = jnp.argmax(jnp.sum(grp_top, -1), -1)
    in_grp = (jnp.arange(N_EXPERTS) // EXPERTS_PER_GROUP)[None, None, :] == best[..., None]
    _, top_idx = lax.top_k(jnp.where(in_grp, score, NEG_INF), TOP_K)
    top_w = jnp.take_along_axis(aff, top_idx, -1)
    top_w = top_w / jnp.sum(top_w, -1, keepdims=True)
    combine = jnp.sum(jax.nn.one_hot(top_idx, N_EXPERTS, dtype=jnp.float32) * top_w[..., None], axis=-2)
    hg = jnp.einsum('ntd,edf->ntef', h, w_gate)
    hu = jnp.einsum('ntd,edf->ntef', h, w_up)
    act = jax.nn.silu(hg) * hu * combine[..., None].astype(h.dtype)
    return jnp.einsum('ntef,efd->ntd', act, w_down)

def trunk_layer(x, pos0, past, lw, w_router, b_router):
    m, st = token_mixers(x, pos0, past, lw)
    x = layer_norm(DN_ALPHA * x + m, lw['ln1_g'], lw['ln1_b'])
    f = moe_ffn(x, w_router, b_router, lw['w_gate'], lw['w_up'], lw['w_down'])
    x = layer_norm(DN_ALPHA * x + f, lw['ln2_g'], lw['ln2_b'])
    return x, st

def gather_pages(pool, page_table):
    g = pool[page_table]
    return g.reshape(g.shape[0], g.shape[1] * g.shape[2], *pool.shape[1:][1:])

def setup_inputs(seed: int = 0) -> dict:
    key = jax.random.key(seed)
    ks = jax.random.split(key, 32)
    f32 = jnp.float32

    def nrm(k, shape, scale):
        return jax.random.normal(k, shape, f32) * scale

    n_pages = PAST_LEN // PAGE_SIZE
    n_used = DEC_BATCH * n_pages
    n_pool = n_used + n_used // 4
    win_keep = min(WINDOW, PAST_LEN)
    page_table = jax.random.permutation(ks[4], n_pool)[:n_used].reshape(DEC_BATCH, n_pages).astype(jnp.int32)
    return {
        'x_prompt': nrm(ks[0], (BATCH, SEQ, D_MODEL), 1.0),
        'x_sample': nrm(ks[1], (DEC_BATCH, DEC_SEQ, D_MODEL), 1.0),
        'cache_cmp_kv': nrm(ks[2], (DEPTH, n_pool, PAGE_SIZE, 2, N_KV_HEADS, HEAD_DIM), 1.0),
        'cache_sel_kv': nrm(ks[3], (DEPTH, n_pool, PAGE_SIZE, 2, N_KV_HEADS, HEAD_DIM), 1.0),
        'state_win_kv': nrm(ks[5], (DEPTH, DEC_BATCH, win_keep, 2, N_KV_HEADS, HEAD_DIM), 1.0),
        'state_pool': nrm(ks[6], (DEPTH, DEC_BATCH, POOL_KEEP, POOL_WIDTH), 1.0),
        'page_table': page_table,
        'w_in': nrm(ks[7], (DEPTH, D_MODEL, IN_WIDTH), D_MODEL ** -0.5),
        'pool_w': nrm(ks[8], (DEPTH, len(POOL_WINDOWS), POOL_GROUP_W, POOL_GROUP_W), POOL_GROUP_W ** -0.5),
        'pool_scale': 1.0 + nrm(ks[9], (DEPTH, POOL_WIDTH), 0.01),
        'gmlp_ln_g': 1.0 + nrm(ks[10], (DEPTH, GMLP_WIDTH), 0.01),
        'gmlp_ln_b': nrm(ks[11], (DEPTH, GMLP_WIDTH), 0.01),
        'gmlp_ws': nrm(ks[12], (DEPTH, GMLP_GROUPS, CHUNK, CHUNK), CHUNK ** -0.5),
        'gmlp_bs': 1.0 + nrm(ks[13], (DEPTH, GMLP_GROUPS, CHUNK), 0.01),
        'cmp_pe': nrm(ks[14], (DEPTH, 2, CMP_LEN, HEAD_DIM), 0.02),
        'cmp_w1': nrm(ks[15], (DEPTH, 2, CMP_LEN * HEAD_DIM, CMP_HIDDEN), (CMP_LEN * HEAD_DIM) ** -0.5),
        'cmp_b1': nrm(ks[16], (DEPTH, 2, CMP_HIDDEN), 0.01),
        'cmp_w2': nrm(ks[17], (DEPTH, 2, CMP_HIDDEN, HEAD_DIM), CMP_HIDDEN ** -0.5),
        'w_branch_pool': nrm(ks[18], (DEPTH, POOL_WIDTH, D_MODEL), POOL_WIDTH ** -0.5),
        'w_branch_gmlp': nrm(ks[19], (DEPTH, GMLP_WIDTH, D_MODEL), GMLP_WIDTH ** -0.5),
        'w_branch_nsa': nrm(ks[20], (DEPTH, NSA_WIDTH, D_MODEL), NSA_WIDTH ** -0.5),
        'w_out': nrm(ks[21], (DEPTH, D_MODEL, D_MODEL), D_MODEL ** -0.5 * DN_BETA),
        'ln1_g': 1.0 + nrm(ks[22], (DEPTH, D_MODEL), 0.01),
        'ln1_b': nrm(ks[23], (DEPTH, D_MODEL), 0.01),
        'ln2_g': 1.0 + nrm(ks[24], (DEPTH, D_MODEL), 0.01),
        'ln2_b': nrm(ks[25], (DEPTH, D_MODEL), 0.01),
        'w_router': nrm(ks[26], (D_MODEL, N_EXPERTS), D_MODEL ** -0.5),
        'b_router': nrm(ks[27], (N_EXPERTS,), 0.01),
        'w_gate': nrm(ks[28], (DEPTH, N_EXPERTS, D_MODEL, D_EXPERT), D_MODEL ** -0.5),
        'w_up': nrm(ks[29], (DEPTH, N_EXPERTS, D_MODEL, D_EXPERT), D_MODEL ** -0.5),
        'w_down': nrm(ks[30], (DEPTH, N_EXPERTS, D_EXPERT, D_MODEL), D_EXPERT ** -0.5 * DN_BETA),
    }

def reference(x_prompt, x_sample, cache_cmp_kv, cache_sel_kv, state_win_kv, state_pool, page_table,
              w_in, pool_w, pool_scale, gmlp_ln_g, gmlp_ln_b, gmlp_ws, gmlp_bs,
              cmp_pe, cmp_w1, cmp_b1, cmp_w2, w_branch_pool, w_branch_gmlp, w_branch_nsa, w_out,
              ln1_g, ln1_b, ln2_g, ln2_b, w_router, b_router, w_gate, w_up, w_down):
    past_len = page_table.shape[1] * cache_cmp_kv.shape[2]
    xp, xs = x_prompt, x_sample
    st_p, st_s = [], []
    for l in range(DEPTH):
        lw = dict(w_in=w_in[l], pool_w=pool_w[l], pool_scale=pool_scale[l],
                  gmlp_ln_g=gmlp_ln_g[l], gmlp_ln_b=gmlp_ln_b[l], gmlp_ws=gmlp_ws[l], gmlp_bs=gmlp_bs[l],
                  cmp_pe=cmp_pe[l], cmp_w1=cmp_w1[l], cmp_b1=cmp_b1[l], cmp_w2=cmp_w2[l],
                  w_branch_pool=w_branch_pool[l], w_branch_gmlp=w_branch_gmlp[l], w_branch_nsa=w_branch_nsa[l],
                  w_out=w_out[l], ln1_g=ln1_g[l], ln1_b=ln1_b[l], ln2_g=ln2_g[l], ln2_b=ln2_b[l],
                  w_gate=w_gate[l], w_up=w_up[l], w_down=w_down[l])
        past = dict(cmp=gather_pages(cache_cmp_kv[l], page_table),
                    sel=gather_pages(cache_sel_kv[l], page_table),
                    win=state_win_kv[l], pool=state_pool[l])
        xp, sp = trunk_layer(xp, 0, None, lw, w_router, b_router)
        xs, ss = trunk_layer(xs, past_len, past, lw, w_router, b_router)
        st_p.append(sp)
        st_s.append(ss)

    def stacked(states, i):
        return jnp.stack([s[i] for s in states], 0)

    return (xp, xs,
            stacked(st_p, 0), stacked(st_p, 1), stacked(st_p, 2), stacked(st_p, 3),
            stacked(st_s, 0), stacked(st_s, 1), stacked(st_s, 2), stacked(st_s, 3), stacked(st_s, 4))


_drawn_inputs = setup_inputs


def setup_inputs(seed=0):
    import zlib

    import numpy as np

    out = dict(_drawn_inputs(seed))
    spreads = {}
    factors = {'cache_sel_kv': 3.832,
     'pool_scale': 10.439,
     'gmlp_ln_g': 16.822,
     'gmlp_ln_b': 16.062,
     'gmlp_bs': 8.964,
     'cmp_pe': 9.038,
     'cmp_b1': 16.444,
     'ln2_g': 3.101,
     'ln2_b': 3.343}
    for name, (base, spread) in spreads.items():
        noise = np.random.default_rng([zlib.crc32(name.encode()), seed]).standard_normal(out[name].shape)
        drawn = base * np.exp(spread * noise) if base else spread * noise
        out[name] = __import__('jax').numpy.asarray(drawn.astype(out[name].dtype))
    for name, factor in factors.items():
        out[name] = (out[name] * factor).astype(out[name].dtype)
    return out
```

```python
from contextlib import ExitStack

import numpy as np
import concourse.bass as bass
from concourse import mybir

F32 = mybir.dt.float32
I32 = mybir.dt.int32
ALU = mybir.AluOpType
ACT = mybir.ActivationFunctionType
AX = mybir.AxisListType

D, SEQ, L = 1024, 512, 2
B, TS, PAST, PAGE = 8, 8, 256, 128
NS = B * TS
TOK = SEQ + NS
KT_D = D // 128
NT = SEQ // 128
TILES = [128] * NT + [NS]
NTT = len(TILES)
WIN = (2, 4, 8, 16)
KEEP = 15
HD, NH, NKV, GQA = 64, 8, 2, 4
CL, CS = 32, 16
HID = 128
E, EG, FE = 16, 4, 256
N_POOL = B * (PAST // PAGE) * 5 // 4
ALPHA = (2 * L) ** 0.25
EPS = 1e-5
NEG = -1e30

Q0, KV0, A0, V0, G0, TM = 0, 512, 1280, 1536, 1792, 1816
NCH = 4
CW = TM // NCH

XC = SEQ + B * PAST + CL
NG = XC // CS
NB = NG - 2
UW = NG

MAXCH = 24
SLOTS = MAXCH * 128

_C = {}
_at = 0
for _n, _w in [("ident", 128), ("diag", 128), ("cos", NTT * 8), ("sin", NTT * 8), ("cm", NT * 32), ("cneg", NT * 32),
               ("newneg", 2 * 64), ("scneg", 2 * 128), ("bcur0", 4 * 128), ("bcur", 4 * 128), ("bprev", 4 * 128),
               ("bst", 4 * 64), ("bnew", 4 * 64), ("tri", 128), ("ones", 128), ("e16", 16), ("g4", 4), ("th", 5),
               ("chunk", 32), ("gm", 128), ("gms", 64), ("blk", 4), ("rowhead", 4), ("mhalf", NTT), ("gsel", 256)]:
    _C[_n] = (_at, _at + _w)
    _at += _w
NCONST = _at

_S = {}
_at = 0
for _n, _w in [("w2", 128), ("poolw", 256), ("wsT", 512), ("bsT", 256), ("pscale", 2), ("b1", 2), ("wss", 32),
               ("vg", 256), ("vb", 256)]:
    _S[_n] = (_at, _at + _w)
    _at += _w
NSMALL = _at


def constants():
    c = np.zeros((128, NCONST), np.float32)

    def put(name, a):
        lo, hi = _C[name]
        a = np.asarray(a, np.float32)
        c[:a.shape[0], lo:hi] = a.reshape(a.shape[0], hi - lo)

    r = np.arange(128)
    put("ident", np.eye(128))
    put("diag", np.where(r[None, :] <= r[:, None], 0.0, NEG))
    pos = np.zeros((NTT, 128), np.float32)
    for i in range(NT):
        pos[i] = i * 128 + r
    pos[NT, :NS] = PAST + r[:NS] % TS
    inv = (1.0 / (np.float32(500000.0) ** (np.arange(8, dtype=np.float32) / np.float32(8)))).astype(np.float32)
    ang = pos[:, :, None] * inv
    put("cos", np.cos(ang).transpose(1, 0, 2))
    put("sin", np.sin(ang).transpose(1, 0, 2))
    c32 = np.arange(32)
    ok = (c32[None, None] < 31) & (c32[None, None] * CS + CL - 1 <= (np.arange(NT)[None, :, None] * 128 + r[:, None, None]))
    put("cm", ok)
    put("cneg", np.where(ok, 0.0, NEG))
    row_b, row_t = r // 32, r % 8
    kb, kt = np.arange(64) // 8, np.arange(64) % 8
    put("newneg", np.stack([np.where((kb[None] == 4 * g + row_b[:, None]) & (kt[None] <= row_t[:, None]), 0.0, NEG)
                            for g in range(2)], 1))
    mb, mc = r // 16, r % 16
    put("scneg", np.stack([np.where((mb[None] == 4 * g + row_b[:, None]) & (mc[None] < 15), 0.0, NEG)
                           for g in range(2)], 1))
    s, t = r[:, None], r[None, :]
    b0, bc, bp, bst, bnew = [], [], [], [], []
    for w in WIN:
        inside = (s <= t) & (s > t - w)
        b0.append(inside / np.minimum(w, t + 1.0) - (s == t))
        bc.append(inside / float(w) - (s == t))
        bp.append((s - 128 > t - w) / float(w))
        sb, sr = np.arange(B * KEEP) // KEEP, np.arange(B * KEEP) % KEEP - KEEP
        bst.append((sb[:, None] == kb[None]) & (sr[:, None] > kt[None] - w))
        bst[-1] = bst[-1] / float(w)
        same = kb[:, None] == kb[None]
        bnew.append((same & (kt[:, None] <= kt[None]) & (kt[:, None] > kt[None] - w)) / float(w) - np.eye(64))
    put("bcur0", np.stack(b0, 1))
    put("bcur", np.stack(bc, 1))
    put("bprev", np.stack(bp, 1))
    put("bst", np.stack(bst, 1))
    put("bnew", np.stack(bnew, 1))
    put("tri", s < t)
    put("ones", np.ones((128, 128)))
    put("e16", np.tile(16 - np.arange(16), (128, 1)))
    put("g4", np.tile(4 - np.arange(4), (128, 1)))
    put("th", np.tile(128 * np.arange(5), (128, 1)))
    put("chunk", np.tile(np.arange(32), (128, 1)))
    put("gm", s <= t)
    put("gms", (kb[:, None] == kb[None]) & (kt[:, None] <= kt[None]))
    put("blk", (r // 32)[:, None] == np.arange(4)[None])
    put("rowhead", (r % 32 // 8)[:, None] == np.arange(4)[None])
    put("mhalf", np.full((128, NTT), -0.5))
    gs = np.zeros((64, 2, 128))
    for g in range(2):
        for p in range(128):
            gs[(4 * g + p // 32) * 8 + p % 8, g, p] = 1
    put("gsel", gs)
    return c


class Steps:

    def __init__(self, eng, sem):
        self.eng, self.sem, self.n = eng, sem, 0

    def after(self, ins):
        self.n += 1
        ins.then_inc(self.sem, 1)
        self.eng.wait_ge(self.sem, self.n)


class Ctx:
    pass


def build(nc, io):
    with ExitStack() as ctx:
        k = Ctx()
        k.nc, k.io = nc, io

        def sb(name, shape, dt=F32):
            return ctx.enter_context(nc.sbuf_tensor(name, shape, dt))

        k.sems = []

        def sem(name):
            s = ctx.enter_context(nc.semaphore(name))
            k.sems.append(s)
            return s
        k.sem = sem

        k.const = sb("const", [128, NCONST])
        k.c = {n: k.const[:, lo:hi] for n, (lo, hi) in _C.items()}
        k.x = sb("x", [128, NTT, D])
        k.xT = sb("xT", [128, KT_D, TOK])
        k.oT = sb("oT", [128, KT_D, TOK])
        k.pt = sb("page_ids", [1, B * PAST // PAGE], I32)
        k.tokid = sb("tokid", [128, NTT], I32)
        k.zero = sb("zero", [128, SLOTS // 128], I32)
        k.zrow = sb("zero_row", [128, 256])
        k.mk = sb("mask16", [128, 5 * 128], mybir.dt.bfloat16)
        k.wr = sb("w_router", [128, KT_D, E])
        k.br = sb("b_router", [128, E])
        k.ps = ctx.enter_context(nc.psum_tensor("ps", [128, 8, 512], F32))
        k.ident = k.c["ident"]

        first_in = sem("first_inputs_in")
        k.const_in, k.x_in = sem("constants_in"), sem("x_in")
        k.sems.clear()
        dve_s, act_s, pool_s = sem("dve_step"), sem("act_step"), sem("pool_step")
        k.dve, k.act, k.pool = Steps(nc.vector, dve_s), Steps(nc.scalar, act_s), Steps(nc.gpsimd, pool_s)
        prologue(k, first_in)
        nc.all_engine_barrier(sems_to_clear=range(pool_s.num, pool_s.num + 1))
        k.pool.n = 0
        with nc.Fori(0, L) as layer:
            k.layer = layer
            with ExitStack() as phase:
                def sp(name, shape, dt=F32):
                    return phase.enter_context(nc.sbuf_tensor(name, shape, dt))
                k.z = sp("z", [128, NTT, TM])
                k.uT = sp("uT", [128, 2, TOK])
                k.vn = sp("vn", [128, NTT, 256])
                k.qT = sp("qT", [128, GQA, SEQ])
                k.qsT = sp("qsT", [128, NKV, B, GQA, TS])
                k.KT = sp("KT", [128, 2, NKV, SEQ])
                k.KTs = sp("KT_sample", [128, 2, NS])
                k.kcT = sp("kcT", [128, NKV, 32])
                k.kcsT = sp("kcT_sample", [128, NB - 32])
                k.vblk = sp("vblk", [128, NKV, GQA, HD])
                k.vcs = sp("vcs", [128, NKV, HD])
                k.gates = sp("gates", [128, NTT, 24])
                k.gsr = sp("gates_by_row", [128, 2, NKV, 3])
                with ExitStack() as early:
                    def se(name, shape, dt=F32):
                        return early.enter_context(nc.sbuf_tensor(name, shape, dt))
                    k.XT = se("XT", [128, 2, XC])
                    k.small = se("small", [128, NSMALL])
                    k.s = {n: k.small[:, lo:hi] for n, (lo, hi) in _S.items()}
                    k.spool = se("pool_state", [128, 256])
                    project(k)
                    mixers(k)
                attention(k)
            merge(k)
            experts(k)
            nums = [s.num for s in k.sems]
            assert sorted(nums) == list(range(min(nums), max(nums) + 1))
            nc.gpsimd.dma_reset(range(min(nums), max(nums) + 1))
            nc.all_engine_barrier(sems_to_clear=range(min(nums), max(nums) + 1))


def prologue(k, first_in):
    nc, io = k.nc, k.io
    with nc.Block() as block:
        @block.sync
        def _(sp):
            sp.dma_start(k.pt[:, :], io["page_table"]).then_inc(first_in, 16)
            sp.dma_start(k.xT[:, :, :], io["x0T"]).then_inc(first_in, 16)
            sp.dma_start(k.tokid[:, :], io["tokid"]).then_inc(first_in, 16)
            sp.dma_start(k.wr[:, :, :], io["w_router"].rearrange("(k p) e -> p k e", p=128)).then_inc(first_in, 16)
            sp.dma_start(k.br[:, :], io["br"]).then_inc(first_in, 16)
            sp.dma_start(k.const[:, :], io["consts"]).then_inc(k.const_in, 16)
            sp.dma_start(k.x[:, 0:NT, :], io["xp"].rearrange("(i p) d -> p i d", p=128)).then_inc(k.x_in, 16)
            sp.dma_start(k.x[0:NS, NT, :], io["xs"]).then_inc(k.x_in, 16)
            sp.wait_ge(first_in, 16 * 5)

        @block.gpsimd
        def _(pool):
            k.pool.after(pool.memset(k.zero[:, :], 0))
            k.pool.after(pool.memset(k.zrow[:, :], 0.0))


def project(k):
    nc, io, l, ps = k.nc, k.io, k.layer, k.ps
    sem = k.sem
    wtm_in = [sem(f"wtm_in{n}") for n in range(2)]
    wu_in, small_in, states_in = sem("wu_in"), sem("small_in"), sem("states_in")
    k.pages_in = sem("cmp_pages_in")
    z_done, z_out, u_done, u_out = sem("z_done"), sem("z_out"), sem("u_done"), sem("u_out")
    z_cleared = sem("z_cleared")
    roped, t_done, t_out = sem("roped"), sem("t_done"), sem("t_out")
    stat_ready, rstd_ready, vn_ready, gate_tanh = (sem("vstat_ready"), sem("vrstd_ready"), sem("vn_ready"),
                                                   sem("gate_tanh"))
    k.stored = sem("stored")
    k.n_stored = 0
    with ExitStack() as ctx:
        wtm = ctx.enter_context(nc.sbuf_tensor("wtm", [128, 2, KT_D, CW], F32))
        wu = ctx.enter_context(nc.sbuf_tensor("wu", [128, KT_D, 256], F32))
        rt = k.oT[:, 0:3, :].rearrange("p a t -> p (a t)")[:, 0:4 * NTT * 64].rearrange("p (a n) -> p a n", a=4)
        st = ctx.enter_context(nc.sbuf_tensor("v_stats", [128, NTT, 6], F32))
        mv = ctx.enter_context(nc.sbuf_tensor("v_mv", [128, NTT, 2], F32))
        rs = ctx.enter_context(nc.sbuf_tensor("v_rstd", [128, NTT], F32))
        block = ctx.enter_context(nc.Block())

        @block.sync
        def _(sp):
            for n in range(NCH):
                if n == 2:
                    sp.dma_start(wu[:, :, :], io["wu"][l]).then_inc(wu_in, 16)
                if n >= 2:
                    sp.wait_ge(z_done, (n - 1) * NTT)
                sp.dma_start(wtm[:, n % 2, :, :], io["wtm"][l, n]).then_inc(wtm_in[n % 2], 16)
                if n == 0:
                    for j in range(B * PAST // PAGE):
                        page = sp.value_load(k.pt[0:1, j:j + 1], min_val=0, max_val=N_POOL - 1)
                        sp.dma_start(k.XT[:, :, SEQ + j * PAGE:SEQ + (j + 1) * PAGE],
                                     io["cmp_pages"][l, page]).then_inc(k.pages_in, 16)
                    for h in range(NKV):
                        sp.dma_start(k.XT[h * HD:(h + 1) * HD, :, XC - CL:XC], io["peT"][l]).then_inc(k.pages_in, 16)
                if n == 1:
                    sp.dma_start(k.small[:, :], io["small"][l]).then_inc(small_in, 16)
                    sp.dma_start(k.spool[0:B * KEEP, :], io["state_pool2"][l]).then_inc(small_in, 16)
            sp.dma_start(io["o_win_s"][l, :, 0:PAST - TS, :], io["state_win"][l, :, TS:PAST, :]).then_inc(k.stored, 16)
            sp.dma_start(io["o_pool_s"][l, :, 0:KEEP - TS, :], io["state_pool"][l, :, TS:KEEP, :]).then_inc(k.stored, 16)
            sp.wait_ge(roped, 2)
            for c, (op, os) in enumerate([("o_cmp_p", "o_cmp_s"), ("o_sel_p", "o_sel_s"), ("o_win_p", None)]):
                cols = slice(KV0 + 256 * c, KV0 + 256 * (c + 1))
                sp.dma_start(io[op][l].rearrange("(i p) c -> p i c", p=128), k.z[:, 0:NT, cols]).then_inc(k.stored, 16)
                if os:
                    sp.dma_start(io[os][l], k.z[0:NS, NT, cols]).then_inc(k.stored, 16)
                else:
                    for b in range(B):
                        sp.dma_start(io["o_win_s"][l, b, PAST - TS:PAST, :],
                                       k.z[b * TS:(b + 1) * TS, NT, cols]).then_inc(k.stored, 16)
            sp.wait_ge(z_out, NCH * NTT)
            sp.dma_start(io["o_pool_p"][l], k.z[128 - KEEP:128, NT - 1, A0:A0 + 256]).then_inc(k.stored, 16)
            for b in range(B):
                sp.dma_start(io["o_pool_s"][l, b, KEEP - TS:KEEP, :],
                               k.z[b * TS:(b + 1) * TS, NT, A0:A0 + 256]).then_inc(k.stored, 16)
            sp.wait_ge(vn_ready, 1)
            sp.dma_start(io["o_gmlp_s"][l], k.vn[0:NS, NT, :]).then_inc(k.stored, 16)

        @block.gpsimd
        def _(pool):
            pool.memset(k.z[64:128, NT, :], 0.0).then_inc(z_cleared, 1)
            pool.wait_ge(z_cleared, 1)
            for h in range(NKV):
                other = slice((1 - h) * HD, (2 - h) * HD)
                k.pool.after(pool.memset(k.KT[other, :, h, :], 0.0))
                k.pool.after(pool.memset(k.kcT[other, h, :], 0.0))
                k.pool.after(pool.memset(k.qsT[other, h, :, :, :], 0.0))
            pool.wait_ge(k.const_in, 16)
            pool.wait_ge(stat_ready, 1)
            k.pool.after(pool.tensor_scalar(rs[:, :], mv[:, :, 1], EPS, None, ALU.add))
            pool.tensor_tensor(rs[:, :], rs[:, :], k.c["mhalf"], ALU.pow).then_inc(rstd_ready, 1)
        k.n_stored = 2 + 5 + B + 1 + B + 1

        @block.tensor
        def _(pe):
            def z_chunk(n):
                pe.wait_ge(wtm_in[n % 2], 16 * (n // 2 + 1))
                for i, rows in enumerate(TILES):
                    j = n * NTT + i
                    if j >= 4:
                        pe.wait_ge(z_out, j - 3)
                    for kk in range(KT_D):
                        last = pe.matmul(ps[0:rows, j % 4, 0:CW], k.xT[:, kk, i * 128:i * 128 + rows],
                                         wtm[:, n % 2, kk, :], start=(kk == 0), stop=(kk == KT_D - 1))
                    last.then_inc(z_done, 1)
            z_chunk(0)
            z_chunk(1)
            z_chunk(2)
            pe.wait_ge(wu_in, 16)
            for m in range(2):
                for kk in range(KT_D):
                    pe.matmul(ps[:, 4 + m, :], wu[:, kk, m * 128:(m + 1) * 128], k.xT[:, kk, 0:SEQ],
                              start=(kk == 0), stop=(kk == KT_D - 1))
                for kk in range(KT_D):
                    last = pe.matmul(ps[:, 6 + m, 0:NS], wu[:, kk, m * 128:(m + 1) * 128], k.xT[:, kk, SEQ:TOK],
                                     start=(kk == 0), stop=(kk == KT_D - 1))
                last.then_inc(u_done, 1)
            z_chunk(3)
            pe.wait_ge(k.const_in, 16)
            pe.wait_ge(z_out, NCH * NTT)
            pe.wait_ge(u_out, 2)
            pe.wait_ge(roped, 1)
            for u in range(4 + 4):
                if u == 4:
                    pe.wait_ge(roped, 2)
                for i in range(NT):
                    if u < 4:
                        src = k.z[:, i, Q0 + u * 128:Q0 + (u + 1) * 128]
                    else:
                        col = KV0 + (256, 512, 0, 128)[u - 4]
                        src = k.z[:, i, col:col + 128]
                    last = pe.transpose(ps[:, u, i * 128:(i + 1) * 128], src, k.ident)
                last.then_inc(t_done, 1)
            pe.wait_ge(t_out, 2)
            for u in range(4):
                src = k.z[0:NS, NT, Q0 + u * 128:Q0 + (u + 1) * 128]
                last = pe.transpose(ps[:, 0, u * NS:(u + 1) * NS], src, k.ident[0:NS, 0:NS])
            last.then_inc(t_done, 1)
            for u in range(2):
                col = KV0 + 256 * (u + 1)
                last = pe.transpose(ps[:, 1, u * NS:(u + 1) * NS], k.z[0:NS, NT, col:col + 128], k.ident[0:NS, 0:NS])
            last.then_inc(t_done, 1)

        @block.scalar
        def _(act):
            act.wait_ge(z_cleared, 1)

            def z_copy(n):
                for i, rows in enumerate(TILES):
                    j = n * NTT + i
                    act.wait_ge(z_done, j + 1)
                    act.copy(k.z[0:rows, i, n * CW:(n + 1) * CW], ps[0:rows, j % 4, 0:CW]).then_inc(z_out, 1)
            z_copy(0)
            z_copy(1)
            z_copy(2)
            for m in range(2):
                act.wait_ge(u_done, m + 1)
                act.copy(k.uT[:, m, 0:SEQ], ps[:, 4 + m, :])
                act.copy(k.uT[:, m, SEQ:TOK], ps[:, 6 + m, 0:NS]).then_inc(u_out, 1)
            z_copy(3)
            act.wait_ge(z_out, NCH * NTT)
            act.activation(k.gates[:, :, :], k.z[:, :, G0:G0 + 24], ACT.Tanh, scale=0.5).then_inc(gate_tanh, 1)
            for u in range(8):
                act.wait_ge(t_done, u + 1)
                if u < 4:
                    act.activation(k.qT[:, u, :], ps[:, u, :], ACT.Copy, scale=HD ** -0.5).then_inc(t_out, 1)
                elif u < 6:
                    for h in range(NKV):
                        hs = slice(h * HD, (h + 1) * HD)
                        last = act.copy(k.KT[hs, u - 4, h, :], ps[hs, u, :])
                    last.then_inc(t_out, 1)
                else:
                    act.copy(k.XT[:, u - 6, 0:SEQ], ps[:, u, :]).then_inc(t_out, 1)
            act.wait_ge(t_done, 9)
            for h in range(NKV):
                hs = slice(h * HD, (h + 1) * HD)
                for i in range(GQA):
                    act.activation(k.qsT[hs, h, :, i, :], ps[hs, 0, i * NS:(i + 1) * NS].rearrange("p (b t) -> p b t", b=B),
                                   ACT.Copy, scale=HD ** -0.5)
            act.wait_ge(t_done, 10)
            act.copy(k.KTs[:, :, :], ps[:, 1, 0:2 * NS].rearrange("p (u t) -> p u t", u=2))

        @block.vector
        def _(dve):
            def rope(base, n, step):
                def half(o):
                    return k.z[:, :, base:base + n * HD].rearrange("p i (h d) -> p i h d", d=HD)[:, :, :, o:o + 8]
                cos = k.c["cos"].rearrange("p (i d) -> p i d", i=NTT).unsqueeze(2).broadcast_to([128, NTT, n, 8])
                sin = k.c["sin"].rearrange("p (i d) -> p i d", i=NTT).unsqueeze(2).broadcast_to([128, NTT, n, 8])
                t = [rt[:, a, 0:NTT * n * 8].rearrange("p (i h d) -> p i h d", i=NTT, h=n) for a in range(4)]
                dve.tensor_tensor(t[0], half(0), cos, ALU.mult)
                dve.tensor_tensor(t[1], half(8), sin, ALU.mult)
                dve.tensor_tensor(t[2], half(8), cos, ALU.mult)
                k.dve.after(dve.tensor_tensor(t[3], half(0), sin, ALU.mult))
                dve.tensor_tensor(half(0), t[0], t[1], ALU.subtract)
                return dve.tensor_tensor(half(8), t[2], t[3], ALU.add)

            dve.wait_ge(k.const_in, 16)
            dve.wait_ge(z_out, 2 * NTT)
            rope(Q0, NH, HD).then_inc(roped, 1)
            dve.wait_ge(roped, 1)
            dve.wait_ge(z_out, 3 * NTT)
            for c in range(3):
                last = rope(KV0 + 256 * c, NKV, HD)
                if c < 2:
                    k.dve.after(last)
            last.then_inc(roped, 1)
            dve.wait_ge(z_out, NCH * NTT)
            for i in range(NTT):
                last = dve.bn_stats(st[:, i, :], k.z[:, i, V0:V0 + 256])
            k.dve.after(last)
            for i in range(NTT):
                last = dve.bn_aggr(mv[:, i, :], st[:, i, :])
            last.then_inc(stat_ready, 1)
            dve.wait_ge(rstd_ready, 1)
            for i in range(NTT):
                last = dve.tensor_scalar(k.vn[:, i, :], k.z[:, i, V0:V0 + 256], mv[:, i, 0:1], rs[:, i:i + 1],
                                         ALU.subtract, ALU.mult)
            k.dve.after(last)
            dve.wait_ge(small_in, 32)
            k.dve.after(dve.tensor_tensor(k.vn[:, :, :], k.vn[:, :, :],
                                          k.s["vg"].unsqueeze(1).broadcast_to([128, NTT, 256]), ALU.mult))
            dve.tensor_tensor(k.vn[:, :, :], k.vn[:, :, :],
                              k.s["vb"].unsqueeze(1).broadcast_to([128, NTT, 256]), ALU.add).then_inc(vn_ready, 1)
            dve.wait_ge(gate_tanh, 1)
            dve.tensor_scalar(k.gates[:, :, :], k.gates[:, :, :], 0.5, 0.5, ALU.mult, ALU.add)


def mixers(k):
    nc, io, l, ps, c = k.nc, k.io, k.layer, k.ps, k.c
    sem = k.sem
    w1_in, masked = sem("w1_in"), sem("gmlp_masked")
    d_done, d_out, mix_done, mix_out, y_done = (sem("pool_d_done"), sem("pool_d_out"), sem("mix_done"),
                                                sem("mix_out"), sem("pool_y_done"))
    u_done, u1_out, x_ready, th_ready, hid_ready = (sem("cmp_u_done"), sem("cmp_u1_out"), sem("cmp_x_ready"),
                                                    sem("cmp_tanh_ready"), sem("cmp_hid_ready"))
    gr_done, kc_done = sem("gate_rows_done"), sem("kc_done")
    with ExitStack() as ctx:
        def sb(name, shape):
            return ctx.enter_context(nc.sbuf_tensor(name, shape, F32))
        w1 = sb("w1", [128, 2, CL, HID])
        dT = k.oT[:, 0:2, :]
        wmT = sb("wmT", [128, 4, 128])
        wmsT = sb("wmsT", [128, 4, NS])
        u1 = sb("u1", [128, 4, UW])
        bias = sb("cmp_bias", [128, 4])
        spare = k.oT[:, 4:8, :].rearrange("p a t -> p (a t)")
        xh, th, hid = (spare[:, n * 4 * NB:(n + 1) * 4 * NB].rearrange("p (n m) -> p n m", n=4) for n in range(3))
        hrep = sb("hrep", [128, NKV, 4, 32])
        gt = sb("gate_tmp", [128, 2, NKV, 3, 4])
        block = ctx.enter_context(nc.Block())
        BANK = [[0, 1], [3, 4]]

        @block.sync
        def _(sp):
            for h in range(NKV):
                sp.dma_start(w1[h * HD:(h + 1) * HD, :, :, :], io["w1"][l]).then_inc(w1_in, 16)

        @block.tensor
        def _(pe):
            for g in range(4):
                p, half = g // 2, slice(64 * (g % 2), 64 * (g % 2) + 64)
                col = slice(A0 + 64 * g, A0 + 64 * g + 64)
                for i in range(NT):
                    out = ps[half, p, i * 128:(i + 1) * 128]
                    cur = c["bcur0" if i == 0 else "bcur"][:, g * 128:(g + 1) * 128]
                    pe.matmul(out, k.z[:, i, col], cur, start=True, stop=(i == 0))
                    if i:
                        pe.matmul(out, k.z[:, i - 1, col], c["bprev"][:, g * 128:(g + 1) * 128], start=False, stop=True)
                out = ps[half, 2, p * 64:p * 64 + 64]
                pe.matmul(out, k.spool[0:B * KEEP, 64 * g:64 * g + 64], c["bst"][0:B * KEEP, g * 64:g * 64 + 64],
                          start=True, stop=False)
                last = pe.matmul(out, k.z[0:NS, NT, col], c["bnew"][0:NS, g * 64:g * 64 + 64], start=False, stop=True)
            last.then_inc(d_done, 1)
            pe.wait_ge(masked, 1)
            for g in range(4):
                p, half = g // 2, slice(64 * (g % 2), 64 * (g % 2) + 64)
                for i in range(NT):
                    pe.matmul(ps[half, 3 + p, i * 128:(i + 1) * 128], k.vn[:, i, 64 * g:64 * g + 64], wmT[:, g, :],
                              start=True, stop=True)
                last = pe.matmul(ps[half, 5, p * 64:p * 64 + 64], k.vn[0:NS, NT, 64 * g:64 * g + 64],
                                 wmsT[0:NS, g, :], start=True, stop=True)
            last.then_inc(mix_done, 1)
            pe.wait_ge(d_out, 1)
            for p in range(2):
                w = k.s["poolw"][:, p * 128:(p + 1) * 128]
                pe.matmul(ps[:, 6 + p, :], w, dT[:, p, 0:SEQ], start=True, stop=True)
                last = pe.matmul(ps[:, 2, 128 + p * 64:192 + p * 64], w, dT[:, p, SEQ:TOK], start=True, stop=True)
            last.then_inc(y_done, 1)
            pe.wait_ge(mix_out, 1)
            for g in range(2):
                last = pe.matmul(ps[:, 5, 256 + 24 * g:280 + 24 * g], c["gsel"][0:NS, g * 128:(g + 1) * 128],
                                 k.gates[0:NS, NT, :], start=True, stop=True)
            last.then_inc(gr_done, 1)
            pe.wait_ge(w1_in, 32)
            pe.wait_ge(k.pages_in, 16 * (B * PAST // PAGE + NKV))
            for kv in range(2):
                for a in range(2):
                    for r in range(CS):
                        for h in range(NKV):
                            hs = slice(h * HD, (h + 1) * HD)
                            last = pe.matmul(ps[:, BANK[h][kv], a * UW:(a + 1) * UW], w1[hs, kv, a * CS + r, :],
                                             k.XT[hs, kv, r:XC:CS], start=(r == 0), stop=(r == CS - 1))
                last.then_inc(u_done, 1)
            pe.wait_ge(hid_ready, 1)
            for h in range(NKV):
                pe.matmul(ps[h * HD:(h + 1) * HD, 5, 0:NB], k.s["w2"][:, 0:64], hid[:, h, :], start=True, stop=True)
            pe.wait_ge(hid_ready, 2)
            for h in range(NKV):
                pe.matmul(ps[:, 7, h * HD:(h + 1) * HD], hrep[:, h, :, :].rearrange("p i c -> p (i c)"),
                          k.s["w2"][:, 64:128], start=True, stop=True)
                last = pe.matmul(ps[:, 7, 128 + h * HD:192 + h * HD], hid[:, 2 + h, 32:NB], k.s["w2"][:, 64:128],
                                 start=True, stop=True)
            last.then_inc(kc_done, 1)

        @block.scalar
        def _(act):
            for n in range(4):
                kv, h = n // 2, n % 2
                act.wait_ge(u_done, kv + 1)
                act.copy(u1[:, n, :], ps[:, BANK[h][kv], UW:2 * UW]).then_inc(u1_out, 1)
            act.wait_ge(x_ready, 1)
            act.activation(th[:, :, :], hid[:, :, :], ACT.Tanh, scale=0.7978845608028654).then_inc(th_ready, 1)
            act.wait_ge(kc_done, 1)
            for h in range(NKV):
                hs = slice(h * HD, (h + 1) * HD)
                act.activation(k.kcT[hs, h, :], ps[hs, 5, 0:32], ACT.Copy, scale=0.5)
            act.activation(k.kcsT[:, :], ps[:, 5, 32:NB], ACT.Copy, scale=0.5)

        @block.vector
        def _(dve):
            step = k.dve.after
            s = k.s
            dve.tensor_tensor(wmT[:, :, :], s["wsT"].rearrange("p (g t) -> p g t", g=4),
                              c["gm"].unsqueeze(1).broadcast_to([128, 4, 128]), ALU.mult)
            dve.tensor_tensor(wmsT[0:NS, :, :].rearrange("p g (b t) -> p g b t", b=B),
                              s["wss"][0:NS].rearrange("p (g t) -> p g t", g=4).unsqueeze(2).broadcast_to([NS, 4, B, TS]),
                              c["gms"][0:NS].rearrange("p (b t) -> p b t", b=B).unsqueeze(1).broadcast_to([NS, 4, B, TS]),
                              ALU.mult).then_inc(masked, 1)
            dve.tensor_copy(k.mk[:, 0:128], k.ident)
            dve.tensor_copy(k.mk[:, 128:256], c["diag"])
            dve.tensor_copy(k.mk[:, 256:512], c["scneg"])
            dve.tensor_copy(k.mk[:, 512:640], c["newneg"])
            dve.wait_ge(d_done, 1)
            dve.tensor_copy(dT[:, :, 0:SEQ], ps[:, 0:2, :])
            dve.tensor_copy(dT[:, :, SEQ:TOK], ps[:, 2, 0:128].rearrange("p (a t) -> p a t", a=2)).then_inc(d_out, 1)
            dve.wait_ge(mix_done, 1)
            bs = s["bsT"].rearrange("p (a t) -> p a t", a=2)
            for p in range(2):
                dve.tensor_tensor(k.oT[:, 2 + p, 0:SEQ].rearrange("p (i t) -> p i t", i=NT),
                                  ps[:, 3 + p, :].rearrange("p (i t) -> p i t", i=NT),
                                  bs[:, p, :].unsqueeze(1).broadcast_to([128, NT, 128]), ALU.add)
            for p in range(2):
                last = dve.tensor_tensor(k.oT[:, 2 + p, SEQ:TOK].rearrange("p (b t) -> p b t", b=B),
                                         ps[:, 5, 64 * p:64 * p + 64].rearrange("p (b t) -> p b t", b=B),
                                         bs[:, p, 0:TS].unsqueeze(1).broadcast_to([128, B, TS]), ALU.add)
            last.then_inc(mix_out, 1)
            dve.wait_ge(mix_out, 1)
            dve.tensor_tensor(k.oT[:, 2:4, :], k.oT[:, 2:4, :], k.uT[:, :, :], ALU.mult)
            dve.wait_ge(y_done, 1)
            for p in range(2):
                sc = s["pscale"][:, p:p + 1]
                dve.tensor_scalar(k.oT[:, p, 0:SEQ], ps[:, 6 + p, :], sc, None, ALU.mult)
                dve.tensor_scalar(k.oT[:, p, SEQ:TOK], ps[:, 2, 128 + 64 * p:192 + 64 * p], sc, None, ALU.mult)
            dve.wait_ge(gr_done, 1)
            for g in range(2):
                for h in range(NKV):
                    dve.tensor_tensor(gt[:, g, h, :, :],
                                      ps[:, 5, 256 + 24 * g + 12 * h:268 + 24 * g + 12 * h].rearrange("p (i c) -> p c i", i=4),
                                      c["rowhead"].unsqueeze(1).broadcast_to([128, 3, 4]), ALU.mult)
            step(dve.memset(bias[:, :], 0.0))
            dve.tensor_reduce(k.gsr[:, :, :, :].rearrange("p g h c -> p (g h c)"),
                              gt[:, :, :, :, :].rearrange("p g h c i -> p (g h c) i"), AX.X, ALU.add)

            for n in range(4):
                kv, h = n // 2, n % 2
                dve.wait_ge(u1_out, n + 1)
                U = ps[:, BANK[h][kv], :]
                step(dve.scalar_tensor_tensor(bias[:, n:n + 1], U[:, NB:NB + 1], s["b1"][:, kv:kv + 1],
                                              u1[:, n, NB + 1:NB + 2], ALU.add, ALU.add))
                last = dve.scalar_tensor_tensor(xh[:, n, :], U[:, 0:NB], bias[:, n:n + 1], u1[:, n, 1:NB + 1],
                                                ALU.add, ALU.add)
            step(last)
            step(dve.tensor_tensor(th[:, :, :], xh[:, :, :], xh[:, :, :], ALU.mult))
            step(dve.tensor_scalar(th[:, :, :], th[:, :, :], 0.044715, 1.0, ALU.mult, ALU.add))
            dve.tensor_tensor(hid[:, :, :], th[:, :, :], xh[:, :, :], ALU.mult).then_inc(x_ready, 1)
            dve.wait_ge(th_ready, 1)
            dve.scalar_tensor_tensor(hid[:, :, :], th[:, :, :], 1.0, xh[:, :, :], ALU.add, ALU.mult).then_inc(hid_ready, 1)
            dve.wait_ge(hid_ready, 1)
            dve.tensor_copy(hrep[:, :, :, :], hid[:, 2:4, 0:32].unsqueeze(2).broadcast_to([128, NKV, 4, 32])).then_inc(hid_ready, 1)
            dve.wait_ge(kc_done, 1)
            dve.tensor_scalar(k.vcs[:, :, :], ps[:, 7, 128:256].rearrange("p (h d) -> p h d", h=2), 0.5, None, ALU.mult)
            for h in range(NKV):
                dve.scalar_tensor_tensor(k.vblk[:, h, :, :],
                                         ps[:, 7, h * HD:(h + 1) * HD].unsqueeze(1).broadcast_to([128, 4, HD]), 0.5,
                                         c["blk"].unsqueeze(2).broadcast_to([128, 4, HD]), ALU.mult, ALU.mult)


def attention(k):
    nc, io, l, ps, c = k.nc, k.io, k.layer, k.ps, k.c
    sem = k.sem
    LAG_T, LAG_V = 2, 3
    units = []
    for t in range(NT):
        units.append(("cmp", t, 0, 0, 0))
        units += [("kv", t, kvh, i, br) for kvh in range(NKV) for i in range(GQA) for br in range(2)]
    for g in range(2):
        for kvh in range(NKV):
            units.append(("scmp", g, kvh, 0, 0))
            units += [("skv", g, kvh, 0, br) for br in range(2)]
    NU = len(units)
    group = [u[1] + (NT if u[0][0] == "s" else 0) for u in units]
    last_of = [max(n for n in range(NU) if group[n] == gr) for gr in range(NT + 2)]

    def on_act(n):
        return n % 2 == 1

    def copied(eng, n):
        if on_act(n):
            eng.wait_ge(pt_by_act, len([m for m in range(n + 1) if on_act(m)]))
        else:
            eng.wait_ge(pt_by_dve, len([m for m in range(n + 1) if not on_act(m)]))

    sel_in, win_in = sem("sel_pages_in"), sem("win_rows_in")
    k.rows_cleared = sem("expert_rows_cleared")
    s_done, masked, p_ready, pm_ready = sem("score_done"), sem("score_masked"), sem("prob_ready"), sem("cmp_prob_ready")
    pt_done, pt_by_act, pt_by_dve, av_done = sem("pt_done"), sem("pt_by_act"), sem("pt_by_dve"), sem("av_done")
    o_out, ot_done = sem("o_out"), sem("ot_done")
    with ExitStack() as ctx:
        def sb(name, shape):
            return ctx.enter_context(nc.sbuf_tensor(name, shape, F32))
        sel = sb("sel_pages", [128, B, 2, 256])
        win = sb("win_rows", [128, B, 2, 256])
        P = sb("probs", [128, 3, 512])
        PT = sb("probsT", [128, 2, 512])
        sc = sb("cmp_scores", [128, 256])
        mx = sb("row_max", [128, 3])
        mx8 = sb("cmp_max", [128, 8])
        den = sb("den", [128, 2, 3, 8])
        wgt = sb("wgt", [128, 3, 8])
        acc = sb("acc", [128, 3, 512])
        otm = sb("otm", [128, NT, 512])
        osm = sb("osm", [128, 2, 128])
        block = ctx.enter_context(nc.Block())
        past = (sel, win)

        def vcol(br, kvh):
            return slice(KV0 + 256 * (br + 1) + 128 + kvh * HD, KV0 + 256 * (br + 1) + 128 + (kvh + 1) * HD)

        @block.sync
        def _(sp):
            for j in range(B * PAST // PAGE):
                page = sp.value_load(k.pt[0:1, j:j + 1], min_val=0, max_val=N_POOL - 1)
                sp.dma_start(sel[:, j // 2, j % 2, :], io["sel_pages"][l, page]).then_inc(sel_in, 16)
            sp.dma_start(win[:, :, :, :], io["win_rows"][l]).then_inc(win_in, 16)
            with sp.Fori(0, l * (MAXCH // 2 - 1) + 1):
                sp.sem_inc(k.rows_cleared, 16)
            with sp.Fori(l * (MAXCH // 2 - 1), MAXCH // 2) as p:
                sp.dma_start(io["ys"][bass.ds(p * 256, 256), :].rearrange("(p c) (q e) -> p (c q) e", p=128, e=256),
                             k.zrow[:, :].unsqueeze(1).broadcast_to([128, 8, 256])).then_inc(k.rows_cleared, 16)

        @block.tensor
        def _(pe):
            def scores(n):
                kind, t, kvh, i, br = units[n]
                bank = n % 3
                if n >= 3:
                    pe.wait_ge(p_ready, n - 2)
                if kind != "cmp":
                    lo, hi, m = {"kv": (t * 128, (t + 1) * 128, 128), "scmp": (0, 128, 256 + 128 * t),
                                 "skv": (256, 320, 512 + 64 * t)}[kind]
                    pe.matmul(ps[:, bank, lo:hi], k.mk[:, 0:128], k.mk[:, m:m + hi - lo], start=True,
                              stop=False, skip_group_check=True)
                if kind == "cmp":
                    out = ps[:, bank, 0:256].rearrange("p (h i c) -> p i h c", h=NKV, i=GQA)
                    for i in range(GQA):
                        last = pe.matmul(out[:, i, :, :], k.qT[:, i, t * 128:(t + 1) * 128], k.kcT[:, :, :],
                                         start=True, stop=True)
                elif kind == "kv":
                    last = pe.matmul(ps[:, bank, 0:(t + 1) * 128], k.qT[:, i, t * 128:(t + 1) * 128],
                                     k.KT[:, br, kvh, 0:(t + 1) * 128], start=False, stop=True,
                                     skip_group_check=True)
                elif kind == "scmp":
                    q = k.qsT[:, kvh, 4 * t:4 * t + 4, :, :].rearrange("p b i t -> p (b i t)")
                    last = pe.matmul(ps[:, bank, 0:128], q, k.kcsT[:, :], start=False, stop=True,
                                     skip_group_check=True)
                else:
                    pe.wait_ge((sel_in, win_in)[br], 16 * (B * PAST // PAGE, 1)[br])
                    q = k.qsT[:, kvh, 4 * t:4 * t + 4, :, :].rearrange("p b i t -> p (b i t)")
                    pe.matmul(ps[:, bank, 256:320], q, k.KTs[:, br, :], start=False, stop=True,
                              skip_group_check=True)
                    for b in range(4):
                        q = k.qsT[:, kvh, 4 * t + b, :, :].rearrange("p i t -> p (i t)")
                        last = pe.matmul(ps[32 * b:32 * b + 32, bank, 0:256].rearrange("p (a t) -> p a t", a=2), q,
                                         past[br][:, 4 * t + b, :, 0:128], start=True, stop=True)
                last.then_inc(s_done, 1)

            def transposes(n):
                kind, t, kvh, i, br = units[n]
                bank = 3 + n % 2
                if kind == "cmp":
                    pe.wait_ge(pm_ready, t + 1)
                pe.wait_ge(p_ready, n + 1)
                if n >= 2:
                    copied(pe, n - 2)
                w = {"cmp": 2, "kv": t + 1, "scmp": 1, "skv": 2}[kind]
                for a in range(w):
                    last = pe.transpose(ps[:, bank, a * 128:(a + 1) * 128], P[:, n % 3, a * 128:(a + 1) * 128], k.ident)
                if kind == "skv":
                    last = pe.transpose(ps[0:64, bank, 256:384], P[:, n % 3, 256:320], k.ident)
                last.then_inc(pt_done, 1)

            def values(n):
                kind, t, kvh, i, br = units[n]
                copied(pe, n)
                if group[n] and (n == 0 or group[n] != group[n - 1]):
                    pe.wait_ge(o_out, group[n])
                pt = PT[:, n % 2, :]
                if kind == "cmp":
                    for h in range(NKV):
                        last = pe.matmul(ps[:, 5, h * 256:(h + 1) * 256], pt[:, h * 128:(h + 1) * 128],
                                         k.vblk[:, h, :, :].rearrange("p i d -> p (i d)"), start=True, stop=True)
                elif kind == "kv":
                    out = ps[:, 6 + br, (kvh * 4 + i) * HD:(kvh * 4 + i + 1) * HD]
                    for a in range(t + 1):
                        last = pe.matmul(out, pt[:, a * 128:(a + 1) * 128], k.z[:, a, vcol(br, kvh)],
                                         start=(a == 0), stop=(a == t))
                elif kind == "scmp":
                    last = pe.matmul(ps[:, 5, kvh * HD:(kvh + 1) * HD], pt[:, 0:128], k.vcs[:, kvh, :],
                                     start=True, stop=True)
                else:
                    pe.matmul(ps[:, 6 + br, kvh * HD:(kvh + 1) * HD], pt[0:NS, 256:384], k.z[0:NS, NT, vcol(br, kvh)],
                              start=True, stop=False, skip_group_check=True)
                    for b in range(4):
                        for a in range(2):
                            last = pe.matmul(ps[32 * b:32 * b + 32, 6 + br, kvh * HD:(kvh + 1) * HD],
                                             pt[:, a * 128 + 32 * b:a * 128 + 32 * b + 32],
                                             past[br][:, 4 * t + b, a, 128 + kvh * HD:128 + (kvh + 1) * HD],
                                             start=False, stop=(a == 1), skip_group_check=True)
                last.then_inc(av_done, 1)

            for n in range(NU + LAG_V):
                if n < NU:
                    scores(n)
                if 0 <= n - LAG_T < NU:
                    transposes(n - LAG_T)
                if n >= LAG_V:
                    values(n - LAG_V)
            pe.wait_ge(o_out, NT + 2)
            for i in range(GQA):
                for t in range(NT):
                    last = pe.transpose(ps[:, i, t * 128:(t + 1) * 128], otm[:, t, i * 128:(i + 1) * 128], k.ident)
                last.then_inc(ot_done, 1)
            for g in range(2):
                last = pe.transpose(ps[:, 4, g * 128:(g + 1) * 128], osm[:, g, :], k.ident)
            last.then_inc(ot_done, 1)

        def copy_probs(eng, copy, n, done):
            kind, t, kvh, i, br = units[n]
            eng.wait_ge(pt_done, n + 1)
            if n >= 2:
                eng.wait_ge(av_done, n - 1)
            w = {"cmp": 256, "kv": (t + 1) * 128, "scmp": 128, "skv": 256}[kind]
            last = copy(PT[:, n % 2, 0:w], ps[:, 3 + n % 2, 0:w])
            if kind == "skv":
                last = copy(PT[0:NS, n % 2, 256:384], ps[0:NS, 3 + n % 2, 256:384])
            last.then_inc(done, 1)

        @block.scalar
        def _(act):
            def probs(n):
                kind, t, kvh, i, br = units[n]
                act.wait_ge(masked, n + 1)
                if n >= 3:
                    act.wait_ge(pt_done, n - 2)
                if kind == "cmp":
                    act.activation(P[:, n % 3, 0:256], sc[:, :], ACT.Exp).then_inc(p_ready, 1)
                    return
                w = {"kv": (t + 1) * 128, "scmp": 128, "skv": 320}[kind]
                g = group[n] % 2
                if kind == "kv":
                    d = den[:, g, br + 1, kvh * 4 + i:kvh * 4 + i + 1]
                else:
                    d = den[:, g, (0 if kind == "scmp" else br + 1), kvh:kvh + 1]
                act.activation(P[:, n % 3, 0:w], ps[:, n % 3, 0:w], ACT.Exp, bias=mx[:, n % 3:n % 3 + 1],
                               accum_out=d).then_inc(p_ready, 1)

            for n in range(NU + 2):
                if n < NU:
                    probs(n)
                if n >= 2 and on_act(n - 2):
                    copy_probs(act, act.copy, n - 2, pt_by_act)
            for i in range(GQA):
                act.wait_ge(ot_done, i + 1)
                act.copy(k.oT[:, 4 + i, 0:SEQ], ps[:, i, :])

        @block.vector
        def _(dve):
            step = k.dve.after

            def mask(n):
                kind, t, kvh, i, br = units[n]
                S = ps[:, n % 3, :]
                dve.wait_ge(s_done, n + 1)
                if kind == "cmp":
                    s3 = sc[:, :].rearrange("p (h c) -> p h c", h=8)
                    neg = c["cneg"][:, 32 * t:32 * t + 32].unsqueeze(1).broadcast_to([128, 8, 32])
                    ok = c["cm"][:, 32 * t:32 * t + 32].unsqueeze(1).broadcast_to([128, 8, 32])
                    step(dve.tensor_tensor(s3, S[:, 0:256].rearrange("p (h c) -> p h c", h=8), neg, ALU.add))
                    step(dve.tensor_reduce(mx8[:, :], s3, AX.X, ALU.max))
                    dve.tensor_tensor(s3, s3, mx8[:, :].unsqueeze(2).broadcast_to([128, 8, 32]),
                                      ALU.subtract).then_inc(masked, 1)
                    dve.wait_ge(p_ready, n + 1)
                    p3 = P[:, n % 3, 0:256].rearrange("p (h c) -> p h c", h=8)
                    dve.tensor_tensor(p3, p3, ok, ALU.mult).then_inc(pm_ready, 1)
                    dve.wait_ge(pm_ready, t + 1)
                    dve.tensor_reduce(den[:, group[n] % 2, 0, :], p3, AX.X, ALU.add)
                    return
                w = {"kv": (t + 1) * 128, "scmp": 128, "skv": 320}[kind]
                if n >= 3:
                    dve.wait_ge(p_ready, n - 2)
                dve.tensor_reduce(mx[:, n % 3:n % 3 + 1], S[:, 0:w], AX.X, ALU.max, negate=True).then_inc(masked, 1)

            def finish(gr):
                dve.wait_ge(av_done, last_of[gr] + 1)
                dve.wait_ge(p_ready, last_of[gr] + 1)
                if gr < NT:
                    n, gates = 8, k.gates[:, gr, :].rearrange("p (h c) -> p c h", c=3)
                    dst = otm[:, gr, :].rearrange("p (i h d) -> p h i d", i=4, h=2)
                else:
                    n, gates = 2, k.gsr[:, gr - NT, :, :].rearrange("p h c -> p c h")
                    dst = osm[:, gr - NT, :]
                d, w = den[:, gr % 2, :, 0:n], wgt[:, :, 0:n]
                step(dve.tensor_scalar(w, d, 1e-30, None, ALU.max))
                step(dve.reciprocal(w, w))
                step(dve.tensor_tensor(w, w, gates, ALU.mult))
                for b in range(3):
                    last = dve.tensor_tensor(acc[:, b, 0:n * HD].rearrange("p (h d) -> p h d", d=HD),
                                             ps[:, 5 + b, 0:n * HD].rearrange("p (h d) -> p h d", d=HD),
                                             wgt[:, b, 0:n].unsqueeze(2).broadcast_to([128, n, HD]), ALU.mult)
                step(last)
                a = [acc[:, b, 0:n * HD] for b in range(3)]
                step(dve.tensor_tensor(a[0], a[0], a[1], ALU.add))
                if gr < NT:
                    a = [x.rearrange("p (h i d) -> p h i d", h=2, i=4) for x in a]
                dve.tensor_tensor(dst, a[0], a[2], ALU.add).then_inc(o_out, 1)

            for n in range(NU + LAG_V + 1):
                if n < NU:
                    mask(n)
                if 2 <= n < NU + 2 and not on_act(n - 2):
                    copy_probs(dve, dve.tensor_copy, n - 2, pt_by_dve)
                for gr in range(NT + 2):
                    if last_of[gr] + LAG_V == n:
                        finish(gr)
            dve.wait_ge(ot_done, GQA + 1)
            src = ps[:, 4, 0:256].rearrange("p (b i t) -> p b i t", b=B, i=4)
            for i in range(GQA):
                dve.tensor_copy(k.oT[:, 4 + i, SEQ:TOK].rearrange("p (b t) -> p b t", b=B), src[:, :, i, :])


class Norm:

    def __init__(self, k, name, row, eps, ctx):
        self.k, self.eps = k, eps
        sem = k.sem
        self.summed, self.rstd_ready = sem(name + "_stats"), sem(name + "_rstd")
        self.scaled, self.ready = sem(name + "_scaled"), sem(name + "_ready")
        self.t_done, self.t_out, self.vec_in = sem(name + "_t_done"), sem(name + "_t_out"), sem(name + "_vec_in")
        nc = k.nc
        self.vec = ctx.enter_context(nc.sbuf_tensor(name + "_gb", [128, 2, D], F32))
        self.st = ctx.enter_context(nc.sbuf_tensor(name + "_st", [128, NTT, 2, 6], F32))
        self.mv = ctx.enter_context(nc.sbuf_tensor(name + "_mv", [128, NTT, 2], F32))
        self.rs = ctx.enter_context(nc.sbuf_tensor(name + "_rs", [128, NTT], F32))
        self.row = row

    def load(self, eng):
        src = self.k.io["ln"][self.k.layer, self.row:self.row + 2, :].unsqueeze(0).broadcast_to([128, 2, D])
        eng.dma_start(self.vec[:, :, :], src).then_inc(self.vec_in, 16)

    def stats(self, dve, i):
        k, rows = self.k, TILES[i]
        for n in range(2):
            last = dve.bn_stats(self.st[0:rows, i, n, :], k.x[0:rows, i, n * 512:(n + 1) * 512])
        k.dve.after(last)
        dve.bn_aggr(self.mv[0:rows, i, :], self.st[0:rows, i, :, :].rearrange("p a s -> p (a s)")).then_inc(self.summed, 1)

    def rstd(self, pool, i):
        rows = TILES[i]
        pool.wait_ge(self.summed, i + 1)
        r = self.rs[0:rows, i:i + 1]
        self.k.pool.after(pool.tensor_scalar(r, self.mv[0:rows, i, 1:2], self.eps, None, ALU.add))
        pool.tensor_tensor(r, r, self.k.c["mhalf"][0:rows, 0:1], ALU.pow).then_inc(self.rstd_ready, 1)

    def scale(self, dve, i):
        k, rows = self.k, TILES[i]
        x = k.x[0:rows, i, :]
        if i == 0:
            dve.wait_ge(self.vec_in, 16)
        dve.wait_ge(self.rstd_ready, i + 1)
        k.dve.after(dve.tensor_scalar(x, x, self.mv[0:rows, i, 0:1], self.rs[0:rows, i:i + 1], ALU.subtract, ALU.mult))
        dve.tensor_tensor(x, x, self.vec[0:rows, 0, :], ALU.mult).then_inc(self.scaled, 1)

    def shift(self, pool, i):
        k, rows = self.k, TILES[i]
        x = k.x[0:rows, i, :]
        pool.wait_ge(self.scaled, i + 1)
        pool.tensor_tensor(x, x, self.vec[0:rows, 1, :], ALU.add).then_inc(self.ready, 1)

    def transposes(self, pe, i):
        k, rows = self.k, TILES[i]
        pe.wait_ge(self.ready, i + 1)
        if i:
            pe.wait_ge(self.t_out, i)
        for kk in range(KT_D):
            last = pe.transpose(k.ps[:, 6 + kk // 4, kk % 4 * 128:kk % 4 * 128 + rows],
                                k.x[0:rows, i, kk * 128:(kk + 1) * 128], k.ident[0:rows, 0:rows])
        last.then_inc(self.t_done, 1)

    def copies(self, act, i):
        k, rows = self.k, TILES[i]
        act.wait_ge(self.t_done, i + 1)
        for h in range(2):
            last = act.copy(k.xT[:, 4 * h:4 * h + 4, i * 128:i * 128 + rows],
                            k.ps[:, 6 + h, :].rearrange("p (a t) -> p a t", a=4)[:, :, 0:rows])
        last.then_inc(self.t_out, 1)


def merge(k):
    nc, io, l, ps = k.nc, k.io, k.layer, k.ps
    sem = k.sem
    RING = 3
    wm_in, wo_in = [sem(f"wm_in{n}") for n in range(RING)], sem("wo_in")
    gb_done, g_ready, b_out, merged = sem("gate_branch_done"), sem("gate_ready"), sem("branch_out"), sem("merged")
    m_done, m_out, x1_stored = sem("mix_product_done"), sem("mix_product_out"), sem("x1_stored")
    k.x1_stored = x1_stored
    with ExitStack() as ctx:
        def sb(name, shape):
            return ctx.enter_context(nc.sbuf_tensor(name, shape, F32))
        wm = sb("wm", [128, RING, 4096])
        wo = sb("wo", [128, KT_D, D])
        tg = sb("tanh_gate", [128, 2, TOK])
        part = sb("branch_part", [128, TOK])
        mT = sb("mergedT", [128, KT_D, TOK])
        norm = Norm(k, "ln1", 0, 4 * EPS, ctx)
        block = ctx.enter_context(nc.Block())
        TILE_OF = ((0, 1), (2, 3), (4, 5, 6, 7))
        NU = KT_D * 3

        @block.sync
        def _(sp):
            for m in range(KT_D):
                if m >= RING:
                    sp.wait_ge(gb_done, 3 * (m - RING + 1))
                sp.dma_start(wm[:, m % RING, :], io["wm"][l, m]).then_inc(wm_in[m % RING], 16)
                if m == RING:
                    sp.dma_start(wo[:, :, :], io["wo"][l]).then_inc(wo_in, 16)
            norm.load(sp)
            for i, rows in enumerate(TILES):
                sp.wait_ge(norm.ready, i + 1)
                sp.dma_start(io["x1"][i * 128:i * 128 + rows, :], k.x[0:rows, i, :]).then_inc(x1_stored, 16)

        @block.tensor
        def _(pe):
            for m in range(KT_D):
                pe.wait_ge(wm_in[m % RING], 16 * (m // RING + 1))
                wg = wm[:, m % RING, 0:3072].rearrange("p (k c) -> p k c", k=KT_D)
                wb = wm[:, m % RING, 3072:4096].rearrange("p (k c) -> p k c", k=KT_D)
                for b in range(3):
                    u = 3 * m + b
                    base = 3 * (u % 2)
                    if u >= 2:
                        pe.wait_ge(b_out, u - 1)
                    for kk in range(KT_D):
                        pe.matmul(ps[:, base, :], wg[:, kk, b * 128:(b + 1) * 128], k.xT[:, kk, 0:SEQ],
                                  start=(kk == 0), stop=(kk == KT_D - 1))
                    for kk in range(KT_D):
                        pe.matmul(ps[:, base + 2, 0:NS], wg[:, kk, b * 128:(b + 1) * 128], k.xT[:, kk, SEQ:TOK],
                                  start=(kk == 0), stop=(kk == KT_D - 1))
                    ks = TILE_OF[b]
                    for kk in ks:
                        pe.matmul(ps[:, base + 1, :], wb[:, kk, :], k.oT[:, kk, 0:SEQ],
                                  start=(kk == ks[0]), stop=(kk == ks[-1]))
                    for kk in ks:
                        last = pe.matmul(ps[:, base + 2, NS:2 * NS], wb[:, kk, :], k.oT[:, kk, SEQ:TOK],
                                         start=(kk == ks[0]), stop=(kk == ks[-1]))
                    last.then_inc(gb_done, 1)
            pe.wait_ge(wo_in, 16)
            pe.wait_ge(merged, KT_D)
            for j in range(2 * NTT + 2):
                if j < 2 * NTT:
                    i, n = j // 2, j % 2
                    if j >= 6:
                        pe.wait_ge(m_out, j - 5)
                    for kk in range(KT_D):
                        last = pe.matmul(ps[0:TILES[i], j % 6, :], mT[:, kk, i * 128:i * 128 + TILES[i]],
                                         wo[:, kk, n * 512:(n + 1) * 512], start=(kk == 0), stop=(kk == KT_D - 1))
                    last.then_inc(m_done, 1)
                if j >= 4 and j % 2 == 0:
                    norm.transposes(pe, j // 2 - 2)
            norm.transposes(pe, NTT - 1)

        @block.scalar
        def _(act):
            for u in range(NU):
                base = 3 * (u % 2)
                act.wait_ge(gb_done, u + 1)
                if u >= 2:
                    act.wait_ge(b_out, u - 1)
                act.activation(tg[:, u % 2, 0:SEQ], ps[:, base, :], ACT.Tanh, scale=0.5)
                act.activation(tg[:, u % 2, SEQ:TOK], ps[:, base + 2, 0:NS], ACT.Tanh, scale=0.5).then_inc(g_ready, 1)
            for i in range(NTT):
                norm.copies(act, i)

        @block.vector
        def _(dve):
            for u in range(NU):
                m, b, base = u // 3, u % 3, 3 * (u % 2)
                dve.wait_ge(g_ready, u + 1)
                dst = mT[:, m, :] if b == 0 else part[:, :]
                dve.scalar_tensor_tensor(dst[:, 0:SEQ], tg[:, u % 2, 0:SEQ], 1.0, ps[:, base + 1, :], ALU.add, ALU.mult)
                last = dve.scalar_tensor_tensor(dst[:, SEQ:TOK], tg[:, u % 2, SEQ:TOK], 1.0, ps[:, base + 2, NS:2 * NS],
                                                ALU.add, ALU.mult)
                last.then_inc(b_out, 1)
                if b:
                    dve.wait_ge(b_out, u + 1)
                    last = dve.tensor_tensor(mT[:, m, :], mT[:, m, :], part[:, :], ALU.add)
                    if b == 1:
                        k.dve.after(last)
                    else:
                        last.then_inc(merged, 1)
                        dve.wait_ge(merged, m + 1)
            dve.wait_ge(k.x_in, 32)
            for i in range(NTT + 1):
                if i < NTT:
                    rows = TILES[i]
                    for n in range(2):
                        dve.wait_ge(m_done, 2 * i + n + 1)
                        xs = k.x[0:rows, i, n * 512:(n + 1) * 512]
                        dve.scalar_tensor_tensor(xs, xs, 2 * ALPHA, ps[0:rows, (2 * i + n) % 6, :],
                                                 ALU.mult, ALU.add).then_inc(m_out, 1)
                    dve.wait_ge(m_out, 2 * i + 2)
                    norm.stats(dve, i)
                if i:
                    norm.scale(dve, i - 1)

        @block.gpsimd
        def _(pool):
            for i in range(NTT + 1):
                if i < NTT:
                    norm.rstd(pool, i)
                if i:
                    norm.shift(pool, i - 1)


def experts(k):
    nc, io, l, ps, c = k.nc, k.io, k.layer, k.ps, k.c
    sem = k.sem
    lg_done, ex_ready, sel_ready, rank_done = sem("logits_done"), sem("exp_ready"), sem("choice_ready"), sem("rank_done")
    plan_ready, ex_clear, table_zeroed, table_in = (sem("plan_ready"), sem("exp_cleared"), sem("table_zeroed"),
                                                    sem("table_written"))
    gu_in = [sem("gate_up_in_a"), sem("gate_up_in_b")]
    dw_in = [sem("down_in_a"), sem("down_in_b")]
    idx_in, x_in = [sem("idx_in_a"), sem("idx_in_b")], [sem("rows_in_a"), sem("rows_in_b")]
    xt_done, xt_act, xt_dve = sem("rowsT_done"), sem("rowsT_by_act"), sem("rowsT_by_dve")
    gu_done, act_ready = sem("gate_up_done"), sem("hidden_ready")
    tanh_ready2 = [sem("silu_ready_a"), sem("silu_ready_b")]
    tanh_ready, at_done, at_out = sem("gate_tanh_ready"), sem("hiddenT_done"), sem("hiddenT_out")
    dn_done = [sem("down_done_a"), sem("down_done_b")]
    y_act, y_dve, y_stored = sem("y_by_act"), sem("y_by_dve"), [sem("y_stored_a"), sem("y_stored_b")]
    x_stored = sem("layer_output_stored")
    all_stored = sem("all_expert_rows_stored")
    yg_in, y_used = [sem(f"y_rows_in{i}") for i in range(2)], sem("y_rows_used")

    with ExitStack() as outer:
        def so(name, shape, dt=F32):
            return outer.enter_context(nc.sbuf_tensor(name, shape, dt))
        norm = Norm(k, "ln2", 2, EPS, outer)
        slot = so("slot", [128, 2, NTT], I32)
        wt = so("pair_weight", [128, 2, NTT])
        plan = so("plan", [1, 34], I32)
        with ExitStack() as ctx:
            def sb(name, shape, dt=F32):
                return ctx.enter_context(nc.sbuf_tensor(name, shape, dt))
            S3 = [128, NTT, E]
            ex, aff, score, ms, t1 = sb("ex", S3), sb("aff", S3), sb("score", S3), sb("ms", S3), sb("rt1", S3)
            oh = sb("onehot", [128, 2, NTT, E])
            both = sb("both", S3)
            g = sb("grp", [128, 8, NTT, EG])
            v = sb("rv", [128, 4, NTT])
            cnt, nch, cum, basev = sb("cnt", [128, E]), sb("nch", [128, E]), sb("cum", [128, E]), sb("base", [128, E])
            big = sb("cmpbuf", [128, 32, E])
            pf = sb("plan_f", [1, 34])
            slotf = sb("slot_f", [128, 2, NTT])
            gu = [sb("gate_up_a", [128, 4096]), sb("gate_up_b", [128, 4096])]
            dw = [sb("down_a", [128, 2048]), sb("down_b", [128, 2048])]
            idx = [sb("idx_a", [128, 1], I32), sb("idx_b", [128, 1], I32)]
            xg = [sb("rows_a", [128, D]), sb("rows_b", [128, D])]
            xgT = [sb("rowsT_a", [128, KT_D, 128]), sb("rowsT_b", [128, KT_D, 128])]
            tgt = [sb("gtanh_a", [128, FE]), sb("gtanh_b", [128, FE])]
            h1 = [sb("hid_a", [128, FE]), sb("hid_b", [128, FE])]
            hT = [sb("hidT_a", [128, 2, 128]), sb("hidT_b", [128, 2, 128])]
            y = [sb("y_a", [128, D]), sb("y_b", [128, D])]
            block = ctx.enter_context(nc.Block())
            XB, GB, HB, YB = [0, 2], [4, 5], [0, 1], [6, 2]

            def pairs(eng):
                eng.wait_ge(plan_ready, 1)
                return eng.value_load(plan[0:1, 32:33], min_val=1, max_val=MAXCH // 2)

            @block.sync
            def _(sp):
                norm.load(sp)
                with sp.Fori(0, pairs(sp)) as p:
                    e = [sp.value_load(plan[0:1, bass.ds(2 * p + a, 1)], min_val=0, max_val=E - 1) for a in range(2)]
                    for a in range(2):
                        sp.wait_ge(gu_done, 2 * p + a + 1)
                        sp.dma_start(gu[a][:, :], io["we"][l, e[a], :, 0:4096]).then_inc(gu_in[a], 16)
                    sp.wait_ge(table_in, 16 * 2 * NTT)
                    for a in range(2):
                        sp.wait_ge(xt_done, 2 * p + 1)
                        sp.dma_start(idx[a][:, :], io["slot_token"][bass.ds((2 * p + a) * 128, 128), :]).then_inc(idx_in[a], 16)
                    for a in range(2):
                        sp.wait_ge(dn_done[a], p + 1)
                        sp.dma_start(dw[a][:, :], io["we"][l, e[a], :, 4096:6144]).then_inc(dw_in[a], 16)

            @block.tensor
            def _(pe):
                for i, rows in enumerate(TILES):
                    for kk in range(KT_D):
                        last = pe.matmul(ps[0:rows, 0, i * E:(i + 1) * E], k.xT[:, kk, i * 128:i * 128 + rows],
                                         k.wr[:, kk, :], start=(kk == 0), stop=(kk == KT_D - 1))
                last.then_inc(lg_done, 1)
                pe.wait_ge(sel_ready, 1)
                for i, rows in enumerate(TILES):
                    for j in range(i):
                        pe.matmul(ps[0:rows, 1, i * E:(i + 1) * E], c["ones"][:, 0:rows], both[:, j, :],
                                  start=(j == 0), stop=False)
                    pe.matmul(ps[0:rows, 1, i * E:(i + 1) * E], c["tri"][0:rows, 0:rows], both[0:rows, i, :],
                              start=(i == 0), stop=True)
                for j, rows in enumerate(TILES):
                    last = pe.matmul(ps[:, 1, NTT * E:(NTT + 1) * E], c["ones"][0:rows, :], both[0:rows, j, :],
                                     start=(j == 0), stop=(j == NTT - 1))
                last.then_inc(rank_done, 1)
                for s in (xt_done, dn_done[0], dn_done[1]):
                    pe.sem_inc(s, 1)
                pe.sem_inc(gu_done, 2)
                with pe.Fori(0, pairs(pe)) as p:
                    for a in range(2):
                        pe.wait_ge(x_in[a], 16 * p + 16)
                        pe.wait_ge(y_act, 2 * p + 1)
                        pe.wait_ge(y_dve, 2 * p + 1)
                        for kk in range(KT_D):
                            last = pe.transpose(ps[:, XB[a] + kk // 4, kk % 4 * 128:(kk % 4 + 1) * 128],
                                                xg[a][:, kk * 128:(kk + 1) * 128], k.ident)
                        last.then_inc(xt_done, 1)
                    for a in range(2):
                        pe.wait_ge(gu_in[a], 16 * p + 16)
                        pe.wait_ge(xt_act, 2 * p + a + 1)
                        pe.wait_ge(xt_dve, 2 * p + a + 1)
                        for kk in range(KT_D):
                            last = pe.matmul(ps[:, GB[a], :], xgT[a][:, kk, :], gu[a][:, kk * 512:(kk + 1) * 512],
                                             start=(kk == 0), stop=(kk == KT_D - 1))
                        last.then_inc(gu_done, 1)
                    for a in range(2):
                        pe.wait_ge(act_ready, 2 * p + a + 1)
                        for f in range(2):
                            last = pe.transpose(ps[:, HB[a], f * 128:(f + 1) * 128], h1[a][:, f * 128:(f + 1) * 128], k.ident)
                        last.then_inc(at_done, 1)
                        pe.wait_ge(at_out, 2 * p + a + 1)
                        pe.wait_ge(dw_in[a], 16 * p + 16)
                        for n in range(2):
                            for f in range(2):
                                last = pe.matmul(ps[:, YB[a] + n, :], hT[a][:, f, :],
                                                 dw[a][:, f * D + n * 512:f * D + (n + 1) * 512],
                                                 start=(f == 0), stop=(f == 1))
                        last.then_inc(dn_done[a], 1)

            @block.scalar
            def _(act):
                act.wait_ge(lg_done, 1)
                act.wait_ge(ex_clear, 1)
                act.activation(ex[:, 0:NT, :], ps[:, 0, 0:NT * E].rearrange("p (i e) -> p i e", i=NT), ACT.Exp, scale=-1.0)
                act.activation(ex[0:NS, NT, :], ps[0:NS, 0, NT * E:NTT * E], ACT.Exp, scale=-1.0).then_inc(ex_ready, 1)
                act.sem_inc(y_act, 1)
                for s in y_stored:
                    act.sem_inc(s, 16)
                act.wait_ge(k.rows_cleared, 16 * (MAXCH // 2 + 1))
                with act.Fori(0, pairs(act)) as p:
                    for a in range(2):
                        act.wait_ge(xt_done, 2 * p + a + 2)
                        act.copy(xgT[a][:, 0:4, :], ps[:, XB[a], :].rearrange("p (a t) -> p a t", a=4)).then_inc(xt_act, 1)
                    for a in range(2):
                        act.wait_ge(gu_done, 2 * p + a + 3)
                        act.activation(tgt[a][:, :], ps[:, GB[a], 0:FE], ACT.Tanh, scale=0.5).then_inc(tanh_ready, 1)
                    for a in range(2):
                        act.wait_ge(dn_done[a], p + 2)
                        act.wait_ge(y_stored[a], 16 * p + 16)
                        act.copy(y[a][:, 0:512], ps[:, YB[a], :]).then_inc(y_act, 1)
                        act.wait_ge(y_act, 2 * p + a + 2)
                        act.wait_ge(y_dve, 2 * p + a + 2)
                        act.dma_start(io["ys"][bass.ds((2 * p + a) * 128, 128), :], y[a][:, :]).then_inc(y_stored[a], 16)

            @block.gpsimd
            def _(pool):
                pool.dma_start(io["slot_token"].rearrange("(p c) o -> p (c o)", p=128), k.zero[:, :]).then_inc(table_zeroed, 16)
                pool.wait_ge(table_zeroed, 16)
                pool.wait_ge(plan_ready, 1)
                for a in range(2):
                    for i, rows in enumerate(TILES):
                        pool.indirect_dma_start(io["slot_token"], bass.IndirectOffsetOnAxis(slot[0:rows, a, i:i + 1], 0),
                                                k.tokid[0:rows, i:i + 1], None).then_inc(table_in, 16)
                pool.wait_ge(table_in, 16 * 2 * NTT)
                pool.wait_ge(k.x1_stored, 16 * NTT)
                n = pairs(pool)
                with pool.Fori(0, n) as p:
                    for a in range(2):
                        pool.wait_ge(idx_in[a], 16)
                        pool.sem_clear(idx_in[a])
                        pool.indirect_dma_start(xg[a][:, :], None, io["x1"], bass.IndirectOffsetOnAxis(idx[a][:, 0:1], 0)
                                                ).then_inc(x_in[a], 16)

            @block.vector
            def _(dve):
                step = k.dve.after
                dve.memset(ex[:, :, :], 1.0).then_inc(ex_clear, 1)
                dve.memset(g[:, :, :, :], 0.0)
                dve.wait_ge(ex_ready, 1)
                step(dve.tensor_scalar(aff[:, :, :], ex[:, :, :], 1.0, None, ALU.add))
                step(dve.reciprocal(aff[:, :, :], aff[:, :, :]))
                step(dve.tensor_tensor(score[:, :, :], aff[:, :, :], k.br[:, :].unsqueeze(1).broadcast_to(S3), ALU.add))
                s4 = score[:, :, :].rearrange("p i (g e) -> p i g e", g=EG)
                G = [g[:, n, :, :] for n in range(8)]
                step(dve.tensor_tensor(G[0], s4[:, :, :, 0], s4[:, :, :, 1], ALU.max))
                step(dve.tensor_tensor(G[1], s4[:, :, :, 0], s4[:, :, :, 1], ALU.min))
                step(dve.tensor_tensor(G[2], s4[:, :, :, 2], s4[:, :, :, 3], ALU.max))
                step(dve.tensor_tensor(G[3], s4[:, :, :, 2], s4[:, :, :, 3], ALU.min))
                step(dve.tensor_tensor(G[4], G[0], G[2], ALU.max))
                step(dve.tensor_tensor(G[5], G[0], G[2], ALU.min))
                step(dve.tensor_tensor(G[6], G[1], G[3], ALU.max))
                step(dve.tensor_tensor(G[5], G[5], G[6], ALU.max))
                step(dve.tensor_tensor(G[4], G[4], G[5], ALU.add))

                def first_best(val, out, order, width, tmp):
                    shape = [128, NTT, width]
                    step(dve.tensor_reduce(v[:, 0, :], val, AX.X, ALU.max))
                    step(dve.tensor_tensor(tmp, val, v[:, 0, :].unsqueeze(2).broadcast_to(shape), ALU.is_equal))
                    step(dve.tensor_tensor(tmp, tmp, order.unsqueeze(1).broadcast_to(shape), ALU.mult))
                    step(dve.tensor_reduce(v[:, 1, :], tmp, AX.X, ALU.max))
                    step(dve.tensor_tensor(out, tmp, v[:, 1, :].unsqueeze(2).broadcast_to(shape), ALU.is_equal))

                first_best(G[4], G[0], c["g4"], EG, G[1])
                step(dve.tensor_scalar(G[1], G[0], 1.0, -NEG, ALU.subtract, ALU.mult))
                ms4 = ms[:, :, :].rearrange("p i (g e) -> p i g e", g=EG)
                for e in range(E // EG):
                    step(dve.tensor_tensor(ms4[:, :, :, e], s4[:, :, :, e], G[0], ALU.mult))
                    step(dve.tensor_tensor(ms4[:, :, :, e], ms4[:, :, :, e], G[1], ALU.add))
                first_best(ms[:, :, :], oh[:, 0, :, :], c["e16"], E, t1[:, :, :])
                step(dve.tensor_scalar(t1[:, :, :], oh[:, 0, :, :], 3 * NEG, None, ALU.mult))
                step(dve.tensor_tensor(ms[:, :, :], ms[:, :, :], t1[:, :, :], ALU.add))
                first_best(ms[:, :, :], oh[:, 1, :, :], c["e16"], E, t1[:, :, :])
                dve.tensor_tensor(both[:, :, :], oh[:, 0, :, :], oh[:, 1, :, :], ALU.add).then_inc(sel_ready, 1)
                for a in range(2):
                    step(dve.tensor_tensor(t1[:, :, :], oh[:, a, :, :], aff[:, :, :], ALU.mult))
                    step(dve.tensor_reduce(v[:, a, :], t1[:, :, :], AX.X, ALU.add))
                step(dve.tensor_tensor(v[:, 2, :], v[:, 0, :], v[:, 1, :], ALU.add))
                step(dve.reciprocal(v[:, 2, :], v[:, 2, :]))
                step(dve.tensor_scalar(v[:, 2, :], v[:, 2, :], 0.5, None, ALU.mult))
                step(dve.tensor_tensor(wt[:, :, :], v[:, 0:2, :], v[:, 2, :].unsqueeze(1).broadcast_to([128, 2, NTT]), ALU.mult))
                dve.wait_ge(rank_done, 1)
                step(dve.tensor_copy(cnt[:, :], ps[:, 1, NTT * E:(NTT + 1) * E]))
                step(dve.tensor_tensor(big[:, 0:5, :], cnt[:, :].unsqueeze(1).broadcast_to([128, 5, E]),
                                       c["th"].unsqueeze(2).broadcast_to([128, 5, E]), ALU.is_gt))
                step(dve.tensor_reduce(nch[:, :], big[:, 0:5, :].rearrange("p m e -> p e m"), AX.X, ALU.add))
                step(dve.tensor_tensor_scan(cum[:, :], c["ones"][:, 0:E], nch[:, :], 0.0, ALU.mult, ALU.add))
                step(dve.tensor_tensor(basev[:, :], cum[:, :], nch[:, :], ALU.subtract))
                step(dve.tensor_scalar(basev[:, :], basev[:, :], 128.0, None, ALU.mult))
                step(dve.tensor_copy(t1[:, :, :], basev[:, :].unsqueeze(1).broadcast_to(S3)))
                step(dve.tensor_tensor(t1[:, 0:NT, :], ps[:, 1, 0:NT * E].rearrange("p (i e) -> p i e", i=NT),
                                       t1[:, 0:NT, :], ALU.add))
                step(dve.tensor_tensor(t1[0:NS, NT, :], ps[0:NS, 1, NT * E:NTT * E], t1[0:NS, NT, :], ALU.add))
                for a in range(2):
                    step(dve.tensor_tensor(ms[:, :, :], t1[:, :, :], oh[:, a, :, :], ALU.mult))
                    step(dve.tensor_reduce(slotf[:, a, :], ms[:, :, :], AX.X, ALU.add))
                dve.tensor_copy(slot[:, :, :], slotf[:, :, :])
                chunk = c["chunk"][0:1, :]
                step(dve.tensor_tensor(big[0:1, :, :], cum[0:1, :].unsqueeze(1).broadcast_to([1, 32, E]),
                                       chunk.unsqueeze(2).broadcast_to([1, 32, E]), ALU.is_le))
                step(dve.tensor_reduce(pf[:, 0:32], big[0:1, :, :], AX.X, ALU.add))
                step(dve.tensor_scalar(pf[:, 0:32], pf[:, 0:32], float(E - 1), None, ALU.min))
                step(dve.tensor_scalar(cum[0:1, 0:1], cum[0:1, E - 1:E], 0.5, None, ALU.mult))
                step(dve.tensor_tensor(big[0:1, :, 0], chunk, cum[0:1, 0:1].broadcast_to([1, 32]), ALU.is_lt))
                step(dve.tensor_reduce(pf[:, 32:33], big[0:1, :, 0], AX.X, ALU.add))
                step(dve.memset(pf[:, 33:34], 0.0))
                dve.tensor_copy(plan[:, :], pf[:, :]).then_inc(plan_ready, 1)
                dve.wait_ge(plan_ready, 1)
                dve.sem_inc(y_dve, 1)
                with dve.Fori(0, pairs(dve)) as p:
                    for a in range(2):
                        dve.wait_ge(xt_done, 2 * p + a + 2)
                        dve.tensor_copy(xgT[a][:, 4:8, :],
                                        ps[:, XB[a] + 1, :].rearrange("p (a t) -> p a t", a=4)).then_inc(xt_dve, 1)
                    for a in range(2):
                        dve.wait_ge(tanh_ready, 2 * p + a + 1)
                        dve.scalar_tensor_tensor(tgt[a][:, :], tgt[a][:, :], 1.0, ps[:, GB[a], 0:FE],
                                                 ALU.add, ALU.mult).then_inc(tanh_ready2[a], 1)
                        dve.wait_ge(tanh_ready2[a], p + 1)
                        dve.tensor_tensor(h1[a][:, :], tgt[a][:, :], ps[:, GB[a], FE:2 * FE], ALU.mult).then_inc(act_ready, 1)
                    for a in range(2):
                        dve.wait_ge(at_done, 2 * p + a + 1)
                        dve.tensor_copy(hT[a][:, :, :], ps[:, HB[a], 0:256].rearrange("p (a t) -> p a t", a=2)).then_inc(at_out, 1)
                        dve.wait_ge(dn_done[a], p + 2)
                        dve.wait_ge(y_stored[a], 16 * p + 16)
                        dve.tensor_copy(y[a][:, 512:1024], ps[:, YB[a] + 1, :]).then_inc(y_dve, 1)

        with ExitStack() as ctx:
            yg = ctx.enter_context(nc.sbuf_tensor("y_rows", [128, 2, 2, D], F32))
            tmp = ctx.enter_context(nc.sbuf_tensor("y_sum", [128, D], F32))
            block = ctx.enter_context(nc.Block())

            @block.gpsimd
            def _(pool):
                pool.wait_ge(all_stored, 1)

                def gather(i):
                    rows = TILES[i]
                    if i >= 2:
                        pool.wait_ge(y_used, i - 1)
                    for a in range(2):
                        pool.indirect_dma_start(yg[0:rows, i % 2, a, :], None, io["ys"],
                                                bass.IndirectOffsetOnAxis(slot[0:rows, a, i:i + 1], 0)).then_inc(yg_in[i % 2], 16)
                gather(0)
                gather(1)
                for i in range(NTT + 1):
                    if i < NTT:
                        norm.rstd(pool, i)
                    if i:
                        norm.shift(pool, i - 1)
                    if i + 2 < NTT:
                        gather(i + 2)
                n = pool.value_load(plan[0:1, 32:33], min_val=1, max_val=MAXCH // 2)
                for a in range(2):
                    pool.wait_ge(x_in[a], 16 * n)
                pool.wait_ge(yg_in[0], 32 * 3)
                pool.wait_ge(yg_in[1], 32 * 2)
                pool.wait_ge(k.stored, 16 * k.n_stored)

            @block.vector
            def _(dve):
                for i in range(NTT + 1):
                    if i < NTT:
                        rows = TILES[i]
                        x, t = k.x[0:rows, i, :], tmp[0:rows, :]
                        dve.wait_ge(yg_in[i % 2], 32 * (i // 2 + 1))
                        k.dve.after(dve.tensor_scalar(t, yg[0:rows, i % 2, 1, :], wt[0:rows, 1, i:i + 1], None, ALU.mult))
                        dve.scalar_tensor_tensor(t, yg[0:rows, i % 2, 0, :], wt[0:rows, 0, i:i + 1], t,
                                                 ALU.mult, ALU.add).then_inc(y_used, 1)
                        dve.wait_ge(y_used, i + 1)
                        k.dve.after(dve.scalar_tensor_tensor(x, x, ALPHA, t, ALU.mult, ALU.add))
                        norm.stats(dve, i)
                    if i:
                        norm.scale(dve, i - 1)

            @block.tensor
            def _(pe):
                for i in range(NTT):
                    norm.transposes(pe, i)

            @block.scalar
            def _(act):
                for i in range(NTT):
                    norm.copies(act, i)

            @block.sync
            def _(sp):
                n = sp.value_load(plan[0:1, 32:33], min_val=1, max_val=MAXCH // 2)
                for a in range(2):
                    sp.wait_ge(y_stored[a], 16 * n + 16)
                sp.sem_inc(all_stored, 1)
                for i, rows in enumerate(TILES):
                    sp.wait_ge(norm.ready, i + 1)
                    out = io["y_p"][i * 128:(i + 1) * 128, :] if i < NT else io["y_s"]
                    sp.dma_start(out, k.x[0:rows, i, :]).then_inc(x_stored, 16)
                sp.wait_ge(x_stored, 16 * NTT)
                sp.wait_ge(k.stored, 16 * k.n_stored)



def layouts(inp):
    a = {n: np.asarray(v) for n, v in inp.items()}
    c = np.ascontiguousarray
    out = {}
    xp, xs = a["x_prompt"].reshape(SEQ, D), a["x_sample"].reshape(NS, D)
    out["xp"], out["xs"] = xp, xs
    out["x0T"] = c(np.concatenate([xp, xs], 0).T.reshape(KT_D, 128, TOK).transpose(1, 0, 2))
    out["consts"] = constants()
    tok = np.zeros((128, NTT), np.int32)
    for i in range(NTT):
        tok[:, i] = np.minimum(i * 128 + np.arange(128), TOK - 1)
    out["tokid"] = tok
    out["page_table"] = a["page_table"].reshape(1, -1).astype(np.int32)
    out["w_router"] = a["w_router"]
    out["br"] = c(np.broadcast_to(a["b_router"], (128, E)))
    w = a["w_in"]
    pa, pu, pv, pq, pkv, pg, pm = (w[:, :, s:e] for s, e in ((0, 256), (256, 512), (512, 768), (768, 1280),
                                                             (1280, 2048), (2048, 2072), (2072, 5144)))
    pq = pq.reshape(L, D, NKV, GQA, HD).transpose(0, 1, 3, 2, 4).reshape(L, D, 512)
    tm = np.concatenate([pq, pkv, pa, pv, pg], 2)
    out["wtm"] = c(tm.reshape(L, KT_D, 128, NCH, CW).transpose(0, 3, 2, 1, 4))
    out["wu"] = c(pu.reshape(L, KT_D, 128, 256).transpose(0, 2, 1, 3))
    g = pm.reshape(L, KT_D, 128, 3, KT_D, 128).transpose(0, 4, 2, 1, 3, 5).reshape(L, KT_D, 128, 3072)
    heads = a["w_branch_nsa"].reshape(L, NKV, GQA, HD, D).transpose(0, 2, 1, 3, 4).reshape(L, 4, 128, D)
    br = np.concatenate([a["w_branch_pool"].reshape(L, 2, 128, D), a["w_branch_gmlp"].reshape(L, 2, 128, D), heads], 1)
    br = br.reshape(L, 8, 128, KT_D, 128).transpose(0, 3, 2, 1, 4).reshape(L, KT_D, 128, 1024)
    out["wm"] = c(np.concatenate([g, br], 3))
    out["wo"] = c(a["w_out"].reshape(L, KT_D, 128, D).transpose(0, 2, 1, 3))
    gu = np.concatenate([a["w_gate"], a["w_up"]], 3).reshape(L, E, KT_D, 128, 512).transpose(0, 1, 3, 2, 4)
    dn = a["w_down"].reshape(L, E, 2, 128, D).transpose(0, 1, 3, 2, 4)
    out["we"] = c(np.concatenate([gu.reshape(L, E, 128, 4096), dn.reshape(L, E, 128, 2048)], 3))
    out["w1"] = c(a["cmp_w1"].reshape(L, 2, CL, HD, HID).transpose(0, 3, 1, 2, 4))
    out["peT"] = c(a["cmp_pe"].transpose(0, 3, 1, 2))
    out["ln"] = c(np.stack([a["ln1_g"], a["ln1_b"], a["ln2_g"], a["ln2_b"]], 1))
    kv = a["cache_cmp_kv"].transpose(0, 1, 4, 5, 3, 2)
    out["cmp_pages"] = c(kv.reshape(L, N_POOL, 128, 2, PAGE))

    def keys_and_values(rows):
        lead = rows.shape[:-4]
        kt = np.moveaxis(rows[..., 0, :, :], -3, -1).reshape(*lead, 128, 128)
        return np.concatenate([kt, rows[..., 1, :, :].reshape(*lead, 128, 128)], -1)
    out["sel_pages"] = c(keys_and_values(a["cache_sel_kv"]))
    win = a["state_win_kv"]
    out["win_rows"] = c(keys_and_values(win.reshape(L, B, 2, 128, 2, NKV, HD)).transpose(0, 3, 1, 2, 4))
    out["state_win"] = win.reshape(L, B, PAST, 256)
    out["state_pool"] = a["state_pool"]
    out["state_pool2"] = a["state_pool"].reshape(L, B * KEEP, 256)
    s = np.zeros((L, 128, NSMALL), np.float32)

    def put(name, v):
        lo, hi = _S[name]
        s[:, :v.shape[1], lo:hi] = v.reshape(L, v.shape[1], hi - lo)
    put("w2", a["cmp_w2"].transpose(0, 2, 1, 3))
    pw = np.zeros((L, 2, 2, 64, 2, 64), np.float32)
    for h in range(2):
        pw[:, :, h, :, h, :] = a["pool_w"].reshape(L, 2, 2, 64, 64)[:, :, h]
    put("poolw", pw.reshape(L, 2, 128, 128).transpose(0, 2, 1, 3))
    put("wsT", a["gmlp_ws"].transpose(0, 3, 1, 2))
    put("bsT", np.repeat(a["gmlp_bs"], 64, 1).reshape(L, 2, 128, 128).transpose(0, 2, 1, 3))
    put("pscale", a["pool_scale"].reshape(L, 2, 128).transpose(0, 2, 1))
    put("b1", a["cmp_b1"].transpose(0, 2, 1))
    put("wss", np.tile(a["gmlp_ws"][:, :, :TS, :TS].transpose(0, 3, 1, 2), (1, B, 1, 1)))
    put("vg", np.broadcast_to(a["gmlp_ln_g"][:, None], (L, 128, 256)))
    put("vb", np.broadcast_to(a["gmlp_ln_b"][:, None], (L, 128, 256)))
    out["small"] = s
    return out


_OUTS = [("y_p", (SEQ, D)), ("y_s", (NS, D)),
         ("o_cmp_p", (L, SEQ, 256)), ("o_sel_p", (L, SEQ, 256)), ("o_win_p", (L, SEQ, 256)), ("o_pool_p", (L, KEEP, 256)),
         ("o_cmp_s", (L, NS, 256)), ("o_sel_s", (L, NS, 256)), ("o_win_s", (L, B, PAST, 256)),
         ("o_pool_s", (L, B, KEEP, 256)), ("o_gmlp_s", (L, NS, 256))]


def kernel(**inputs):
    import concourse.bacc as _bacc
    from concourse.bass_utils import run_bass_kernel_spmd as _run

    arrays = layouts(inputs)
    nc = _bacc.Bacc("TRN2", target_bir_lowering=False, num_devices=1)
    io = {n: nc.dram_tensor("in_" + n, v.shape, mybir.dt.from_np(v.dtype), kind="ExternalInput").ap() for n, v in arrays.items()}
    for n, shape in _OUTS:
        io[n] = nc.dram_tensor("out_" + n, shape, F32, kind="ExternalOutput").ap()
    io["x1"] = nc.dram_tensor("x1_rows", (TOK, D), F32).ap()
    io["ys"] = nc.dram_tensor("expert_rows", (SLOTS, D), F32).ap()
    io["slot_token"] = nc.dram_tensor("slot_token", (SLOTS, 1), I32).ap()
    build(nc, io)
    r = _run(nc, [{"in_" + n: v for n, v in arrays.items()}], core_ids=[0]).results[0]
    r = {n: r["out_" + n] for n, _ in _OUTS}
    kv = (2, NKV, HD)
    return (r["y_p"].reshape(1, SEQ, D), r["y_s"].reshape(B, TS, D),
            r["o_cmp_p"].reshape(L, 1, SEQ, *kv), r["o_sel_p"].reshape(L, 1, SEQ, *kv), r["o_win_p"].reshape(L, 1, SEQ, *kv),
            r["o_pool_p"].reshape(L, 1, KEEP, 256),
            r["o_cmp_s"].reshape(L, B, TS, *kv), r["o_sel_s"].reshape(L, B, TS, *kv), r["o_win_s"].reshape(L, B, PAST, *kv),
            r["o_pool_s"], r["o_gmlp_s"].reshape(L, B, TS, 256))
```

```python
from contextlib import ExitStack

import numpy as np
import concourse.bass as bass
from concourse import mybir

F32 = mybir.dt.float32
F32R = mybir.dt.float32r
I32 = mybir.dt.int32
ALU = mybir.AluOpType
ACT = mybir.ActivationFunctionType
AX = mybir.AxisListType

D, SEQ, L = 1024, 512, 2
B, TS, PAST, PAGE = 8, 8, 256, 128
NS = B * TS
TOK = SEQ + NS
KT_D = D // 128
NT = SEQ // 128
TILES = [128] * NT + [NS]
NTT = len(TILES)
WIN = (2, 4, 8, 16)
KEEP = 15
HD, NH, NKV, GQA = 64, 8, 2, 4
CL, CS = 32, 16
HID = 128
E, EG, FE = 16, 4, 256
N_POOL = B * (PAST // PAGE) * 5 // 4
ALPHA = (2 * L) ** 0.25
EPS = 1e-5
NEG = -1e30

Q0, KV0, A0, V0, G0, TM = 0, 512, 1280, 1536, 1792, 1816
NCH = 4
CW = TM // NCH

XC = SEQ + B * PAST + CL
NG = XC // CS
NB = NG - 2
UW = NG

MAXCH = 24
SLOTS = MAXCH * 128

_C = {}
_at = 0
for _n, _w in [("ident", 128), ("diag", 128), ("cos", NTT * 8), ("sin", NTT * 8), ("cm", NT * 32), ("cneg", NT * 32),
               ("newneg", 2 * 64), ("scneg", 2 * 128), ("bcur0", 4 * 128), ("bcur", 4 * 128), ("bprev", 4 * 128),
               ("bst", 4 * 64), ("bnew", 4 * 64), ("tri", 128), ("ones", 128), ("e16", 16), ("g4", 4), ("th", 5),
               ("chunk", 32), ("gm", 128), ("gms", 64), ("blk", 4), ("rowhead", 4), ("mhalf", NTT), ("gsel", 256)]:
    _C[_n] = (_at, _at + _w)
    _at += _w
NCONST = _at

_S = {}
_at = 0
for _n, _w in [("w2", 128), ("poolw", 256), ("wsT", 512), ("bsT", 256), ("pscale", 2), ("b1", 2), ("wss", 32),
               ("vg", 256), ("vb", 256)]:
    _S[_n] = (_at, _at + _w)
    _at += _w
NSMALL = _at


def constants():
    c = np.zeros((128, NCONST), np.float32)

    def put(name, a):
        lo, hi = _C[name]
        a = np.asarray(a, np.float32)
        c[:a.shape[0], lo:hi] = a.reshape(a.shape[0], hi - lo)

    r = np.arange(128)
    put("ident", np.eye(128))
    put("diag", np.where(r[None, :] <= r[:, None], 0.0, NEG))
    pos = np.zeros((NTT, 128), np.float32)
    for i in range(NT):
        pos[i] = i * 128 + r
    pos[NT, :NS] = PAST + r[:NS] % TS
    inv = (1.0 / (np.float32(500000.0) ** (np.arange(8, dtype=np.float32) / np.float32(8)))).astype(np.float32)
    ang = pos[:, :, None] * inv
    put("cos", np.cos(ang).transpose(1, 0, 2))
    put("sin", np.sin(ang).transpose(1, 0, 2))
    c32 = np.arange(32)
    ok = (c32[None, None] < 31) & (c32[None, None] * CS + CL - 1 <= (np.arange(NT)[None, :, None] * 128 + r[:, None, None]))
    put("cm", ok)
    put("cneg", np.where(ok, 0.0, NEG))
    row_b, row_t = r // 32, r % 8
    kb, kt = np.arange(64) // 8, np.arange(64) % 8
    put("newneg", np.stack([np.where((kb[None] == 4 * g + row_b[:, None]) & (kt[None] <= row_t[:, None]), 0.0, NEG)
                            for g in range(2)], 1))
    mb, mc = r // 16, r % 16
    put("scneg", np.stack([np.where((mb[None] == 4 * g + row_b[:, None]) & (mc[None] < 15), 0.0, NEG)
                           for g in range(2)], 1))
    s, t = r[:, None], r[None, :]
    b0, bc, bp, bst, bnew = [], [], [], [], []
    for w in WIN:
        inside = (s <= t) & (s > t - w)
        b0.append(inside / np.minimum(w, t + 1.0) - (s == t))
        bc.append(inside / float(w) - (s == t))
        bp.append((s - 128 > t - w) / float(w))
        sb, sr = np.arange(B * KEEP) // KEEP, np.arange(B * KEEP) % KEEP - KEEP
        bst.append((sb[:, None] == kb[None]) & (sr[:, None] > kt[None] - w))
        bst[-1] = bst[-1] / float(w)
        same = kb[:, None] == kb[None]
        bnew.append((same & (kt[:, None] <= kt[None]) & (kt[:, None] > kt[None] - w)) / float(w) - np.eye(64))
    put("bcur0", np.stack(b0, 1))
    put("bcur", np.stack(bc, 1))
    put("bprev", np.stack(bp, 1))
    put("bst", np.stack(bst, 1))
    put("bnew", np.stack(bnew, 1))
    put("tri", s < t)
    put("ones", np.ones((128, 128)))
    put("e16", np.tile(16 - np.arange(16), (128, 1)))
    put("g4", np.tile(4 - np.arange(4), (128, 1)))
    put("th", np.tile(128 * np.arange(5), (128, 1)))
    put("chunk", np.tile(np.arange(32), (128, 1)))
    put("gm", s <= t)
    put("gms", (kb[:, None] == kb[None]) & (kt[:, None] <= kt[None]))
    put("blk", (r // 32)[:, None] == np.arange(4)[None])
    put("rowhead", (r % 32 // 8)[:, None] == np.arange(4)[None])
    put("mhalf", np.full((128, NTT), -0.5))
    gs = np.zeros((64, 2, 128))
    for g in range(2):
        for p in range(128):
            gs[(4 * g + p // 32) * 8 + p % 8, g, p] = 1
    put("gsel", gs)
    return c


class Steps:

    def __init__(self, eng, sem):
        self.eng, self.sem, self.n = eng, sem, 0

    def after(self, ins):
        self.n += 1
        ins.then_inc(self.sem, 1)
        self.eng.wait_ge(self.sem, self.n)


def two_types(nc, ctx, name, shape):
    with nc.sbuf_tensor(name + "_low", shape, F32R) as low:
        pass
    return ctx.enter_context(nc.sbuf_tensor(name, shape, F32)), low


class Ctx:
    pass


def build(nc, io):
    with ExitStack() as ctx:
        k = Ctx()
        k.nc, k.io = nc, io

        def sb(name, shape, dt=F32):
            return ctx.enter_context(nc.sbuf_tensor(name, shape, dt))

        k.sems = []

        def sem(name):
            s = ctx.enter_context(nc.semaphore(name))
            k.sems.append(s)
            return s
        k.sem = sem

        k.const = sb("const", [128, NCONST])
        k.c = {n: k.const[:, lo:hi] for n, (lo, hi) in _C.items()}
        k.x = sb("x", [128, NTT, D])
        k.xT, k.xT_low = two_types(nc, ctx, "xT", [128, KT_D, TOK])
        k.oT, k.oT_low = two_types(nc, ctx, "oT", [128, KT_D, TOK])
        k.pt = sb("page_ids", [1, B * PAST // PAGE], I32)
        k.tokid = sb("tokid", [128, NTT], I32)
        k.zero = sb("zero", [128, SLOTS // 128], I32)
        k.zrow = sb("zero_row", [128, 256])
        k.mk = sb("mask16", [128, 5 * 128], mybir.dt.bfloat16)
        k.wr = sb("w_router", [128, KT_D, E])
        k.br = sb("b_router", [128, E])
        k.ps = ctx.enter_context(nc.psum_tensor("ps", [128, 8, 512], F32))
        k.ident = k.c["ident"]

        first_in = sem("first_inputs_in")
        k.const_in, k.x_in = sem("constants_in"), sem("x_in")
        k.sems.clear()
        dve_s, act_s, pool_s = sem("dve_step"), sem("act_step"), sem("pool_step")
        k.dve, k.act, k.pool = Steps(nc.vector, dve_s), Steps(nc.scalar, act_s), Steps(nc.gpsimd, pool_s)
        prologue(k, first_in)
        nc.all_engine_barrier(sems_to_clear=range(pool_s.num, pool_s.num + 1))
        k.pool.n = 0
        with nc.Fori(0, L) as layer:
            k.layer = layer
            with ExitStack() as phase:
                def sp(name, shape, dt=F32):
                    return phase.enter_context(nc.sbuf_tensor(name, shape, dt))
                k.z = sp("z", [128, NTT, TM])
                k.uT = sp("uT", [128, 2, TOK])
                k.vn = sp("vn", [128, NTT, 256])
                k.qT = sp("qT", [128, GQA, SEQ])
                k.qsT = sp("qsT", [128, NKV, B, GQA, TS])
                k.KT = sp("KT", [128, 2, NKV, SEQ])
                k.KTs = sp("KT_sample", [128, 2, NS])
                k.kcT = sp("kcT", [128, NKV, 32])
                k.kcsT = sp("kcT_sample", [128, NB - 32])
                k.vblk = sp("vblk", [128, NKV, GQA, HD])
                k.vcs = sp("vcs", [128, NKV, HD])
                k.gates = sp("gates", [128, NTT, 24])
                k.gsr = sp("gates_by_row", [128, 2, NKV, 3])
                with ExitStack() as early:
                    def se(name, shape, dt=F32):
                        return early.enter_context(nc.sbuf_tensor(name, shape, dt))
                    k.XT = se("XT", [128, 2, XC])
                    k.small = se("small", [128, NSMALL])
                    k.s = {n: k.small[:, lo:hi] for n, (lo, hi) in _S.items()}
                    k.spool = se("pool_state", [128, 256])
                    project(k)
                    mixers(k)
                attention(k)
            merge(k)
            experts(k)
            nums = [s.num for s in k.sems]
            assert sorted(nums) == list(range(min(nums), max(nums) + 1))
            nc.gpsimd.dma_reset(range(min(nums), max(nums) + 1))
            nc.all_engine_barrier(sems_to_clear=range(min(nums), max(nums) + 1))


def prologue(k, first_in):
    nc, io = k.nc, k.io
    with nc.Block() as block:
        @block.sync
        def _(sp):
            sp.dma_start(k.pt[:, :], io["page_table"]).then_inc(first_in, 16)
            sp.dma_start(k.xT[:, :, :], io["x0T"]).then_inc(first_in, 16)
            sp.dma_start(k.tokid[:, :], io["tokid"]).then_inc(first_in, 16)
            sp.dma_start(k.wr[:, :, :], io["w_router"].rearrange("(k p) e -> p k e", p=128)).then_inc(first_in, 16)
            sp.dma_start(k.br[:, :], io["br"]).then_inc(first_in, 16)
            sp.dma_start(k.const[:, :], io["consts"]).then_inc(k.const_in, 16)
            sp.dma_start(k.x[:, 0:NT, :], io["xp"].rearrange("(i p) d -> p i d", p=128)).then_inc(k.x_in, 16)
            sp.dma_start(k.x[0:NS, NT, :], io["xs"]).then_inc(k.x_in, 16)
            sp.wait_ge(first_in, 16 * 5)

        @block.gpsimd
        def _(pool):
            k.pool.after(pool.memset(k.zero[:, :], 0))
            k.pool.after(pool.memset(k.zrow[:, :], 0.0))


def project(k):
    nc, io, l, ps = k.nc, k.io, k.layer, k.ps
    sem = k.sem
    RING, HRING = 4, 3
    w_in, small_in = [sem(f"z_w_in{n}") for n in range(RING)], sem("small_in")
    x_hi, x_lo, w_hi, w_lo = sem("z_x_high"), sem("z_x_low"), sem("z_w_high"), sem("z_w_low")
    k.pages_in = sem("cmp_pages_in")
    unit_done, z_done, z_out = sem("z_unit_done"), sem("z_done"), sem("z_out")
    z_cleared = sem("z_cleared")
    roped, t_done, t_out = sem("roped"), sem("t_done"), sem("t_out")
    stat_ready, rstd_ready, vn_ready, gate_tanh = (sem("vstat_ready"), sem("vrstd_ready"), sem("vn_ready"),
                                                   sem("gate_tanh"))
    k.stored = sem("stored")
    k.n_stored = 0
    with ExitStack() as ctx:
        w32, wl = two_types(nc, ctx, "z_w_ring", [128, RING, 2 * CW])
        wh = ctx.enter_context(nc.sbuf_tensor("z_w_high_part", [128, HRING, 2 * CW], F32R))
        xh = k.oT_low
        rt = ctx.enter_context(nc.sbuf_tensor("rope_tmp", [128, 4, NTT * 8 * 8], F32))
        st = ctx.enter_context(nc.sbuf_tensor("v_stats", [128, NTT, 6], F32))
        mv = ctx.enter_context(nc.sbuf_tensor("v_mv", [128, NTT, 2], F32))
        rs = ctx.enter_context(nc.sbuf_tensor("v_rstd", [128, NTT], F32))
        block = ctx.enter_context(nc.Block())
        CHUNKS = (0, 1, 2, "u", 3)
        BANKS = [4 if n == "u" else NTT for n in CHUNKS]
        FIRST = [sum(BANKS[:c]) for c in range(len(CHUNKS) + 1)]
        NRES = FIRST[-1]
        NU = 4 * len(CHUNKS)
        TH = TOK // 2
        width = [512 if CHUNKS[u // 4] == "u" else 2 * CW for u in range(NU)]

        def unit_ended(eng, u):
            if u % 4 == 3:
                eng.wait_ge(z_done, FIRST[u // 4 + 1])
            else:
                eng.wait_ge(unit_done, u // 4 * 3 + u % 4 + 1)

        @block.sync
        def _(sp):
            for u in range(NU):
                n, kk = CHUNKS[u // 4], 2 * (u % 4)
                if u >= RING:
                    unit_ended(sp, u - RING)
                src = io["wu"][l, :, kk:kk + 2, :] if n == "u" else io["wtm"][l, n, :, kk:kk + 2, :]
                sp.dma_start(w32[:, u % RING, 0:width[u]].rearrange("p (k n) -> p k n", k=2), src
                             ).then_inc(w_in[u % RING], 16)
                if u == RING:
                    for j in range(B * PAST // PAGE):
                        page = sp.value_load(k.pt[0:1, j:j + 1], min_val=0, max_val=N_POOL - 1)
                        sp.dma_start(k.XT[:, :, SEQ + j * PAGE:SEQ + (j + 1) * PAGE],
                                     io["cmp_pages"][l, page]).then_inc(k.pages_in, 16)
                if u == RING + 2:
                    for h in range(NKV):
                        sp.dma_start(k.XT[h * HD:(h + 1) * HD, :, XC - CL:XC], io["peT"][l]).then_inc(k.pages_in, 16)
                    sp.dma_start(k.small[:, :], io["small"][l]).then_inc(small_in, 16)
                    sp.dma_start(k.spool[0:B * KEEP, :], io["state_pool2"][l]).then_inc(small_in, 16)
            sp.dma_start(io["o_win_s"][l, :, 0:PAST - TS, :], io["state_win"][l, :, TS:PAST, :]).then_inc(k.stored, 16)
            sp.dma_start(io["o_pool_s"][l, :, 0:KEEP - TS, :], io["state_pool"][l, :, TS:KEEP, :]).then_inc(k.stored, 16)
            sp.wait_ge(roped, 2)
            for c, (op, os) in enumerate([("o_cmp_p", "o_cmp_s"), ("o_sel_p", "o_sel_s"), ("o_win_p", None)]):
                cols = slice(KV0 + 256 * c, KV0 + 256 * (c + 1))
                sp.dma_start(io[op][l].rearrange("(i p) c -> p i c", p=128), k.z[:, 0:NT, cols]).then_inc(k.stored, 16)
                if os:
                    sp.dma_start(io[os][l], k.z[0:NS, NT, cols]).then_inc(k.stored, 16)
                else:
                    for b in range(B):
                        sp.dma_start(io["o_win_s"][l, b, PAST - TS:PAST, :],
                                       k.z[b * TS:(b + 1) * TS, NT, cols]).then_inc(k.stored, 16)
            sp.wait_ge(z_out, NRES)
            sp.dma_start(io["o_pool_p"][l], k.z[128 - KEEP:128, NT - 1, A0:A0 + 256]).then_inc(k.stored, 16)
            for b in range(B):
                sp.dma_start(io["o_pool_s"][l, b, KEEP - TS:KEEP, :],
                               k.z[b * TS:(b + 1) * TS, NT, A0:A0 + 256]).then_inc(k.stored, 16)
            sp.wait_ge(vn_ready, 1)
            sp.dma_start(io["o_gmlp_s"][l], k.vn[0:NS, NT, :]).then_inc(k.stored, 16)

        @block.gpsimd
        def _(pool):
            pool.memset(k.z[64:128, NT, :], 0.0).then_inc(z_cleared, 1)
            pool.wait_ge(z_cleared, 1)
            for h in range(NKV):
                other = slice((1 - h) * HD, (2 - h) * HD)
                k.pool.after(pool.memset(k.KT[other, :, h, :], 0.0))
                k.pool.after(pool.memset(k.kcT[other, h, :], 0.0))
                k.pool.after(pool.memset(k.qsT[other, h, :, :, :], 0.0))
            pool.wait_ge(k.const_in, 16)
            pool.wait_ge(stat_ready, 1)
            k.pool.after(pool.tensor_scalar(rs[:, :], mv[:, :, 1], EPS, None, ALU.add))
            k.pool.after(pool.tensor_tensor(rs[:, :], rs[:, :], k.c["mhalf"], ALU.pow))
            pool.sem_inc(rstd_ready, 1)
            unit_ended(pool, NU - 1)
            k.pool.after(pool.tensor_tensor(k.xT[:, :, :], k.xT_low[:, :, :].bitcast(F32), xh[:, :, :].bitcast(F32), ALU.add))
        k.n_stored = 2 + 5 + B + 1 + B + 1

        @block.tensor
        def _(pe):
            def product(out, w, x, first, last):
                pe.matmul(out, w[0], x[0], start=first, stop=False)
                pe.matmul(out, w[0], x[1], start=False, stop=False)
                return pe.matmul(out, w[1], x[0], start=False, stop=last)

            for u in range(NU):
                chunk, q = u // 4, u % 4
                pe.wait_ge(w_lo, u + 1)
                if chunk == 0:
                    pe.wait_ge(x_lo, q + 1)
                for r in range(BANKS[chunk]):
                    res = FIRST[chunk] + r
                    if q == 0 and res >= 8:
                        pe.wait_ge(z_out, res - 7)
                    for a in range(2):
                        kk = 2 * q + a

                        def x(cols):
                            return xh[:, kk, cols], k.xT_low[:, kk, cols]

                        def w(cols):
                            return wh[:, u % HRING, cols], wl[:, u % RING, cols]
                        if CHUNKS[chunk] == "u":
                            m, half = r // 2, r % 2
                            at = a * 256 + m * 128
                            last = product(ps[:, res % 8, 0:TH], w(slice(at, at + 128)), x(slice(half * TH, (half + 1) * TH)),
                                           kk == 0, kk == KT_D - 1)
                        else:
                            rows = TILES[r]
                            last = product(ps[0:rows, res % 8, 0:CW], x(slice(r * 128, r * 128 + rows)),
                                           w(slice(a * CW, (a + 1) * CW)), kk == 0, kk == KT_D - 1)
                    if q == 3:
                        last.then_inc(z_done, 1)
                if q < 3:
                    last.then_inc(unit_done, 1)
            pe.wait_ge(k.const_in, 16)
            pe.wait_ge(z_out, NRES)
            pe.wait_ge(roped, 1)
            for u in range(4 + 4):
                if u == 4:
                    pe.wait_ge(roped, 2)
                for i in range(NT):
                    if u < 4:
                        src = k.z[:, i, Q0 + u * 128:Q0 + (u + 1) * 128]
                    else:
                        col = KV0 + (256, 512, 0, 128)[u - 4]
                        src = k.z[:, i, col:col + 128]
                    last = pe.transpose(ps[:, u, i * 128:(i + 1) * 128], src, k.ident)
                last.then_inc(t_done, 1)
            pe.wait_ge(t_out, 2)
            for u in range(4):
                src = k.z[0:NS, NT, Q0 + u * 128:Q0 + (u + 1) * 128]
                last = pe.transpose(ps[:, 0, u * NS:(u + 1) * NS], src, k.ident[0:NS, 0:NS])
            last.then_inc(t_done, 1)
            for u in range(2):
                col = KV0 + 256 * (u + 1)
                last = pe.transpose(ps[:, 1, u * NS:(u + 1) * NS], k.z[0:NS, NT, col:col + 128], k.ident[0:NS, 0:NS])
            last.then_inc(t_done, 1)

        @block.scalar
        def _(act):
            act.wait_ge(z_cleared, 1)

            def x_high(q):
                act.copy(xh[:, 2 * q:2 * q + 2, :], k.xT[:, 2 * q:2 * q + 2, :]).then_inc(x_hi, 1)

            def w_high(u):
                act.wait_ge(w_in[u % RING], 16 * (u // RING + 1))
                if u >= HRING:
                    unit_ended(act, u - HRING)
                act.copy(wh[:, u % HRING, 0:width[u]], w32[:, u % RING, 0:width[u]]).then_inc(w_hi, 1)

            def results(chunk):
                for r in range(BANKS[chunk]):
                    res, n = FIRST[chunk] + r, CHUNKS[chunk]
                    act.wait_ge(z_done, res + 1)
                    if n == "u":
                        dst, rows, cols = k.uT[:, r // 2, r % 2 * TH:(r % 2 + 1) * TH], 128, TH
                    else:
                        dst, rows, cols = k.z[0:TILES[r], r, n * CW:(n + 1) * CW], TILES[r], CW
                    act.copy(dst, ps[0:rows, res % 8, 0:cols]).then_inc(z_out, 1)
            x_high(0)
            w_high(0)
            x_high(1)
            w_high(1)
            x_high(2)
            x_high(3)
            for u in range(NU):
                if u + 2 < NU:
                    w_high(u + 2)
                if u % 4 == 3:
                    results(u // 4)
            act.wait_ge(z_out, NRES)
            act.activation(k.gates[:, :, :], k.z[:, :, G0:G0 + 24], ACT.Tanh, scale=0.5).then_inc(gate_tanh, 1)
            for u in range(8):
                act.wait_ge(t_done, u + 1)
                if u < 4:
                    act.activation(k.qT[:, u, :], ps[:, u, :], ACT.Copy, scale=HD ** -0.5).then_inc(t_out, 1)
                elif u < 6:
                    for h in range(NKV):
                        hs = slice(h * HD, (h + 1) * HD)
                        last = act.copy(k.KT[hs, u - 4, h, :], ps[hs, u, :])
                    last.then_inc(t_out, 1)
                else:
                    act.copy(k.XT[:, u - 6, 0:SEQ], ps[:, u, :]).then_inc(t_out, 1)
            act.wait_ge(t_done, 9)
            for h in range(NKV):
                hs = slice(h * HD, (h + 1) * HD)
                for i in range(GQA):
                    act.activation(k.qsT[hs, h, :, i, :], ps[hs, 0, i * NS:(i + 1) * NS].rearrange("p (b t) -> p b t", b=B),
                                   ACT.Copy, scale=HD ** -0.5)
            act.wait_ge(t_done, 10)
            act.copy(k.KTs[:, :, :], ps[:, 1, 0:2 * NS].rearrange("p (u t) -> p u t", u=2))

        @block.vector
        def _(dve):
            def rope(base, n, step):
                def half(o):
                    return k.z[:, :, base:base + n * HD].rearrange("p i (h d) -> p i h d", d=HD)[:, :, :, o:o + 8]
                cos = k.c["cos"].rearrange("p (i d) -> p i d", i=NTT).unsqueeze(2).broadcast_to([128, NTT, n, 8])
                sin = k.c["sin"].rearrange("p (i d) -> p i d", i=NTT).unsqueeze(2).broadcast_to([128, NTT, n, 8])
                t = [rt[:, a, 0:NTT * n * 8].rearrange("p (i h d) -> p i h d", i=NTT, h=n) for a in range(4)]
                dve.tensor_tensor(t[0], half(0), cos, ALU.mult)
                dve.tensor_tensor(t[1], half(8), sin, ALU.mult)
                dve.tensor_tensor(t[2], half(8), cos, ALU.mult)
                k.dve.after(dve.tensor_tensor(t[3], half(0), sin, ALU.mult))
                dve.tensor_tensor(half(0), t[0], t[1], ALU.subtract)
                return dve.tensor_tensor(half(8), t[2], t[3], ALU.add)

            def rest(low, src, high):
                return dve.tensor_tensor(low, src, high.bitcast(F32), ALU.subtract)

            def x_low(q):
                ks = slice(2 * q, 2 * q + 2)
                dve.wait_ge(x_hi, q + 1)
                rest(k.xT_low[:, ks, :], k.xT[:, ks, :], xh[:, ks, :]).then_inc(x_lo, 1)

            def w_low(u):
                dve.wait_ge(w_hi, u + 1)
                rest(wl[:, u % RING, 0:width[u]], w32[:, u % RING, 0:width[u]],
                     wh[:, u % HRING, 0:width[u]]).then_inc(w_lo, 1)
            x_low(0)
            w_low(0)
            x_low(1)
            w_low(1)
            x_low(2)
            x_low(3)
            for u in range(2, NU):
                w_low(u)
                if u == 10:
                    dve.wait_ge(k.const_in, 16)
                    dve.wait_ge(z_out, FIRST[2])
                    rope(Q0, NH, HD).then_inc(roped, 1)
                    dve.wait_ge(roped, 1)
                if u == 14:
                    dve.wait_ge(z_out, FIRST[3])
                    for c in range(3):
                        last = rope(KV0 + 256 * c, NKV, HD)
                        if c < 2:
                            k.dve.after(last)
                    last.then_inc(roped, 1)
            dve.wait_ge(z_out, NRES)
            for i in range(NTT):
                last = dve.bn_stats(st[:, i, :], k.z[:, i, V0:V0 + 256])
            k.dve.after(last)
            for i in range(NTT):
                last = dve.bn_aggr(mv[:, i, :], st[:, i, :])
            last.then_inc(stat_ready, 1)
            dve.wait_ge(rstd_ready, 1)
            for i in range(NTT):
                last = dve.tensor_scalar(k.vn[:, i, :], k.z[:, i, V0:V0 + 256], mv[:, i, 0:1], rs[:, i:i + 1],
                                         ALU.subtract, ALU.mult)
            k.dve.after(last)
            dve.wait_ge(small_in, 32)
            k.dve.after(dve.tensor_tensor(k.vn[:, :, :], k.vn[:, :, :],
                                          k.s["vg"].unsqueeze(1).broadcast_to([128, NTT, 256]), ALU.mult))
            dve.tensor_tensor(k.vn[:, :, :], k.vn[:, :, :],
                              k.s["vb"].unsqueeze(1).broadcast_to([128, NTT, 256]), ALU.add).then_inc(vn_ready, 1)
            dve.wait_ge(gate_tanh, 1)
            dve.tensor_scalar(k.gates[:, :, :], k.gates[:, :, :], 0.5, 0.5, ALU.mult, ALU.add)


def mixers(k):
    nc, io, l, ps, c = k.nc, k.io, k.layer, k.ps, k.c
    sem = k.sem
    w1_in, masked = sem("w1_in"), sem("gmlp_masked")
    d_done, d_out, mix_done, mix_out, y_done = (sem("pool_d_done"), sem("pool_d_out"), sem("mix_done"),
                                                sem("mix_out"), sem("pool_y_done"))
    u_done, u1_out, x_ready, th_ready, hid_ready = (sem("cmp_u_done"), sem("cmp_u1_out"), sem("cmp_x_ready"),
                                                    sem("cmp_tanh_ready"), sem("cmp_hid_ready"))
    gr_done, kc_done = sem("gate_rows_done"), sem("kc_done")
    with ExitStack() as ctx:
        def sb(name, shape):
            return ctx.enter_context(nc.sbuf_tensor(name, shape, F32))
        w1 = sb("w1", [128, 2, CL, HID])
        dT = k.oT[:, 0:2, :]
        wmT = sb("wmT", [128, 4, 128])
        wmsT = sb("wmsT", [128, 4, NS])
        u1 = sb("u1", [128, 4, UW])
        bias = sb("cmp_bias", [128, 4])
        spare = k.oT[:, 4:8, :].rearrange("p a t -> p (a t)")
        xh, th, hid = (spare[:, n * 4 * NB:(n + 1) * 4 * NB].rearrange("p (n m) -> p n m", n=4) for n in range(3))
        hrep = sb("hrep", [128, NKV, 4, 32])
        gt = sb("gate_tmp", [128, 2, NKV, 3, 4])
        block = ctx.enter_context(nc.Block())
        BANK = [[0, 1], [3, 4]]

        @block.sync
        def _(sp):
            for h in range(NKV):
                sp.dma_start(w1[h * HD:(h + 1) * HD, :, :, :], io["w1"][l]).then_inc(w1_in, 16)

        @block.tensor
        def _(pe):
            for g in range(4):
                p, half = g // 2, slice(64 * (g % 2), 64 * (g % 2) + 64)
                col = slice(A0 + 64 * g, A0 + 64 * g + 64)
                for i in range(NT):
                    out = ps[half, p, i * 128:(i + 1) * 128]
                    cur = c["bcur0" if i == 0 else "bcur"][:, g * 128:(g + 1) * 128]
                    pe.matmul(out, k.z[:, i, col], cur, start=True, stop=(i == 0))
                    if i:
                        pe.matmul(out, k.z[:, i - 1, col], c["bprev"][:, g * 128:(g + 1) * 128], start=False, stop=True)
                out = ps[half, 2, p * 64:p * 64 + 64]
                pe.matmul(out, k.spool[0:B * KEEP, 64 * g:64 * g + 64], c["bst"][0:B * KEEP, g * 64:g * 64 + 64],
                          start=True, stop=False)
                last = pe.matmul(out, k.z[0:NS, NT, col], c["bnew"][0:NS, g * 64:g * 64 + 64], start=False, stop=True)
            last.then_inc(d_done, 1)
            pe.wait_ge(masked, 1)
            for g in range(4):
                p, half = g // 2, slice(64 * (g % 2), 64 * (g % 2) + 64)
                for i in range(NT):
                    pe.matmul(ps[half, 3 + p, i * 128:(i + 1) * 128], k.vn[:, i, 64 * g:64 * g + 64], wmT[:, g, :],
                              start=True, stop=True)
                last = pe.matmul(ps[half, 5, p * 64:p * 64 + 64], k.vn[0:NS, NT, 64 * g:64 * g + 64],
                                 wmsT[0:NS, g, :], start=True, stop=True)
            last.then_inc(mix_done, 1)
            pe.wait_ge(d_out, 1)
            for p in range(2):
                w = k.s["poolw"][:, p * 128:(p + 1) * 128]
                pe.matmul(ps[:, 6 + p, :], w, dT[:, p, 0:SEQ], start=True, stop=True)
                last = pe.matmul(ps[:, 2, 128 + p * 64:192 + p * 64], w, dT[:, p, SEQ:TOK], start=True, stop=True)
            last.then_inc(y_done, 1)
            pe.wait_ge(mix_out, 1)
            for g in range(2):
                last = pe.matmul(ps[:, 5, 256 + 24 * g:280 + 24 * g], c["gsel"][0:NS, g * 128:(g + 1) * 128],
                                 k.gates[0:NS, NT, :], start=True, stop=True)
            last.then_inc(gr_done, 1)
            pe.wait_ge(w1_in, 32)
            pe.wait_ge(k.pages_in, 16 * (B * PAST // PAGE + NKV))
            for kv in range(2):
                for a in range(2):
                    for r in range(CS):
                        for h in range(NKV):
                            hs = slice(h * HD, (h + 1) * HD)
                            last = pe.matmul(ps[:, BANK[h][kv], a * UW:(a + 1) * UW], w1[hs, kv, a * CS + r, :],
                                             k.XT[hs, kv, r:XC:CS], start=(r == 0), stop=(r == CS - 1))
                last.then_inc(u_done, 1)
            pe.wait_ge(hid_ready, 1)
            for h in range(NKV):
                pe.matmul(ps[h * HD:(h + 1) * HD, 5, 0:NB], k.s["w2"][:, 0:64], hid[:, h, :], start=True, stop=True)
            pe.wait_ge(hid_ready, 2)
            for h in range(NKV):
                pe.matmul(ps[:, 7, h * HD:(h + 1) * HD], hrep[:, h, :, :].rearrange("p i c -> p (i c)"),
                          k.s["w2"][:, 64:128], start=True, stop=True)
                last = pe.matmul(ps[:, 7, 128 + h * HD:192 + h * HD], hid[:, 2 + h, 32:NB], k.s["w2"][:, 64:128],
                                 start=True, stop=True)
            last.then_inc(kc_done, 1)

        @block.scalar
        def _(act):
            for n in range(4):
                kv, h = n // 2, n % 2
                act.wait_ge(u_done, kv + 1)
                act.copy(u1[:, n, :], ps[:, BANK[h][kv], UW:2 * UW]).then_inc(u1_out, 1)
            act.wait_ge(x_ready, 1)
            act.activation(th[:, :, :], hid[:, :, :], ACT.Tanh, scale=0.7978845608028654).then_inc(th_ready, 1)
            act.wait_ge(kc_done, 1)
            for h in range(NKV):
                hs = slice(h * HD, (h + 1) * HD)
                act.activation(k.kcT[hs, h, :], ps[hs, 5, 0:32], ACT.Copy, scale=0.5)
            act.activation(k.kcsT[:, :], ps[:, 5, 32:NB], ACT.Copy, scale=0.5)

        @block.vector
        def _(dve):
            step = k.dve.after
            s = k.s
            dve.tensor_tensor(wmT[:, :, :], s["wsT"].rearrange("p (g t) -> p g t", g=4),
                              c["gm"].unsqueeze(1).broadcast_to([128, 4, 128]), ALU.mult)
            dve.tensor_tensor(wmsT[0:NS, :, :].rearrange("p g (b t) -> p g b t", b=B),
                              s["wss"][0:NS].rearrange("p (g t) -> p g t", g=4).unsqueeze(2).broadcast_to([NS, 4, B, TS]),
                              c["gms"][0:NS].rearrange("p (b t) -> p b t", b=B).unsqueeze(1).broadcast_to([NS, 4, B, TS]),
                              ALU.mult).then_inc(masked, 1)
            dve.tensor_copy(k.mk[:, 0:128], k.ident)
            dve.tensor_copy(k.mk[:, 128:256], c["diag"])
            dve.tensor_copy(k.mk[:, 256:512], c["scneg"])
            dve.tensor_copy(k.mk[:, 512:640], c["newneg"])
            dve.wait_ge(d_done, 1)
            dve.tensor_copy(dT[:, :, 0:SEQ], ps[:, 0:2, :])
            dve.tensor_copy(dT[:, :, SEQ:TOK], ps[:, 2, 0:128].rearrange("p (a t) -> p a t", a=2)).then_inc(d_out, 1)
            dve.wait_ge(mix_done, 1)
            bs = s["bsT"].rearrange("p (a t) -> p a t", a=2)
            for p in range(2):
                dve.tensor_tensor(k.oT[:, 2 + p, 0:SEQ].rearrange("p (i t) -> p i t", i=NT),
                                  ps[:, 3 + p, :].rearrange("p (i t) -> p i t", i=NT),
                                  bs[:, p, :].unsqueeze(1).broadcast_to([128, NT, 128]), ALU.add)
            for p in range(2):
                last = dve.tensor_tensor(k.oT[:, 2 + p, SEQ:TOK].rearrange("p (b t) -> p b t", b=B),
                                         ps[:, 5, 64 * p:64 * p + 64].rearrange("p (b t) -> p b t", b=B),
                                         bs[:, p, 0:TS].unsqueeze(1).broadcast_to([128, B, TS]), ALU.add)
            last.then_inc(mix_out, 1)
            dve.wait_ge(mix_out, 1)
            dve.tensor_tensor(k.oT[:, 2:4, :], k.oT[:, 2:4, :], k.uT[:, :, :], ALU.mult)
            dve.wait_ge(y_done, 1)
            for p in range(2):
                sc = s["pscale"][:, p:p + 1]
                dve.tensor_scalar(k.oT[:, p, 0:SEQ], ps[:, 6 + p, :], sc, None, ALU.mult)
                dve.tensor_scalar(k.oT[:, p, SEQ:TOK], ps[:, 2, 128 + 64 * p:192 + 64 * p], sc, None, ALU.mult)
            dve.wait_ge(gr_done, 1)
            for g in range(2):
                for h in range(NKV):
                    dve.tensor_tensor(gt[:, g, h, :, :],
                                      ps[:, 5, 256 + 24 * g + 12 * h:268 + 24 * g + 12 * h].rearrange("p (i c) -> p c i", i=4),
                                      c["rowhead"].unsqueeze(1).broadcast_to([128, 3, 4]), ALU.mult)
            step(dve.memset(bias[:, :], 0.0))
            dve.tensor_reduce(k.gsr[:, :, :, :].rearrange("p g h c -> p (g h c)"),
                              gt[:, :, :, :, :].rearrange("p g h c i -> p (g h c) i"), AX.X, ALU.add)

            for n in range(4):
                kv, h = n // 2, n % 2
                dve.wait_ge(u1_out, n + 1)
                U = ps[:, BANK[h][kv], :]
                step(dve.scalar_tensor_tensor(bias[:, n:n + 1], U[:, NB:NB + 1], s["b1"][:, kv:kv + 1],
                                              u1[:, n, NB + 1:NB + 2], ALU.add, ALU.add))
                last = dve.scalar_tensor_tensor(xh[:, n, :], U[:, 0:NB], bias[:, n:n + 1], u1[:, n, 1:NB + 1],
                                                ALU.add, ALU.add)
            step(last)
            step(dve.tensor_tensor(th[:, :, :], xh[:, :, :], xh[:, :, :], ALU.mult))
            step(dve.tensor_scalar(th[:, :, :], th[:, :, :], 0.044715, 1.0, ALU.mult, ALU.add))
            dve.tensor_tensor(hid[:, :, :], th[:, :, :], xh[:, :, :], ALU.mult).then_inc(x_ready, 1)
            dve.wait_ge(th_ready, 1)
            dve.scalar_tensor_tensor(hid[:, :, :], th[:, :, :], 1.0, xh[:, :, :], ALU.add, ALU.mult).then_inc(hid_ready, 1)
            dve.wait_ge(hid_ready, 1)
            dve.tensor_copy(hrep[:, :, :, :], hid[:, 2:4, 0:32].unsqueeze(2).broadcast_to([128, NKV, 4, 32])).then_inc(hid_ready, 1)
            dve.wait_ge(kc_done, 1)
            dve.tensor_scalar(k.vcs[:, :, :], ps[:, 7, 128:256].rearrange("p (h d) -> p h d", h=2), 0.5, None, ALU.mult)
            for h in range(NKV):
                dve.scalar_tensor_tensor(k.vblk[:, h, :, :],
                                         ps[:, 7, h * HD:(h + 1) * HD].unsqueeze(1).broadcast_to([128, 4, HD]), 0.5,
                                         c["blk"].unsqueeze(2).broadcast_to([128, 4, HD]), ALU.mult, ALU.mult)


def attention(k):
    nc, io, l, ps, c = k.nc, k.io, k.layer, k.ps, k.c
    sem = k.sem
    LAG_T, LAG_V = 2, 3
    units = []
    for t in range(NT):
        units.append(("cmp", t, 0, 0, 0))
        units += [("kv", t, kvh, i, br) for kvh in range(NKV) for i in range(GQA) for br in range(2)]
    for g in range(2):
        for kvh in range(NKV):
            units.append(("scmp", g, kvh, 0, 0))
            units += [("skv", g, kvh, 0, br) for br in range(2)]
    NU = len(units)
    group = [u[1] + (NT if u[0][0] == "s" else 0) for u in units]
    last_of = [max(n for n in range(NU) if group[n] == gr) for gr in range(NT + 2)]

    def on_act(n):
        return n % 2 == 1

    def copied(eng, n):
        if on_act(n):
            eng.wait_ge(pt_by_act, len([m for m in range(n + 1) if on_act(m)]))
        else:
            eng.wait_ge(pt_by_dve, len([m for m in range(n + 1) if not on_act(m)]))

    sel_in, win_in = sem("sel_pages_in"), sem("win_rows_in")
    k.rows_cleared = sem("expert_rows_cleared")
    s_done, masked, p_ready, pm_ready = sem("score_done"), sem("score_masked"), sem("prob_ready"), sem("cmp_prob_ready")
    pt_done, pt_by_act, pt_by_dve, av_done = sem("pt_done"), sem("pt_by_act"), sem("pt_by_dve"), sem("av_done")
    o_out, ot_done = sem("o_out"), sem("ot_done")
    with ExitStack() as ctx:
        def sb(name, shape):
            return ctx.enter_context(nc.sbuf_tensor(name, shape, F32))
        sel = sb("sel_pages", [128, B, 2, 256])
        win = sb("win_rows", [128, B, 2, 256])
        P = sb("probs", [128, 3, 512])
        PT = sb("probsT", [128, 2, 512])
        sc = sb("cmp_scores", [128, 256])
        mx = sb("row_max", [128, 3])
        mx8 = sb("cmp_max", [128, 8])
        den = sb("den", [128, 2, 3, 8])
        wgt = sb("wgt", [128, 3, 8])
        acc = sb("acc", [128, 3, 512])
        otm = sb("otm", [128, NT, 512])
        osm = sb("osm", [128, 2, 128])
        block = ctx.enter_context(nc.Block())
        past = (sel, win)

        def vcol(br, kvh):
            return slice(KV0 + 256 * (br + 1) + 128 + kvh * HD, KV0 + 256 * (br + 1) + 128 + (kvh + 1) * HD)

        @block.sync
        def _(sp):
            for j in range(B * PAST // PAGE):
                page = sp.value_load(k.pt[0:1, j:j + 1], min_val=0, max_val=N_POOL - 1)
                sp.dma_start(sel[:, j // 2, j % 2, :], io["sel_pages"][l, page]).then_inc(sel_in, 16)
            sp.dma_start(win[:, :, :, :], io["win_rows"][l]).then_inc(win_in, 16)
            with sp.Fori(0, l * (MAXCH // 2 - 1) + 1):
                sp.sem_inc(k.rows_cleared, 16)
            with sp.Fori(l * (MAXCH // 2 - 1), MAXCH // 2) as p:
                sp.dma_start(io["ys"][bass.ds(p * 256, 256), :].rearrange("(p c) (q e) -> p (c q) e", p=128, e=256),
                             k.zrow[:, :].unsqueeze(1).broadcast_to([128, 8, 256])).then_inc(k.rows_cleared, 16)

        @block.tensor
        def _(pe):
            def scores(n):
                kind, t, kvh, i, br = units[n]
                bank = n % 3
                if n >= 3:
                    pe.wait_ge(p_ready, n - 2)
                if kind != "cmp":
                    lo, hi, m = {"kv": (t * 128, (t + 1) * 128, 128), "scmp": (0, 128, 256 + 128 * t),
                                 "skv": (256, 320, 512 + 64 * t)}[kind]
                    pe.matmul(ps[:, bank, lo:hi], k.mk[:, 0:128], k.mk[:, m:m + hi - lo], start=True,
                              stop=False, skip_group_check=True)
                if kind == "cmp":
                    out = ps[:, bank, 0:256].rearrange("p (h i c) -> p i h c", h=NKV, i=GQA)
                    for i in range(GQA):
                        last = pe.matmul(out[:, i, :, :], k.qT[:, i, t * 128:(t + 1) * 128], k.kcT[:, :, :],
                                         start=True, stop=True)
                elif kind == "kv":
                    last = pe.matmul(ps[:, bank, 0:(t + 1) * 128], k.qT[:, i, t * 128:(t + 1) * 128],
                                     k.KT[:, br, kvh, 0:(t + 1) * 128], start=False, stop=True,
                                     skip_group_check=True)
                elif kind == "scmp":
                    q = k.qsT[:, kvh, 4 * t:4 * t + 4, :, :].rearrange("p b i t -> p (b i t)")
                    last = pe.matmul(ps[:, bank, 0:128], q, k.kcsT[:, :], start=False, stop=True,
                                     skip_group_check=True)
                else:
                    pe.wait_ge((sel_in, win_in)[br], 16 * (B * PAST // PAGE, 1)[br])
                    q = k.qsT[:, kvh, 4 * t:4 * t + 4, :, :].rearrange("p b i t -> p (b i t)")
                    pe.matmul(ps[:, bank, 256:320], q, k.KTs[:, br, :], start=False, stop=True,
                              skip_group_check=True)
                    for b in range(4):
                        q = k.qsT[:, kvh, 4 * t + b, :, :].rearrange("p i t -> p (i t)")
                        last = pe.matmul(ps[32 * b:32 * b + 32, bank, 0:256].rearrange("p (a t) -> p a t", a=2), q,
                                         past[br][:, 4 * t + b, :, 0:128], start=True, stop=True)
                last.then_inc(s_done, 1)

            def transposes(n):
                kind, t, kvh, i, br = units[n]
                bank = 3 + n % 2
                if kind == "cmp":
                    pe.wait_ge(pm_ready, t + 1)
                pe.wait_ge(p_ready, n + 1)
                if n >= 2:
                    copied(pe, n - 2)
                w = {"cmp": 2, "kv": t + 1, "scmp": 1, "skv": 2}[kind]
                for a in range(w):
                    last = pe.transpose(ps[:, bank, a * 128:(a + 1) * 128], P[:, n % 3, a * 128:(a + 1) * 128], k.ident)
                if kind == "skv":
                    last = pe.transpose(ps[0:64, bank, 256:384], P[:, n % 3, 256:320], k.ident)
                last.then_inc(pt_done, 1)

            def values(n):
                kind, t, kvh, i, br = units[n]
                copied(pe, n)
                if group[n] and (n == 0 or group[n] != group[n - 1]):
                    pe.wait_ge(o_out, group[n])
                pt = PT[:, n % 2, :]
                if kind == "cmp":
                    for h in range(NKV):
                        last = pe.matmul(ps[:, 5, h * 256:(h + 1) * 256], pt[:, h * 128:(h + 1) * 128],
                                         k.vblk[:, h, :, :].rearrange("p i d -> p (i d)"), start=True, stop=True)
                elif kind == "kv":
                    out = ps[:, 6 + br, (kvh * 4 + i) * HD:(kvh * 4 + i + 1) * HD]
                    for a in range(t + 1):
                        last = pe.matmul(out, pt[:, a * 128:(a + 1) * 128], k.z[:, a, vcol(br, kvh)],
                                         start=(a == 0), stop=(a == t))
                elif kind == "scmp":
                    last = pe.matmul(ps[:, 5, kvh * HD:(kvh + 1) * HD], pt[:, 0:128], k.vcs[:, kvh, :],
                                     start=True, stop=True)
                else:
                    pe.matmul(ps[:, 6 + br, kvh * HD:(kvh + 1) * HD], pt[0:NS, 256:384], k.z[0:NS, NT, vcol(br, kvh)],
                              start=True, stop=False, skip_group_check=True)
                    for b in range(4):
                        for a in range(2):
                            last = pe.matmul(ps[32 * b:32 * b + 32, 6 + br, kvh * HD:(kvh + 1) * HD],
                                             pt[:, a * 128 + 32 * b:a * 128 + 32 * b + 32],
                                             past[br][:, 4 * t + b, a, 128 + kvh * HD:128 + (kvh + 1) * HD],
                                             start=False, stop=(a == 1), skip_group_check=True)
                last.then_inc(av_done, 1)

            for n in range(NU + LAG_V):
                if n < NU:
                    scores(n)
                if 0 <= n - LAG_T < NU:
                    transposes(n - LAG_T)
                if n >= LAG_V:
                    values(n - LAG_V)
            pe.wait_ge(o_out, NT + 2)
            for i in range(GQA):
                for t in range(NT):
                    last = pe.transpose(ps[:, i, t * 128:(t + 1) * 128], otm[:, t, i * 128:(i + 1) * 128], k.ident)
                last.then_inc(ot_done, 1)
            for g in range(2):
                last = pe.transpose(ps[:, 4, g * 128:(g + 1) * 128], osm[:, g, :], k.ident)
            last.then_inc(ot_done, 1)

        def copy_probs(eng, copy, n, done):
            kind, t, kvh, i, br = units[n]
            eng.wait_ge(pt_done, n + 1)
            if n >= 2:
                eng.wait_ge(av_done, n - 1)
            w = {"cmp": 256, "kv": (t + 1) * 128, "scmp": 128, "skv": 256}[kind]
            last = copy(PT[:, n % 2, 0:w], ps[:, 3 + n % 2, 0:w])
            if kind == "skv":
                last = copy(PT[0:NS, n % 2, 256:384], ps[0:NS, 3 + n % 2, 256:384])
            last.then_inc(done, 1)

        @block.scalar
        def _(act):
            def probs(n):
                kind, t, kvh, i, br = units[n]
                act.wait_ge(masked, n + 1)
                if n >= 3:
                    act.wait_ge(pt_done, n - 2)
                if kind == "cmp":
                    act.activation(P[:, n % 3, 0:256], sc[:, :], ACT.Exp).then_inc(p_ready, 1)
                    return
                w = {"kv": (t + 1) * 128, "scmp": 128, "skv": 320}[kind]
                g = group[n] % 2
                if kind == "kv":
                    d = den[:, g, br + 1, kvh * 4 + i:kvh * 4 + i + 1]
                else:
                    d = den[:, g, (0 if kind == "scmp" else br + 1), kvh:kvh + 1]
                act.activation(P[:, n % 3, 0:w], ps[:, n % 3, 0:w], ACT.Exp, bias=mx[:, n % 3:n % 3 + 1],
                               accum_out=d).then_inc(p_ready, 1)

            for n in range(NU + 2):
                if n < NU:
                    probs(n)
                if n >= 2 and on_act(n - 2):
                    copy_probs(act, act.copy, n - 2, pt_by_act)
            for i in range(GQA):
                act.wait_ge(ot_done, i + 1)
                act.copy(k.oT[:, 4 + i, 0:SEQ], ps[:, i, :])

        @block.vector
        def _(dve):
            step = k.dve.after

            def mask(n):
                kind, t, kvh, i, br = units[n]
                S = ps[:, n % 3, :]
                dve.wait_ge(s_done, n + 1)
                if kind == "cmp":
                    s3 = sc[:, :].rearrange("p (h c) -> p h c", h=8)
                    neg = c["cneg"][:, 32 * t:32 * t + 32].unsqueeze(1).broadcast_to([128, 8, 32])
                    ok = c["cm"][:, 32 * t:32 * t + 32].unsqueeze(1).broadcast_to([128, 8, 32])
                    step(dve.tensor_tensor(s3, S[:, 0:256].rearrange("p (h c) -> p h c", h=8), neg, ALU.add))
                    step(dve.tensor_reduce(mx8[:, :], s3, AX.X, ALU.max))
                    dve.tensor_tensor(s3, s3, mx8[:, :].unsqueeze(2).broadcast_to([128, 8, 32]),
                                      ALU.subtract).then_inc(masked, 1)
                    dve.wait_ge(p_ready, n + 1)
                    p3 = P[:, n % 3, 0:256].rearrange("p (h c) -> p h c", h=8)
                    dve.tensor_tensor(p3, p3, ok, ALU.mult).then_inc(pm_ready, 1)
                    dve.wait_ge(pm_ready, t + 1)
                    dve.tensor_reduce(den[:, group[n] % 2, 0, :], p3, AX.X, ALU.add)
                    return
                w = {"kv": (t + 1) * 128, "scmp": 128, "skv": 320}[kind]
                if n >= 3:
                    dve.wait_ge(p_ready, n - 2)
                dve.tensor_reduce(mx[:, n % 3:n % 3 + 1], S[:, 0:w], AX.X, ALU.max, negate=True).then_inc(masked, 1)

            def finish(gr):
                dve.wait_ge(av_done, last_of[gr] + 1)
                dve.wait_ge(p_ready, last_of[gr] + 1)
                if gr < NT:
                    n, gates = 8, k.gates[:, gr, :].rearrange("p (h c) -> p c h", c=3)
                    dst = otm[:, gr, :].rearrange("p (i h d) -> p h i d", i=4, h=2)
                else:
                    n, gates = 2, k.gsr[:, gr - NT, :, :].rearrange("p h c -> p c h")
                    dst = osm[:, gr - NT, :]
                d, w = den[:, gr % 2, :, 0:n], wgt[:, :, 0:n]
                step(dve.tensor_scalar(w, d, 1e-30, None, ALU.max))
                step(dve.reciprocal(w, w))
                step(dve.tensor_tensor(w, w, gates, ALU.mult))
                for b in range(3):
                    last = dve.tensor_tensor(acc[:, b, 0:n * HD].rearrange("p (h d) -> p h d", d=HD),
                                             ps[:, 5 + b, 0:n * HD].rearrange("p (h d) -> p h d", d=HD),
                                             wgt[:, b, 0:n].unsqueeze(2).broadcast_to([128, n, HD]), ALU.mult)
                step(last)
                a = [acc[:, b, 0:n * HD] for b in range(3)]
                step(dve.tensor_tensor(a[0], a[0], a[1], ALU.add))
                if gr < NT:
                    a = [x.rearrange("p (h i d) -> p h i d", h=2, i=4) for x in a]
                dve.tensor_tensor(dst, a[0], a[2], ALU.add).then_inc(o_out, 1)

            for n in range(NU + LAG_V + 1):
                if n < NU:
                    mask(n)
                if 2 <= n < NU + 2 and not on_act(n - 2):
                    copy_probs(dve, dve.tensor_copy, n - 2, pt_by_dve)
                for gr in range(NT + 2):
                    if last_of[gr] + LAG_V == n:
                        finish(gr)
            dve.wait_ge(ot_done, GQA + 1)
            src = ps[:, 4, 0:256].rearrange("p (b i t) -> p b i t", b=B, i=4)
            for i in range(GQA):
                dve.tensor_copy(k.oT[:, 4 + i, SEQ:TOK].rearrange("p (b t) -> p b t", b=B), src[:, :, i, :])


class Norm:

    def __init__(self, k, name, row, eps, ctx):
        self.k, self.eps = k, eps
        sem = k.sem
        self.summed, self.rstd_ready = sem(name + "_stats"), sem(name + "_rstd")
        self.scaled, self.ready = sem(name + "_scaled"), sem(name + "_ready")
        self.t_done, self.t_out, self.vec_in = sem(name + "_t_done"), sem(name + "_t_out"), sem(name + "_vec_in")
        nc = k.nc
        self.vec = ctx.enter_context(nc.sbuf_tensor(name + "_gb", [128, 2, D], F32))
        self.st = ctx.enter_context(nc.sbuf_tensor(name + "_st", [128, NTT, 2, 6], F32))
        self.mv = ctx.enter_context(nc.sbuf_tensor(name + "_mv", [128, NTT, 2], F32))
        self.rs = ctx.enter_context(nc.sbuf_tensor(name + "_rs", [128, NTT], F32))
        self.row = row

    def load(self, eng):
        src = self.k.io["ln"][self.k.layer, self.row:self.row + 2, :].unsqueeze(0).broadcast_to([128, 2, D])
        eng.dma_start(self.vec[:, :, :], src).then_inc(self.vec_in, 16)

    def stats(self, dve, i):
        k, rows = self.k, TILES[i]
        for n in range(2):
            last = dve.bn_stats(self.st[0:rows, i, n, :], k.x[0:rows, i, n * 512:(n + 1) * 512])
        k.dve.after(last)
        dve.bn_aggr(self.mv[0:rows, i, :], self.st[0:rows, i, :, :].rearrange("p a s -> p (a s)")).then_inc(self.summed, 1)

    def rstd(self, pool, i):
        rows = TILES[i]
        pool.wait_ge(self.summed, i + 1)
        r = self.rs[0:rows, i:i + 1]
        self.k.pool.after(pool.tensor_scalar(r, self.mv[0:rows, i, 1:2], self.eps, None, ALU.add))
        pool.tensor_tensor(r, r, self.k.c["mhalf"][0:rows, 0:1], ALU.pow).then_inc(self.rstd_ready, 1)

    def scale(self, dve, i):
        k, rows = self.k, TILES[i]
        x = k.x[0:rows, i, :]
        if i == 0:
            dve.wait_ge(self.vec_in, 16)
        dve.wait_ge(self.rstd_ready, i + 1)
        k.dve.after(dve.tensor_scalar(x, x, self.mv[0:rows, i, 0:1], self.rs[0:rows, i:i + 1], ALU.subtract, ALU.mult))
        dve.tensor_tensor(x, x, self.vec[0:rows, 0, :], ALU.mult).then_inc(self.scaled, 1)

    def shift(self, pool, i):
        k, rows = self.k, TILES[i]
        x = k.x[0:rows, i, :]
        pool.wait_ge(self.scaled, i + 1)
        pool.tensor_tensor(x, x, self.vec[0:rows, 1, :], ALU.add).then_inc(self.ready, 1)

    def transposes(self, pe, i):
        k, rows = self.k, TILES[i]
        pe.wait_ge(self.ready, i + 1)
        if i:
            pe.wait_ge(self.t_out, i)
        for kk in range(KT_D):
            last = pe.transpose(k.ps[:, 6 + kk // 4, kk % 4 * 128:kk % 4 * 128 + rows],
                                k.x[0:rows, i, kk * 128:(kk + 1) * 128], k.ident[0:rows, 0:rows])
        last.then_inc(self.t_done, 1)

    def copies(self, act, i):
        k, rows = self.k, TILES[i]
        act.wait_ge(self.t_done, i + 1)
        for h in range(2):
            last = act.copy(k.xT[:, 4 * h:4 * h + 4, i * 128:i * 128 + rows],
                            k.ps[:, 6 + h, :].rearrange("p (a t) -> p a t", a=4)[:, :, 0:rows])
        last.then_inc(self.t_out, 1)


def merge(k):
    nc, io, l, ps = k.nc, k.io, k.layer, k.ps
    sem = k.sem
    RING, HRING = 4, 3
    HALF = D // 2
    w_in, wo_in = [sem(f"w_in{n}") for n in range(RING)], [sem(f"wo_in{n}") for n in range(4)]
    x_hi, x_lo, w_hi, w_lo = sem("x_high_ready"), sem("x_low_ready"), sem("w_high_ready"), sem("w_low_ready")
    m_hi, m_lo, wo_hi, wo_lo = sem("merged_high"), sem("merged_low"), sem("wo_high"), sem("wo_low")
    unit_done, g_ready, b_out, merged = sem("unit_done"), sem("gate_ready"), sem("branch_out"), sem("merged")
    m_done, m_out, x1_stored = sem("mix_product_done"), sem("mix_product_out"), sem("x1_stored")
    k.x1_stored = x1_stored
    with ExitStack() as ctx:
        def sb(name, shape, dt=F32):
            return ctx.enter_context(nc.sbuf_tensor(name, shape, dt))
        w32, wl = two_types(nc, ctx, "w_ring", [128, RING, 1536])
        wh = sb("w_high", [128, HRING, 1536], F32R)
        xh = sb("xT_high", [128, KT_D, TOK], F32R)
        oh = sb("oT_high", [128, KT_D, TOK], F32R)
        mT, ml = two_types(nc, ctx, "mergedT", [128, KT_D, TOK])
        mh = sb("mergedT_high", [128, KT_D, TOK], F32R)
        tg = sb("tanh_gate", [128, 2, TOK])
        part = sb("branch_part", [128, TOK])
        wo32 = k.oT[:, :, 0:HALF]
        wol = k.oT_low[:, :, 0:HALF]
        woh = oh[:, :, 0:HALF]
        norm = Norm(k, "ln1", 0, 4 * EPS, ctx)
        block = ctx.enter_context(nc.Block())
        TILE_OF = ((0, 1), (2, 3), (4, 5, 6, 7))
        TH = TOK // 2
        HALVES = (slice(0, TH), slice(TH, TOK))
        UNIT_AT = (0, 1280, 2560, 4096)
        NG_ = KT_D * 3
        NU = NG_ + 4
        width = [UNIT_AT[u % 3 + 1] - UNIT_AT[u % 3] if u < NG_ else 2 * HALF for u in range(NU)]
        X_PARTS = (("x", 0, 4), ("x", 4, 8), ("o", 0, 2), ("o", 2, 4), ("o", 4, 8))

        @block.sync
        def _(sp):
            for u in range(NU):
                if u >= RING:
                    sp.wait_ge(unit_done, u - RING + 1)
                dst = w32[:, u % RING, 0:width[u]]
                if u < NG_:
                    sp.dma_start(dst, io["wm"][l, u // 3, :, UNIT_AT[u % 3]:UNIT_AT[u % 3 + 1]]).then_inc(w_in[u % RING], 16)
                else:
                    kk = 2 * (u - NG_)
                    sp.dma_start(dst.rearrange("p (k n) -> p k n", k=2), io["wo"][l, :, kk:kk + 2, 0:HALF]
                                 ).then_inc(w_in[u % RING], 16)
            sp.wait_ge(unit_done, NG_)
            for q in range(4):
                sp.dma_start(wo32[:, 2 * q:2 * q + 2, :], io["wo"][l, :, 2 * q:2 * q + 2, HALF:D]).then_inc(wo_in[q], 16)
            norm.load(sp)
            for i, rows in enumerate(TILES):
                sp.wait_ge(norm.ready, i + 1)
                sp.dma_start(io["x1"][i * 128:i * 128 + rows, :], k.x[0:rows, i, :]).then_inc(x1_stored, 16)

        @block.tensor
        def _(pe):
            def product(out, w, x, first, last):
                pe.matmul(out, w[0], x[0], start=first, stop=False)
                pe.matmul(out, w[0], x[1], start=False, stop=False)
                return pe.matmul(out, w[1], x[0], start=False, stop=last)

            def parts(x, xl, kk, cols):
                return x[:, kk, cols], xl[:, kk, cols]
            for u in range(NG_):
                b, base = u % 3, 4 * (u % 2)
                pe.wait_ge(w_lo, u + 1)
                if u >= 2:
                    pe.wait_ge(b_out, u - 1)

                def w(kk):
                    return wh[:, u % HRING, kk * 128:(kk + 1) * 128], wl[:, u % RING, kk * 128:(kk + 1) * 128]
                for half, cols in enumerate(HALVES):
                    for kk in range(KT_D):
                        if u == 0 and kk % 4 == 0:
                            pe.wait_ge(x_lo, kk // 4 + 1)
                        product(ps[:, base + half, 0:TH], w(kk), parts(xh, k.xT_low, kk, cols), kk == 0, kk == KT_D - 1)
                ks = TILE_OF[b]
                if u < 3:
                    pe.wait_ge(x_lo, 3 + u)
                for half, cols in enumerate(HALVES):
                    for n, kk in enumerate(ks):
                        last = product(ps[:, base + 2 + half, 0:TH], w(KT_D + n), parts(oh, k.oT_low, kk, cols), n == 0, n == len(ks) - 1)
                last.then_inc(unit_done, 1)
            pe.wait_ge(b_out, NG_)
            for q in range(4):
                u = NG_ + q
                pe.wait_ge(w_lo, u + 1)
                pe.wait_ge(m_lo, 2 * q + 2)
                for i, rows in enumerate(TILES):
                    for a in range(2):
                        kk, cols = 2 * q + a, slice(i * 128, i * 128 + rows)
                        wsl = slice(a * HALF, (a + 1) * HALF)
                        last = product(ps[0:rows, i, :], parts(mh, ml, kk, cols), (wh[:, u % HRING, wsl], wl[:, u % RING, wsl]),
                                       kk == 0, kk == KT_D - 1)
                last.then_inc(unit_done, 1)
            for i in range(NTT + 2):
                if i < NTT:
                    rows = TILES[i]
                    if i:
                        pe.wait_ge(m_out, i)
                    for kk in range(KT_D):
                        if i == 0 and kk % 2 == 0:
                            pe.wait_ge(wo_lo, kk // 2 + 1)
                        last = product(ps[0:rows, (i + 5) % 6, :], parts(mh, ml, kk, slice(i * 128, i * 128 + rows)),
                                       (woh[:, kk, :], wol[:, kk, :]), kk == 0, kk == KT_D - 1)
                    last.then_inc(m_done, 1)
                if i >= 2:
                    norm.transposes(pe, i - 2)

        @block.scalar
        def _(act):
            def x_high(n):
                what, lo, hi = X_PARTS[n]
                src, dst = (k.xT, xh) if what == "x" else (k.oT, oh)
                act.copy(dst[:, lo:hi, :], src[:, lo:hi, :]).then_inc(x_hi, 1)

            def w_high(u):
                act.wait_ge(w_in[u % RING], 16 * (u // RING + 1))
                if u >= HRING:
                    act.wait_ge(unit_done, u - HRING + 1)
                act.copy(wh[:, u % HRING, 0:width[u]], w32[:, u % RING, 0:width[u]]).then_inc(w_hi, 1)

            def m_high(m):
                act.wait_ge(merged, m + 1)
                act.copy(mh[:, m, :], mT[:, m, :]).then_inc(m_hi, 1)
            x_high(0)
            w_high(0)
            x_high(1)
            x_high(2)
            w_high(1)
            x_high(3)
            x_high(4)
            for u in range(NG_):
                base = 4 * (u % 2)
                w_high(u + 2)
                act.wait_ge(unit_done, u + 1)
                if u >= 2:
                    act.wait_ge(b_out, u - 1)
                act.activation(tg[:, u % 2, :].rearrange("p (a t) -> p a t", a=2), ps[:, base:base + 2, 0:TH],
                               ACT.Tanh, scale=0.5).then_inc(g_ready, 1)
                if u >= 3 and u % 3 == 0:
                    m_high(u // 3 - 1)
            m_high(KT_D - 1)
            w_high(NG_ + 2)
            w_high(NG_ + 3)
            for q in range(4):
                act.wait_ge(wo_in[q], 16)
                act.copy(woh[:, 2 * q:2 * q + 2, :], wo32[:, 2 * q:2 * q + 2, :]).then_inc(wo_hi, 1)
            for i in range(NTT):
                norm.copies(act, i)

        @block.vector
        def _(dve):
            def rest(low, src, high):
                return dve.tensor_tensor(low, src, high.bitcast(F32), ALU.subtract)

            def x_low(n):
                what, lo, hi = X_PARTS[n]
                low, src, high = (k.xT_low, k.xT, xh) if what == "x" else (k.oT_low, k.oT, oh)
                dve.wait_ge(x_hi, n + 1)
                rest(low[:, lo:hi, :], src[:, lo:hi, :], high[:, lo:hi, :]).then_inc(x_lo, 1)

            def w_low(u):
                dve.wait_ge(w_hi, u + 1)
                rest(wl[:, u % RING, 0:width[u]], w32[:, u % RING, 0:width[u]], wh[:, u % HRING, 0:width[u]]).then_inc(w_lo, 1)

            def m_low(m):
                dve.wait_ge(m_hi, m + 1)
                rest(ml[:, m, :], mT[:, m, :], mh[:, m, :]).then_inc(m_lo, 1)
            x_low(0)
            w_low(0)
            x_low(1)
            x_low(2)
            w_low(1)
            x_low(3)
            x_low(4)
            for u in range(NG_):
                m, b, base = u // 3, u % 3, 4 * (u % 2)
                w_low(u + 2)
                dve.wait_ge(g_ready, u + 1)
                dst = (mT[:, m, :] if b == 0 else part[:, :]).rearrange("p (a t) -> p a t", a=2)
                dve.scalar_tensor_tensor(dst, tg[:, u % 2, :].rearrange("p (a t) -> p a t", a=2), 1.0,
                                         ps[:, base + 2:base + 4, 0:TH], ALU.add, ALU.mult).then_inc(b_out, 1)
                if b:
                    dve.wait_ge(b_out, u + 1)
                    last = dve.tensor_tensor(mT[:, m, :], mT[:, m, :], part[:, :], ALU.add)
                    if b == 1:
                        k.dve.after(last)
                    else:
                        last.then_inc(merged, 1)
                        dve.wait_ge(merged, m + 1)
                if u >= 3 and b == 0:
                    m_low(m - 1)
            m_low(KT_D - 1)
            w_low(NG_ + 2)
            w_low(NG_ + 3)
            for q in range(4):
                dve.wait_ge(wo_hi, q + 1)
                rest(wol[:, 2 * q:2 * q + 2, :], wo32[:, 2 * q:2 * q + 2, :], woh[:, 2 * q:2 * q + 2, :]).then_inc(wo_lo, 1)
            dve.wait_ge(k.x_in, 32)
            dve.wait_ge(unit_done, NU)
            for i, rows in enumerate(TILES):
                xs = k.x[0:rows, i, 0:HALF]
                dve.scalar_tensor_tensor(xs, xs, 2 * ALPHA, ps[0:rows, i, :], ALU.mult, ALU.add).then_inc(m_out, 1)
            for i in range(NTT + 1):
                if i < NTT:
                    rows = TILES[i]
                    dve.wait_ge(m_done, i + 1)
                    xs = k.x[0:rows, i, HALF:D]
                    dve.scalar_tensor_tensor(xs, xs, 2 * ALPHA, ps[0:rows, (i + 5) % 6, :], ALU.mult, ALU.add).then_inc(m_out, 1)
                    dve.wait_ge(m_out, NTT + i + 1)
                    norm.stats(dve, i)
                if i:
                    norm.scale(dve, i - 1)

        @block.gpsimd
        def _(pool):
            for i in range(NTT + 1):
                if i < NTT:
                    norm.rstd(pool, i)
                if i:
                    norm.shift(pool, i - 1)


def experts(k):
    nc, io, l, ps, c = k.nc, k.io, k.layer, k.ps, k.c
    sem = k.sem
    lg_done, ex_ready, sel_ready, rank_done = sem("logits_done"), sem("exp_ready"), sem("choice_ready"), sem("rank_done")
    plan_ready, ex_clear, table_zeroed, table_in = (sem("plan_ready"), sem("exp_cleared"), sem("table_zeroed"),
                                                    sem("table_written"))
    gu_in = [sem("gate_up_in_a"), sem("gate_up_in_b")]
    dw_in = [sem("down_in_a"), sem("down_in_b")]
    idx_in, x_in = [sem("idx_in_a"), sem("idx_in_b")], [sem("rows_in_a"), sem("rows_in_b")]
    xt_done, xt_act, xt_dve = sem("rowsT_done"), sem("rowsT_by_act"), sem("rowsT_by_dve")
    gu_done, act_ready = sem("gate_up_done"), sem("hidden_ready")
    tanh_ready2 = [sem("silu_ready_a"), sem("silu_ready_b")]
    tanh_ready, at_done, at_out = sem("gate_tanh_ready"), sem("hiddenT_done"), sem("hiddenT_out")
    dn_done = [sem("down_done_a"), sem("down_done_b")]
    y_act, y_dve, y_stored = sem("y_by_act"), sem("y_by_dve"), [sem("y_stored_a"), sem("y_stored_b")]
    x_stored = sem("layer_output_stored")
    all_stored = sem("all_expert_rows_stored")
    yg_in, y_used = [sem(f"y_rows_in{i}") for i in range(2)], sem("y_rows_used")

    with ExitStack() as outer:
        def so(name, shape, dt=F32):
            return outer.enter_context(nc.sbuf_tensor(name, shape, dt))
        norm = Norm(k, "ln2", 2, EPS, outer)
        slot = so("slot", [128, 2, NTT], I32)
        wt = so("pair_weight", [128, 2, NTT])
        plan = so("plan", [1, 34], I32)
        with ExitStack() as ctx:
            def sb(name, shape, dt=F32):
                return ctx.enter_context(nc.sbuf_tensor(name, shape, dt))
            S3 = [128, NTT, E]
            ex, aff, score, ms, t1 = sb("ex", S3), sb("aff", S3), sb("score", S3), sb("ms", S3), sb("rt1", S3)
            oh = sb("onehot", [128, 2, NTT, E])
            both = sb("both", S3)
            g = sb("grp", [128, 8, NTT, EG])
            v = sb("rv", [128, 4, NTT])
            cnt, nch, cum, basev = sb("cnt", [128, E]), sb("nch", [128, E]), sb("cum", [128, E]), sb("base", [128, E])
            big = sb("cmpbuf", [128, 32, E])
            pf = sb("plan_f", [1, 34])
            slotf = sb("slot_f", [128, 2, NTT])
            gu = [sb("gate_up_a", [128, 4096]), sb("gate_up_b", [128, 4096])]
            dw = [sb("down_a", [128, 2048]), sb("down_b", [128, 2048])]
            idx = [sb("idx_a", [128, 1], I32), sb("idx_b", [128, 1], I32)]
            xg = [sb("rows_a", [128, D]), sb("rows_b", [128, D])]
            xgT = [sb("rowsT_a", [128, KT_D, 128]), sb("rowsT_b", [128, KT_D, 128])]
            tgt = [sb("gtanh_a", [128, FE]), sb("gtanh_b", [128, FE])]
            h1 = [sb("hid_a", [128, FE]), sb("hid_b", [128, FE])]
            hT = [sb("hidT_a", [128, 2, 128]), sb("hidT_b", [128, 2, 128])]
            y = [sb("y_a", [128, D]), sb("y_b", [128, D])]
            block = ctx.enter_context(nc.Block())
            XB, GB, HB, YB = [0, 2], [4, 5], [0, 1], [6, 2]

            def pairs(eng):
                eng.wait_ge(plan_ready, 1)
                return eng.value_load(plan[0:1, 32:33], min_val=1, max_val=MAXCH // 2)

            @block.sync
            def _(sp):
                norm.load(sp)
                with sp.Fori(0, pairs(sp)) as p:
                    e = [sp.value_load(plan[0:1, bass.ds(2 * p + a, 1)], min_val=0, max_val=E - 1) for a in range(2)]
                    for a in range(2):
                        sp.wait_ge(gu_done, 2 * p + a + 1)
                        sp.dma_start(gu[a][:, :], io["we"][l, e[a], :, 0:4096]).then_inc(gu_in[a], 16)
                    sp.wait_ge(table_in, 16 * 2 * NTT)
                    for a in range(2):
                        sp.wait_ge(xt_done, 2 * p + 1)
                        sp.dma_start(idx[a][:, :], io["slot_token"][bass.ds((2 * p + a) * 128, 128), :]).then_inc(idx_in[a], 16)
                    for a in range(2):
                        sp.wait_ge(dn_done[a], p + 1)
                        sp.dma_start(dw[a][:, :], io["we"][l, e[a], :, 4096:6144]).then_inc(dw_in[a], 16)

            @block.tensor
            def _(pe):
                for i, rows in enumerate(TILES):
                    for kk in range(KT_D):
                        last = pe.matmul(ps[0:rows, 0, i * E:(i + 1) * E], k.xT[:, kk, i * 128:i * 128 + rows],
                                         k.wr[:, kk, :], start=(kk == 0), stop=(kk == KT_D - 1))
                last.then_inc(lg_done, 1)
                pe.wait_ge(sel_ready, 1)
                for i, rows in enumerate(TILES):
                    for j in range(i):
                        pe.matmul(ps[0:rows, 1, i * E:(i + 1) * E], c["ones"][:, 0:rows], both[:, j, :],
                                  start=(j == 0), stop=False)
                    pe.matmul(ps[0:rows, 1, i * E:(i + 1) * E], c["tri"][0:rows, 0:rows], both[0:rows, i, :],
                              start=(i == 0), stop=True)
                for j, rows in enumerate(TILES):
                    last = pe.matmul(ps[:, 1, NTT * E:(NTT + 1) * E], c["ones"][0:rows, :], both[0:rows, j, :],
                                     start=(j == 0), stop=(j == NTT - 1))
                last.then_inc(rank_done, 1)
                for s in (xt_done, dn_done[0], dn_done[1]):
                    pe.sem_inc(s, 1)
                pe.sem_inc(gu_done, 2)
                with pe.Fori(0, pairs(pe)) as p:
                    for a in range(2):
                        pe.wait_ge(x_in[a], 16 * p + 16)
                        pe.wait_ge(y_act, 2 * p + 1)
                        pe.wait_ge(y_dve, 2 * p + 1)
                        for kk in range(KT_D):
                            last = pe.transpose(ps[:, XB[a] + kk // 4, kk % 4 * 128:(kk % 4 + 1) * 128],
                                                xg[a][:, kk * 128:(kk + 1) * 128], k.ident)
                        last.then_inc(xt_done, 1)
                    for a in range(2):
                        pe.wait_ge(gu_in[a], 16 * p + 16)
                        pe.wait_ge(xt_act, 2 * p + a + 1)
                        pe.wait_ge(xt_dve, 2 * p + a + 1)
                        for kk in range(KT_D):
                            last = pe.matmul(ps[:, GB[a], :], xgT[a][:, kk, :], gu[a][:, kk * 512:(kk + 1) * 512],
                                             start=(kk == 0), stop=(kk == KT_D - 1))
                        last.then_inc(gu_done, 1)
                    for a in range(2):
                        pe.wait_ge(act_ready, 2 * p + a + 1)
                        for f in range(2):
                            last = pe.transpose(ps[:, HB[a], f * 128:(f + 1) * 128], h1[a][:, f * 128:(f + 1) * 128], k.ident)
                        last.then_inc(at_done, 1)
                        pe.wait_ge(at_out, 2 * p + a + 1)
                        pe.wait_ge(dw_in[a], 16 * p + 16)
                        for n in range(2):
                            for f in range(2):
                                last = pe.matmul(ps[:, YB[a] + n, :], hT[a][:, f, :],
                                                 dw[a][:, f * D + n * 512:f * D + (n + 1) * 512],
                                                 start=(f == 0), stop=(f == 1))
                        last.then_inc(dn_done[a], 1)

            @block.scalar
            def _(act):
                act.wait_ge(lg_done, 1)
                act.wait_ge(ex_clear, 1)
                act.activation(ex[:, 0:NT, :], ps[:, 0, 0:NT * E].rearrange("p (i e) -> p i e", i=NT), ACT.Exp, scale=-1.0)
                act.activation(ex[0:NS, NT, :], ps[0:NS, 0, NT * E:NTT * E], ACT.Exp, scale=-1.0).then_inc(ex_ready, 1)
                act.sem_inc(y_act, 1)
                for s in y_stored:
                    act.sem_inc(s, 16)
                act.wait_ge(k.rows_cleared, 16 * (MAXCH // 2 + 1))
                with act.Fori(0, pairs(act)) as p:
                    for a in range(2):
                        act.wait_ge(xt_done, 2 * p + a + 2)
                        act.copy(xgT[a][:, 0:4, :], ps[:, XB[a], :].rearrange("p (a t) -> p a t", a=4)).then_inc(xt_act, 1)
                    for a in range(2):
                        act.wait_ge(gu_done, 2 * p + a + 3)
                        act.activation(tgt[a][:, :], ps[:, GB[a], 0:FE], ACT.Tanh, scale=0.5).then_inc(tanh_ready, 1)
                    for a in range(2):
                        act.wait_ge(dn_done[a], p + 2)
                        act.wait_ge(y_stored[a], 16 * p + 16)
                        act.copy(y[a][:, 0:512], ps[:, YB[a], :]).then_inc(y_act, 1)
                        act.wait_ge(y_act, 2 * p + a + 2)
                        act.wait_ge(y_dve, 2 * p + a + 2)
                        act.dma_start(io["ys"][bass.ds((2 * p + a) * 128, 128), :], y[a][:, :]).then_inc(y_stored[a], 16)

            @block.gpsimd
            def _(pool):
                pool.dma_start(io["slot_token"].rearrange("(p c) o -> p (c o)", p=128), k.zero[:, :]).then_inc(table_zeroed, 16)
                pool.wait_ge(table_zeroed, 16)
                pool.wait_ge(plan_ready, 1)
                for a in range(2):
                    for i, rows in enumerate(TILES):
                        pool.indirect_dma_start(io["slot_token"], bass.IndirectOffsetOnAxis(slot[0:rows, a, i:i + 1], 0),
                                                k.tokid[0:rows, i:i + 1], None).then_inc(table_in, 16)
                pool.wait_ge(table_in, 16 * 2 * NTT)
                pool.wait_ge(k.x1_stored, 16 * NTT)
                n = pairs(pool)
                with pool.Fori(0, n) as p:
                    for a in range(2):
                        pool.wait_ge(idx_in[a], 16)
                        pool.sem_clear(idx_in[a])
                        pool.indirect_dma_start(xg[a][:, :], None, io["x1"], bass.IndirectOffsetOnAxis(idx[a][:, 0:1], 0)
                                                ).then_inc(x_in[a], 16)

            @block.vector
            def _(dve):
                step = k.dve.after
                dve.memset(ex[:, :, :], 1.0).then_inc(ex_clear, 1)
                dve.memset(g[:, :, :, :], 0.0)
                dve.wait_ge(ex_ready, 1)
                step(dve.tensor_scalar(aff[:, :, :], ex[:, :, :], 1.0, None, ALU.add))
                step(dve.reciprocal(aff[:, :, :], aff[:, :, :]))
                step(dve.tensor_tensor(score[:, :, :], aff[:, :, :], k.br[:, :].unsqueeze(1).broadcast_to(S3), ALU.add))
                s4 = score[:, :, :].rearrange("p i (g e) -> p i g e", g=EG)
                G = [g[:, n, :, :] for n in range(8)]
                step(dve.tensor_tensor(G[0], s4[:, :, :, 0], s4[:, :, :, 1], ALU.max))
                step(dve.tensor_tensor(G[1], s4[:, :, :, 0], s4[:, :, :, 1], ALU.min))
                step(dve.tensor_tensor(G[2], s4[:, :, :, 2], s4[:, :, :, 3], ALU.max))
                step(dve.tensor_tensor(G[3], s4[:, :, :, 2], s4[:, :, :, 3], ALU.min))
                step(dve.tensor_tensor(G[4], G[0], G[2], ALU.max))
                step(dve.tensor_tensor(G[5], G[0], G[2], ALU.min))
                step(dve.tensor_tensor(G[6], G[1], G[3], ALU.max))
                step(dve.tensor_tensor(G[5], G[5], G[6], ALU.max))
                step(dve.tensor_tensor(G[4], G[4], G[5], ALU.add))

                def first_best(val, out, order, width, tmp):
                    shape = [128, NTT, width]
                    step(dve.tensor_reduce(v[:, 0, :], val, AX.X, ALU.max))
                    step(dve.tensor_tensor(tmp, val, v[:, 0, :].unsqueeze(2).broadcast_to(shape), ALU.is_equal))
                    step(dve.tensor_tensor(tmp, tmp, order.unsqueeze(1).broadcast_to(shape), ALU.mult))
                    step(dve.tensor_reduce(v[:, 1, :], tmp, AX.X, ALU.max))
                    step(dve.tensor_tensor(out, tmp, v[:, 1, :].unsqueeze(2).broadcast_to(shape), ALU.is_equal))

                first_best(G[4], G[0], c["g4"], EG, G[1])
                step(dve.tensor_scalar(G[1], G[0], 1.0, -NEG, ALU.subtract, ALU.mult))
                ms4 = ms[:, :, :].rearrange("p i (g e) -> p i g e", g=EG)
                for e in range(E // EG):
                    step(dve.tensor_tensor(ms4[:, :, :, e], s4[:, :, :, e], G[0], ALU.mult))
                    step(dve.tensor_tensor(ms4[:, :, :, e], ms4[:, :, :, e], G[1], ALU.add))
                first_best(ms[:, :, :], oh[:, 0, :, :], c["e16"], E, t1[:, :, :])
                step(dve.tensor_scalar(t1[:, :, :], oh[:, 0, :, :], 3 * NEG, None, ALU.mult))
                step(dve.tensor_tensor(ms[:, :, :], ms[:, :, :], t1[:, :, :], ALU.add))
                first_best(ms[:, :, :], oh[:, 1, :, :], c["e16"], E, t1[:, :, :])
                dve.tensor_tensor(both[:, :, :], oh[:, 0, :, :], oh[:, 1, :, :], ALU.add).then_inc(sel_ready, 1)
                for a in range(2):
                    step(dve.tensor_tensor(t1[:, :, :], oh[:, a, :, :], aff[:, :, :], ALU.mult))
                    step(dve.tensor_reduce(v[:, a, :], t1[:, :, :], AX.X, ALU.add))
                step(dve.tensor_tensor(v[:, 2, :], v[:, 0, :], v[:, 1, :], ALU.add))
                step(dve.reciprocal(v[:, 2, :], v[:, 2, :]))
                step(dve.tensor_scalar(v[:, 2, :], v[:, 2, :], 0.5, None, ALU.mult))
                step(dve.tensor_tensor(wt[:, :, :], v[:, 0:2, :], v[:, 2, :].unsqueeze(1).broadcast_to([128, 2, NTT]), ALU.mult))
                dve.wait_ge(rank_done, 1)
                step(dve.tensor_copy(cnt[:, :], ps[:, 1, NTT * E:(NTT + 1) * E]))
                step(dve.tensor_tensor(big[:, 0:5, :], cnt[:, :].unsqueeze(1).broadcast_to([128, 5, E]),
                                       c["th"].unsqueeze(2).broadcast_to([128, 5, E]), ALU.is_gt))
                step(dve.tensor_reduce(nch[:, :], big[:, 0:5, :].rearrange("p m e -> p e m"), AX.X, ALU.add))
                step(dve.tensor_tensor_scan(cum[:, :], c["ones"][:, 0:E], nch[:, :], 0.0, ALU.mult, ALU.add))
                step(dve.tensor_tensor(basev[:, :], cum[:, :], nch[:, :], ALU.subtract))
                step(dve.tensor_scalar(basev[:, :], basev[:, :], 128.0, None, ALU.mult))
                step(dve.tensor_copy(t1[:, :, :], basev[:, :].unsqueeze(1).broadcast_to(S3)))
                step(dve.tensor_tensor(t1[:, 0:NT, :], ps[:, 1, 0:NT * E].rearrange("p (i e) -> p i e", i=NT),
                                       t1[:, 0:NT, :], ALU.add))
                step(dve.tensor_tensor(t1[0:NS, NT, :], ps[0:NS, 1, NT * E:NTT * E], t1[0:NS, NT, :], ALU.add))
                for a in range(2):
                    step(dve.tensor_tensor(ms[:, :, :], t1[:, :, :], oh[:, a, :, :], ALU.mult))
                    step(dve.tensor_reduce(slotf[:, a, :], ms[:, :, :], AX.X, ALU.add))
                dve.tensor_copy(slot[:, :, :], slotf[:, :, :])
                chunk = c["chunk"][0:1, :]
                step(dve.tensor_tensor(big[0:1, :, :], cum[0:1, :].unsqueeze(1).broadcast_to([1, 32, E]),
                                       chunk.unsqueeze(2).broadcast_to([1, 32, E]), ALU.is_le))
                step(dve.tensor_reduce(pf[:, 0:32], big[0:1, :, :], AX.X, ALU.add))
                step(dve.tensor_scalar(pf[:, 0:32], pf[:, 0:32], float(E - 1), None, ALU.min))
                step(dve.tensor_scalar(cum[0:1, 0:1], cum[0:1, E - 1:E], 0.5, None, ALU.mult))
                step(dve.tensor_tensor(big[0:1, :, 0], chunk, cum[0:1, 0:1].broadcast_to([1, 32]), ALU.is_lt))
                step(dve.tensor_reduce(pf[:, 32:33], big[0:1, :, 0], AX.X, ALU.add))
                step(dve.memset(pf[:, 33:34], 0.0))
                dve.tensor_copy(plan[:, :], pf[:, :]).then_inc(plan_ready, 1)
                dve.wait_ge(plan_ready, 1)
                dve.sem_inc(y_dve, 1)
                with dve.Fori(0, pairs(dve)) as p:
                    for a in range(2):
                        dve.wait_ge(xt_done, 2 * p + a + 2)
                        dve.tensor_copy(xgT[a][:, 4:8, :],
                                        ps[:, XB[a] + 1, :].rearrange("p (a t) -> p a t", a=4)).then_inc(xt_dve, 1)
                    for a in range(2):
                        dve.wait_ge(tanh_ready, 2 * p + a + 1)
                        dve.scalar_tensor_tensor(tgt[a][:, :], tgt[a][:, :], 1.0, ps[:, GB[a], 0:FE],
                                                 ALU.add, ALU.mult).then_inc(tanh_ready2[a], 1)
                        dve.wait_ge(tanh_ready2[a], p + 1)
                        dve.tensor_tensor(h1[a][:, :], tgt[a][:, :], ps[:, GB[a], FE:2 * FE], ALU.mult).then_inc(act_ready, 1)
                    for a in range(2):
                        dve.wait_ge(at_done, 2 * p + a + 1)
                        dve.tensor_copy(hT[a][:, :, :], ps[:, HB[a], 0:256].rearrange("p (a t) -> p a t", a=2)).then_inc(at_out, 1)
                        dve.wait_ge(dn_done[a], p + 2)
                        dve.wait_ge(y_stored[a], 16 * p + 16)
                        dve.tensor_copy(y[a][:, 512:1024], ps[:, YB[a] + 1, :]).then_inc(y_dve, 1)

        with ExitStack() as ctx:
            yg = ctx.enter_context(nc.sbuf_tensor("y_rows", [128, 2, 2, D], F32))
            tmp = ctx.enter_context(nc.sbuf_tensor("y_sum", [128, D], F32))
            block = ctx.enter_context(nc.Block())

            @block.gpsimd
            def _(pool):
                pool.wait_ge(all_stored, 1)

                def gather(i):
                    rows = TILES[i]
                    if i >= 2:
                        pool.wait_ge(y_used, i - 1)
                    for a in range(2):
                        pool.indirect_dma_start(yg[0:rows, i % 2, a, :], None, io["ys"],
                                                bass.IndirectOffsetOnAxis(slot[0:rows, a, i:i + 1], 0)).then_inc(yg_in[i % 2], 16)
                gather(0)
                gather(1)
                for i in range(NTT + 1):
                    if i < NTT:
                        norm.rstd(pool, i)
                    if i:
                        norm.shift(pool, i - 1)
                    if i + 2 < NTT:
                        gather(i + 2)
                n = pool.value_load(plan[0:1, 32:33], min_val=1, max_val=MAXCH // 2)
                for a in range(2):
                    pool.wait_ge(x_in[a], 16 * n)
                pool.wait_ge(yg_in[0], 32 * 3)
                pool.wait_ge(yg_in[1], 32 * 2)
                pool.wait_ge(k.stored, 16 * k.n_stored)

            @block.vector
            def _(dve):
                for i in range(NTT + 1):
                    if i < NTT:
                        rows = TILES[i]
                        x, t = k.x[0:rows, i, :], tmp[0:rows, :]
                        dve.wait_ge(yg_in[i % 2], 32 * (i // 2 + 1))
                        k.dve.after(dve.tensor_scalar(t, yg[0:rows, i % 2, 1, :], wt[0:rows, 1, i:i + 1], None, ALU.mult))
                        dve.scalar_tensor_tensor(t, yg[0:rows, i % 2, 0, :], wt[0:rows, 0, i:i + 1], t,
                                                 ALU.mult, ALU.add).then_inc(y_used, 1)
                        dve.wait_ge(y_used, i + 1)
                        k.dve.after(dve.scalar_tensor_tensor(x, x, ALPHA, t, ALU.mult, ALU.add))
                        norm.stats(dve, i)
                    if i:
                        norm.scale(dve, i - 1)

            @block.tensor
            def _(pe):
                for i in range(NTT):
                    norm.transposes(pe, i)

            @block.scalar
            def _(act):
                for i in range(NTT):
                    norm.copies(act, i)

            @block.sync
            def _(sp):
                n = sp.value_load(plan[0:1, 32:33], min_val=1, max_val=MAXCH // 2)
                for a in range(2):
                    sp.wait_ge(y_stored[a], 16 * n + 16)
                sp.sem_inc(all_stored, 1)
                for i, rows in enumerate(TILES):
                    sp.wait_ge(norm.ready, i + 1)
                    out = io["y_p"][i * 128:(i + 1) * 128, :] if i < NT else io["y_s"]
                    sp.dma_start(out, k.x[0:rows, i, :]).then_inc(x_stored, 16)
                sp.wait_ge(x_stored, 16 * NTT)
                sp.wait_ge(k.stored, 16 * k.n_stored)



def layouts(inp):
    a = {n: np.asarray(v) for n, v in inp.items()}
    c = np.ascontiguousarray
    out = {}
    xp, xs = a["x_prompt"].reshape(SEQ, D), a["x_sample"].reshape(NS, D)
    out["xp"], out["xs"] = xp, xs
    out["x0T"] = c(np.concatenate([xp, xs], 0).T.reshape(KT_D, 128, TOK).transpose(1, 0, 2))
    out["consts"] = constants()
    tok = np.zeros((128, NTT), np.int32)
    for i in range(NTT):
        tok[:, i] = np.minimum(i * 128 + np.arange(128), TOK - 1)
    out["tokid"] = tok
    out["page_table"] = a["page_table"].reshape(1, -1).astype(np.int32)
    out["w_router"] = a["w_router"]
    out["br"] = c(np.broadcast_to(a["b_router"], (128, E)))
    w = a["w_in"]
    pa, pu, pv, pq, pkv, pg, pm = (w[:, :, s:e] for s, e in ((0, 256), (256, 512), (512, 768), (768, 1280),
                                                             (1280, 2048), (2048, 2072), (2072, 5144)))
    pq = pq.reshape(L, D, NKV, GQA, HD).transpose(0, 1, 3, 2, 4).reshape(L, D, 512)
    tm = np.concatenate([pq, pkv, pa, pv, pg], 2)
    out["wtm"] = c(tm.reshape(L, KT_D, 128, NCH, CW).transpose(0, 3, 2, 1, 4))
    out["wu"] = c(pu.reshape(L, KT_D, 128, 256).transpose(0, 2, 1, 3))
    g = pm.reshape(L, KT_D, 128, 3, KT_D, 128).transpose(0, 4, 2, 3, 1, 5).reshape(L, KT_D, 128, 3, 1024)
    heads = a["w_branch_nsa"].reshape(L, NKV, GQA, HD, D).transpose(0, 2, 1, 3, 4).reshape(L, 4, 128, D)
    parts = []
    for b, br in enumerate((a["w_branch_pool"].reshape(L, 2, 128, D), a["w_branch_gmlp"].reshape(L, 2, 128, D), heads)):
        br = br.reshape(L, -1, 128, KT_D, 128).transpose(0, 3, 2, 1, 4).reshape(L, KT_D, 128, -1)
        parts += [g[:, :, :, b], br]
    out["wm"] = c(np.concatenate(parts, 3))
    out["wo"] = c(a["w_out"].reshape(L, KT_D, 128, D).transpose(0, 2, 1, 3))
    gu = np.concatenate([a["w_gate"], a["w_up"]], 3).reshape(L, E, KT_D, 128, 512).transpose(0, 1, 3, 2, 4)
    dn = a["w_down"].reshape(L, E, 2, 128, D).transpose(0, 1, 3, 2, 4)
    out["we"] = c(np.concatenate([gu.reshape(L, E, 128, 4096), dn.reshape(L, E, 128, 2048)], 3))
    out["w1"] = c(a["cmp_w1"].reshape(L, 2, CL, HD, HID).transpose(0, 3, 1, 2, 4))
    out["peT"] = c(a["cmp_pe"].transpose(0, 3, 1, 2))
    out["ln"] = c(np.stack([a["ln1_g"], a["ln1_b"], a["ln2_g"], a["ln2_b"]], 1))
    kv = a["cache_cmp_kv"].transpose(0, 1, 4, 5, 3, 2)
    out["cmp_pages"] = c(kv.reshape(L, N_POOL, 128, 2, PAGE))

    def keys_and_values(rows):
        lead = rows.shape[:-4]
        kt = np.moveaxis(rows[..., 0, :, :], -3, -1).reshape(*lead, 128, 128)
        return np.concatenate([kt, rows[..., 1, :, :].reshape(*lead, 128, 128)], -1)
    out["sel_pages"] = c(keys_and_values(a["cache_sel_kv"]))
    win = a["state_win_kv"]
    out["win_rows"] = c(keys_and_values(win.reshape(L, B, 2, 128, 2, NKV, HD)).transpose(0, 3, 1, 2, 4))
    out["state_win"] = win.reshape(L, B, PAST, 256)
    out["state_pool"] = a["state_pool"]
    out["state_pool2"] = a["state_pool"].reshape(L, B * KEEP, 256)
    s = np.zeros((L, 128, NSMALL), np.float32)

    def put(name, v):
        lo, hi = _S[name]
        s[:, :v.shape[1], lo:hi] = v.reshape(L, v.shape[1], hi - lo)
    put("w2", a["cmp_w2"].transpose(0, 2, 1, 3))
    pw = np.zeros((L, 2, 2, 64, 2, 64), np.float32)
    for h in range(2):
        pw[:, :, h, :, h, :] = a["pool_w"].reshape(L, 2, 2, 64, 64)[:, :, h]
    put("poolw", pw.reshape(L, 2, 128, 128).transpose(0, 2, 1, 3))
    put("wsT", a["gmlp_ws"].transpose(0, 3, 1, 2))
    put("bsT", np.repeat(a["gmlp_bs"], 64, 1).reshape(L, 2, 128, 128).transpose(0, 2, 1, 3))
    put("pscale", a["pool_scale"].reshape(L, 2, 128).transpose(0, 2, 1))
    put("b1", a["cmp_b1"].transpose(0, 2, 1))
    put("wss", np.tile(a["gmlp_ws"][:, :, :TS, :TS].transpose(0, 3, 1, 2), (1, B, 1, 1)))
    put("vg", np.broadcast_to(a["gmlp_ln_g"][:, None], (L, 128, 256)))
    put("vb", np.broadcast_to(a["gmlp_ln_b"][:, None], (L, 128, 256)))
    out["small"] = s
    return out


_OUTS = [("y_p", (SEQ, D)), ("y_s", (NS, D)),
         ("o_cmp_p", (L, SEQ, 256)), ("o_sel_p", (L, SEQ, 256)), ("o_win_p", (L, SEQ, 256)), ("o_pool_p", (L, KEEP, 256)),
         ("o_cmp_s", (L, NS, 256)), ("o_sel_s", (L, NS, 256)), ("o_win_s", (L, B, PAST, 256)),
         ("o_pool_s", (L, B, KEEP, 256)), ("o_gmlp_s", (L, NS, 256))]


def kernel(**inputs):
    import concourse.bacc as _bacc
    from concourse.bass_utils import run_bass_kernel_spmd as _run

    arrays = layouts(inputs)
    nc = _bacc.Bacc("TRN2", target_bir_lowering=False, num_devices=1)
    io = {n: nc.dram_tensor("in_" + n, v.shape, mybir.dt.from_np(v.dtype), kind="ExternalInput").ap() for n, v in arrays.items()}
    for n, shape in _OUTS:
        io[n] = nc.dram_tensor("out_" + n, shape, F32, kind="ExternalOutput").ap()
    io["x1"] = nc.dram_tensor("x1_rows", (TOK, D), F32).ap()
    io["ys"] = nc.dram_tensor("expert_rows", (SLOTS, D), F32).ap()
    io["slot_token"] = nc.dram_tensor("slot_token", (SLOTS, 1), I32).ap()
    build(nc, io)
    r = _run(nc, [{"in_" + n: v for n, v in arrays.items()}], core_ids=[0]).results[0]
    r = {n: r["out_" + n] for n, _ in _OUTS}
    kv = (2, NKV, HD)
    return (r["y_p"].reshape(1, SEQ, D), r["y_s"].reshape(B, TS, D),
            r["o_cmp_p"].reshape(L, 1, SEQ, *kv), r["o_sel_p"].reshape(L, 1, SEQ, *kv), r["o_win_p"].reshape(L, 1, SEQ, *kv),
            r["o_pool_p"].reshape(L, 1, KEEP, 256),
            r["o_cmp_s"].reshape(L, B, TS, *kv), r["o_sel_s"].reshape(L, B, TS, *kv), r["o_win_s"].reshape(L, B, PAST, *kv),
            r["o_pool_s"], r["o_gmlp_s"].reshape(L, B, TS, 256))
```

```python
from contextlib import ExitStack

import numpy as np
import concourse.bass as bass
from concourse import mybir

F32 = mybir.dt.float32
F32R = mybir.dt.float32r
I32 = mybir.dt.int32
ALU = mybir.AluOpType
ACT = mybir.ActivationFunctionType
AX = mybir.AxisListType

D, SEQ, L = 1024, 512, 2
B, TS, PAST, PAGE = 8, 8, 256, 128
NS = B * TS
TOK = SEQ + NS
KT_D = D // 128
NT = SEQ // 128
TILES = [128] * NT + [NS]
NTT = len(TILES)
WIN = (2, 4, 8, 16)
KEEP = 15
HD, NH, NKV, GQA = 64, 8, 2, 4
CL, CS = 32, 16
HID = 128
E, EG, FE = 16, 4, 256
N_POOL = B * (PAST // PAGE) * 5 // 4
ALPHA = (2 * L) ** 0.25
EPS = 1e-5
NEG = -1e30

Q0, KV0, A0, V0, G0, TM = 0, 512, 1280, 1536, 1792, 1816
NCH = 4
CW = TM // NCH

XC = SEQ + B * PAST + CL
HC = XC // 2
NG = XC // CS
NB = NG - 2
UW = NG

LOGITS = 4

MAXCH = 24
SLOTS = MAXCH * 128

_C = {}
_at = 0
for _n, _w in [("ident", 128), ("diag", 128), ("cos", NTT * 8), ("sin", NTT * 8), ("cm", NT * 32), ("cneg", NT * 32),
               ("newneg", 2 * 64), ("scneg", 2 * 128), ("bcur0", 4 * 128), ("bcur", 4 * 128), ("bprev", 4 * 128),
               ("bst", 4 * 64), ("bnew", 4 * 64), ("tri", 128), ("ones", 128), ("e16", 16), ("g4", 4), ("th", 5),
               ("chunk", 32), ("gm", 128), ("gms", 64), ("blk", 4), ("rowhead", 4), ("mhalf", NTT), ("gsel", 256), ("lane", 128), ("tok", NTT)]:
    _C[_n] = (_at, _at + _w)
    _at += _w
NCONST = _at

_S = {}
_at = 0
for _n, _w in [("w2", 128), ("poolw", 256), ("wsT", 512), ("bsT", 256), ("pscale", 2), ("b1", 2), ("wss", 32),
               ("vg", 256), ("vb", 256)]:
    _S[_n] = (_at, _at + _w)
    _at += _w
NSMALL = _at


def constants():
    c = np.zeros((128, NCONST), np.float32)

    def put(name, a):
        lo, hi = _C[name]
        a = np.asarray(a, np.float32)
        c[:a.shape[0], lo:hi] = a.reshape(a.shape[0], hi - lo)

    r = np.arange(128)
    put("ident", np.eye(128))
    put("diag", np.where(r[None, :] <= r[:, None], 0.0, NEG))
    pos = np.zeros((NTT, 128), np.float32)
    for i in range(NT):
        pos[i] = i * 128 + r
    pos[NT, :NS] = PAST + r[:NS] % TS
    inv = (1.0 / (np.float32(500000.0) ** (np.arange(8, dtype=np.float32) / np.float32(8)))).astype(np.float32)
    ang = pos[:, :, None] * inv
    put("cos", np.cos(ang).transpose(1, 0, 2))
    put("sin", np.sin(ang).transpose(1, 0, 2))
    c32 = np.arange(32)
    ok = (c32[None, None] < 31) & (c32[None, None] * CS + CL - 1 <= (np.arange(NT)[None, :, None] * 128 + r[:, None, None]))
    put("cm", ok)
    put("cneg", np.where(ok, 0.0, NEG))
    row_b, row_t = r // 32, r % 8
    kb, kt = np.arange(64) // 8, np.arange(64) % 8
    put("newneg", np.stack([np.where((kb[None] == 4 * g + row_b[:, None]) & (kt[None] <= row_t[:, None]), 0.0, NEG)
                            for g in range(2)], 1))
    mb, mc = r // 16, r % 16
    put("scneg", np.stack([np.where((mb[None] == 4 * g + row_b[:, None]) & (mc[None] < 15), 0.0, NEG)
                           for g in range(2)], 1))
    s, t = r[:, None], r[None, :]
    b0, bc, bp, bst, bnew = [], [], [], [], []
    for w in WIN:
        inside = (s <= t) & (s > t - w)
        b0.append(inside / np.minimum(w, t + 1.0) - (s == t))
        bc.append(inside / float(w) - (s == t))
        bp.append((s - 128 > t - w) / float(w))
        sb, sr = np.arange(B * KEEP) // KEEP, np.arange(B * KEEP) % KEEP - KEEP
        bst.append((sb[:, None] == kb[None]) & (sr[:, None] > kt[None] - w))
        bst[-1] = bst[-1] / float(w)
        same = kb[:, None] == kb[None]
        bnew.append((same & (kt[:, None] <= kt[None]) & (kt[:, None] > kt[None] - w)) / float(w) - np.eye(64))
    put("bcur0", np.stack(b0, 1))
    put("bcur", np.stack(bc, 1))
    put("bprev", np.stack(bp, 1))
    put("bst", np.stack(bst, 1))
    put("bnew", np.stack(bnew, 1))
    put("tri", s < t)
    put("ones", np.ones((128, 128)))
    put("e16", np.tile(16 - np.arange(16), (128, 1)))
    put("g4", np.tile(4 - np.arange(4), (128, 1)))
    put("th", np.tile(128 * np.arange(5), (128, 1)))
    put("chunk", np.tile(np.arange(32), (128, 1)))
    put("gm", s <= t)
    put("gms", (kb[:, None] == kb[None]) & (kt[:, None] <= kt[None]))
    put("blk", (r // 32)[:, None] == np.arange(4)[None])
    put("rowhead", (r % 32 // 8)[:, None] == np.arange(4)[None])
    put("mhalf", np.full((128, NTT), -0.5))
    put("lane", np.tile(r, (128, 1)))
    put("tok", np.minimum(np.arange(NTT)[None] * 128 + r[:, None], TOK - 1))
    gs = np.zeros((64, 2, 128))
    for g in range(2):
        for p in range(128):
            gs[(4 * g + p // 32) * 8 + p % 8, g, p] = 1
    put("gsel", gs)
    return c


class Steps:

    def __init__(self, eng, sem):
        self.eng, self.sem, self.n = eng, sem, 0

    def after(self, ins):
        self.n += 1
        ins.then_inc(self.sem, 1)
        self.eng.wait_ge(self.sem, self.n)


def two_types(nc, ctx, name, shape):
    with nc.sbuf_tensor(name + "_low", shape, F32R) as low:
        pass
    return ctx.enter_context(nc.sbuf_tensor(name, shape, F32)), low


class Ctx:
    pass


def build(nc, io):
    with ExitStack() as ctx:
        k = Ctx()
        k.nc, k.io = nc, io

        def sb(name, shape, dt=F32):
            return ctx.enter_context(nc.sbuf_tensor(name, shape, dt))

        k.sems = []

        def sem(name):
            s = ctx.enter_context(nc.semaphore(name))
            k.sems.append(s)
            return s
        k.sem = sem

        k.const = sb("const", [128, NCONST])
        k.c = {n: k.const[:, lo:hi] for n, (lo, hi) in _C.items()}
        k.x = sb("x", [128, NTT, D])
        k.xT, k.xT_low = two_types(nc, ctx, "xT", [128, KT_D, TOK])
        k.oT, k.oT_low = two_types(nc, ctx, "oT", [128, KT_D, TOK])
        k.pt = sb("page_ids", [1, B * PAST // PAGE], I32)
        k.zrow = sb("zero_row", [128, 256])
        k.mk = sb("mask16", [128, 5 * 128], mybir.dt.bfloat16)
        k.wr = sb("w_router", [128, KT_D, E])
        k.br = sb("b_router", [128, E])
        k.ps = ctx.enter_context(nc.psum_tensor("ps", [128, 8, 512], F32))
        k.ident = k.c["ident"]

        first_in = sem("first_inputs_in")
        k.x_in = sem("x_in")
        k.sems.clear()
        dve_s, act_s, pool_s = sem("dve_step"), sem("act_step"), sem("pool_step")
        k.dve, k.act, k.pool = Steps(nc.vector, dve_s), Steps(nc.scalar, act_s), Steps(nc.gpsimd, pool_s)
        prologue(k, first_in)
        nc.all_engine_barrier(sems_to_clear=range(pool_s.num, pool_s.num + 1))
        k.pool.n = 0
        with nc.Fori(0, L) as layer:
            k.layer = layer
            with ExitStack() as phase:
                def sp(name, shape, dt=F32):
                    return phase.enter_context(nc.sbuf_tensor(name, shape, dt))
                k.z = sp("z", [128, NTT, TM])
                k.uT = sp("uT", [128, 2, TOK])
                k.vn = sp("vn", [128, NTT, 256])
                k.qT = sp("qT", [128, GQA, SEQ])
                k.qsT = sp("qsT", [128, NKV, B, GQA, TS])
                k.KT = sp("KT", [128, 2, NKV, SEQ])
                k.KTs = sp("KT_sample", [128, 2, NS])
                k.kcT = sp("kcT", [128, NKV, 32])
                k.kcsT = sp("kcT_sample", [128, NB - 32])
                k.vblk = sp("vblk", [128, NKV, GQA, HD])
                k.vcs = sp("vcs", [128, NKV, HD])
                k.gates = sp("gates", [128, NTT, 24])
                k.gsr = sp("gates_by_row", [128, 2, NKV, 3])
                with ExitStack() as early:
                    def se(name, shape, dt=F32):
                        return early.enter_context(nc.sbuf_tensor(name, shape, dt))
                    k.XT = se("XT", [128, NKV, 2, HC])
                    k.small = se("small", [128, NSMALL])
                    k.s = {n: k.small[:, lo:hi] for n, (lo, hi) in _S.items()}
                    k.spool = se("pool_state", [128, 256])
                    project(k)
                    mixers(k)
                attention(k)
            merge(k)
            experts(k)
            nums = [s.num for s in k.sems]
            assert sorted(nums) == list(range(min(nums), max(nums) + 1))
            nc.gpsimd.dma_reset(range(min(nums), max(nums) + 1))
            nc.all_engine_barrier(sems_to_clear=range(min(nums), max(nums) + 1))


def prologue(k, first_in):
    nc, io = k.nc, k.io
    with nc.Block() as block:
        @block.sync
        def _(sp):
            sp.dma_start(k.pt[:, :], io["page_table"]).then_inc(first_in, 16)
            sp.dma_start(k.xT[:, :, :], io["x0T"]).then_inc(first_in, 16)
            sp.dma_start(k.wr[:, :, :], io["w_router"].rearrange("(k p) e -> p k e", p=128)).then_inc(first_in, 16)
            sp.dma_start(k.br[:, :], io["br"]).then_inc(first_in, 16)
            sp.dma_start(k.x[:, 0:NT, :], io["xp"].rearrange("(i p) d -> p i d", p=128)).then_inc(k.x_in, 16)
            sp.dma_start(k.x[0:NS, NT, :], io["xs"]).then_inc(k.x_in, 16)
            sp.wait_ge(first_in, 16 * 4)

        @block.gpsimd
        def _(pool):
            k.pool.after(pool.memset(k.zrow[:, :], 0.0))


def project(k):
    nc, io, l, ps = k.nc, k.io, k.layer, k.ps
    sem = k.sem
    RING, HRING = 4, 3
    w_in, small_in = [sem(f"z_w_in{n}") for n in range(RING)], sem("small_in")
    x_hi, x_lo, w_hi, w_lo = sem("z_x_high"), sem("z_x_low"), sem("z_w_high"), sem("z_w_low")
    k.pages_in, k.const_in = sem("cmp_pages_in"), sem("constants_in")
    unit_done, z_done, z_out = sem("z_unit_done"), sem("z_done"), sem("z_out")
    z_cleared = sem("z_cleared")
    roped, t_done, t_out = sem("roped"), sem("t_done"), sem("t_out")
    stat_ready, rstd_ready, vn_ready, gate_tanh = (sem("vstat_ready"), sem("vrstd_ready"), sem("vn_ready"),
                                                   sem("gate_tanh"))
    k.stored = sem("stored")
    k.n_stored = 0
    with ExitStack() as ctx:
        w32, wl = two_types(nc, ctx, "z_w_ring", [128, RING, 2 * CW])
        wh = ctx.enter_context(nc.sbuf_tensor("z_w_high_part", [128, HRING, 2 * CW], F32R))
        xh = k.oT_low
        rt = ctx.enter_context(nc.sbuf_tensor("rope_tmp", [128, 4, NTT * 8 * 8], F32))
        st = ctx.enter_context(nc.sbuf_tensor("v_stats", [128, NTT, 6], F32))
        mv = ctx.enter_context(nc.sbuf_tensor("v_mv", [128, NTT, 2], F32))
        rs = ctx.enter_context(nc.sbuf_tensor("v_rstd", [128, NTT], F32))
        block = ctx.enter_context(nc.Block())
        CHUNKS = (0, 1, 2, "u", 3)
        BANKS = [4 if n == "u" else NTT for n in CHUNKS]
        FIRST = [sum(BANKS[:c]) for c in range(len(CHUNKS) + 1)]
        NRES = FIRST[-1]
        NU = 4 * len(CHUNKS)
        TH = TOK // 2
        width = [512 if CHUNKS[u // 4] == "u" else 2 * CW for u in range(NU)]

        def unit_ended(eng, u):
            if u % 4 == 3:
                eng.wait_ge(z_done, FIRST[u // 4 + 1])
            else:
                eng.wait_ge(unit_done, u // 4 * 3 + u % 4 + 1)

        @block.sync
        def _(sp):
            for u in range(NU):
                n, kk = CHUNKS[u // 4], 2 * (u % 4)
                if u >= RING:
                    unit_ended(sp, u - RING)
                src = io["wu"][l, :, kk:kk + 2, :] if n == "u" else io["wtm"][l, n, :, kk:kk + 2, :]
                sp.dma_start(w32[:, u % RING, 0:width[u]].rearrange("p (k n) -> p k n", k=2), src
                             ).then_inc(w_in[u % RING], 16)
                if u == RING:
                    sp.dma_start(k.const[:, :], io["consts"]).then_inc(k.const_in, 16)
                    for j in range(B * PAST // PAGE):
                        page = sp.value_load(k.pt[0:1, j:j + 1], min_val=0, max_val=N_POOL - 1)
                        at = (SEQ + j * PAGE) // 2
                        sp.dma_start(k.XT[:, :, :, at:at + PAGE // 2], io["cmp_pages"][l, page]).then_inc(k.pages_in, 16)
                if u == RING + 2:
                    for h in range(NKV):
                        sp.dma_start(k.XT[:, h, :, HC - CL // 2:HC], io["peT"][l]).then_inc(k.pages_in, 16)
                    sp.dma_start(k.small[:, :], io["small"][l]).then_inc(small_in, 16)
                    sp.dma_start(k.spool[0:B * KEEP, :], io["state_pool2"][l]).then_inc(small_in, 16)
            sp.dma_start(io["o_win_s"][l, :, 0:PAST - TS, :], io["state_win"][l, :, TS:PAST, :]).then_inc(k.stored, 16)
            sp.dma_start(io["o_pool_s"][l, :, 0:KEEP - TS, :], io["state_pool"][l, :, TS:KEEP, :]).then_inc(k.stored, 16)
            sp.wait_ge(roped, 2)
            for c, (op, os) in enumerate([("o_cmp_p", "o_cmp_s"), ("o_sel_p", "o_sel_s"), ("o_win_p", None)]):
                cols = slice(KV0 + 256 * c, KV0 + 256 * (c + 1))
                sp.dma_start(io[op][l].rearrange("(i p) c -> p i c", p=128), k.z[:, 0:NT, cols]).then_inc(k.stored, 16)
                if os:
                    sp.dma_start(io[os][l], k.z[0:NS, NT, cols]).then_inc(k.stored, 16)
                else:
                    for b in range(B):
                        sp.dma_start(io["o_win_s"][l, b, PAST - TS:PAST, :],
                                       k.z[b * TS:(b + 1) * TS, NT, cols]).then_inc(k.stored, 16)
            sp.wait_ge(z_out, NRES)
            sp.dma_start(io["o_pool_p"][l], k.z[128 - KEEP:128, NT - 1, A0:A0 + 256]).then_inc(k.stored, 16)
            for b in range(B):
                sp.dma_start(io["o_pool_s"][l, b, KEEP - TS:KEEP, :],
                               k.z[b * TS:(b + 1) * TS, NT, A0:A0 + 256]).then_inc(k.stored, 16)
            sp.wait_ge(vn_ready, 1)
            sp.dma_start(io["o_gmlp_s"][l], k.vn[0:NS, NT, :]).then_inc(k.stored, 16)

        @block.gpsimd
        def _(pool):
            pool.memset(k.z[64:128, NT, :], 0.0).then_inc(z_cleared, 1)
            pool.wait_ge(z_cleared, 1)
            for h in range(NKV):
                other = slice((1 - h) * HD, (2 - h) * HD)
                k.pool.after(pool.memset(k.KT[other, :, h, :], 0.0))
                k.pool.after(pool.memset(k.kcT[other, h, :], 0.0))
                k.pool.after(pool.memset(k.qsT[other, h, :, :, :], 0.0))
            pool.wait_ge(k.const_in, 16)
            for q in range(4):
                unit_ended(pool, NU - 4 + q)
                ks = slice(2 * q, 2 * q + 2)
                k.pool.after(pool.tensor_tensor(k.xT[:, ks, :], k.xT_low[:, ks, :].bitcast(F32),
                                                xh[:, ks, :].bitcast(F32), ALU.add))
            pool.wait_ge(stat_ready, 1)
            k.pool.after(pool.tensor_scalar(rs[:, :], mv[:, :, 1], EPS, None, ALU.add))
            pool.tensor_tensor(rs[:, :], rs[:, :], k.c["mhalf"], ALU.pow).then_inc(rstd_ready, 1)
        k.n_stored = 2 + 5 + B + 1 + B + 1

        @block.tensor
        def _(pe):
            def product(out, w, x, first, last):
                pe.matmul(out, w[0], x[0], start=first, stop=False)
                pe.matmul(out, w[0], x[1], start=False, stop=False)
                return pe.matmul(out, w[1], x[0], start=False, stop=last)

            for u in range(NU):
                chunk, q = u // 4, u % 4
                pe.wait_ge(w_lo, u + 1)
                if chunk == 0:
                    pe.wait_ge(x_lo, q + 1)
                for r in range(BANKS[chunk]):
                    res = FIRST[chunk] + r
                    if q == 0 and res >= 8:
                        pe.wait_ge(z_out, res - 7)
                    for a in range(2):
                        kk = 2 * q + a

                        def x(cols):
                            return xh[:, kk, cols], k.xT_low[:, kk, cols]

                        def w(cols):
                            return wh[:, u % HRING, cols], wl[:, u % RING, cols]
                        if CHUNKS[chunk] == "u":
                            m, half = r // 2, r % 2
                            at = a * 256 + m * 128
                            last = product(ps[:, res % 8, 0:TH], w(slice(at, at + 128)), x(slice(half * TH, (half + 1) * TH)),
                                           kk == 0, kk == KT_D - 1)
                        else:
                            rows = TILES[r]
                            last = product(ps[0:rows, res % 8, 0:CW], x(slice(r * 128, r * 128 + rows)),
                                           w(slice(a * CW, (a + 1) * CW)), kk == 0, kk == KT_D - 1)
                    if q == 3:
                        last.then_inc(z_done, 1)
                if q < 3:
                    last.then_inc(unit_done, 1)
            pe.wait_ge(k.const_in, 16)
            pe.wait_ge(z_out, NRES)
            pe.wait_ge(roped, 1)
            for u in range(4 + 4):
                if u == 4:
                    pe.wait_ge(roped, 2)
                for i in range(NT):
                    if u < 6:
                        col = Q0 + u * 128 if u < 4 else KV0 + 256 * (u - 3)
                        last = pe.transpose(ps[:, u, i * 128:(i + 1) * 128], k.z[:, i, col:col + 128], k.ident)
                        continue
                    for h in range(NKV):
                        col = KV0 + 128 * (u - 6) + HD * h
                        for odd in range(2):
                            last = pe.matmul(ps[odd * HD:(odd + 1) * HD, u, h * 256 + i * 64:h * 256 + (i + 1) * 64],
                                             k.z[:, i, col:col + HD], k.ident[:, odd:128:2], start=True, stop=True)
                last.then_inc(t_done, 1)
            pe.wait_ge(t_out, 2)
            for u in range(4):
                src = k.z[0:NS, NT, Q0 + u * 128:Q0 + (u + 1) * 128]
                last = pe.transpose(ps[:, 0, u * NS:(u + 1) * NS], src, k.ident[0:NS, 0:NS])
            last.then_inc(t_done, 1)
            for u in range(2):
                col = KV0 + 256 * (u + 1)
                last = pe.transpose(ps[:, 1, u * NS:(u + 1) * NS], k.z[0:NS, NT, col:col + 128], k.ident[0:NS, 0:NS])
            last.then_inc(t_done, 1)

        @block.scalar
        def _(act):
            act.wait_ge(z_cleared, 1)

            def x_high(q):
                act.copy(xh[:, 2 * q:2 * q + 2, :], k.xT[:, 2 * q:2 * q + 2, :]).then_inc(x_hi, 1)

            def w_high(u):
                act.wait_ge(w_in[u % RING], 16 * (u // RING + 1))
                if u >= HRING:
                    unit_ended(act, u - HRING)
                act.copy(wh[:, u % HRING, 0:width[u]], w32[:, u % RING, 0:width[u]]).then_inc(w_hi, 1)

            def results(chunk):
                for r in range(BANKS[chunk]):
                    res, n = FIRST[chunk] + r, CHUNKS[chunk]
                    act.wait_ge(z_done, res + 1)
                    if n == "u":
                        dst, rows, cols = k.uT[:, r // 2, r % 2 * TH:(r % 2 + 1) * TH], 128, TH
                    else:
                        dst, rows, cols = k.z[0:TILES[r], r, n * CW:(n + 1) * CW], TILES[r], CW
                    act.copy(dst, ps[0:rows, res % 8, 0:cols]).then_inc(z_out, 1)
            x_high(0)
            w_high(0)
            x_high(1)
            w_high(1)
            x_high(2)
            x_high(3)
            for u in range(NU):
                if u + 2 < NU:
                    w_high(u + 2)
                if u % 4 == 3:
                    results(u // 4)
            act.wait_ge(z_out, NRES)
            act.activation(k.gates[:, :, :], k.z[:, :, G0:G0 + 24], ACT.Tanh, scale=0.5).then_inc(gate_tanh, 1)
            for u in range(8):
                act.wait_ge(t_done, u + 1)
                if u < 4:
                    act.activation(k.qT[:, u, :], ps[:, u, :], ACT.Copy, scale=HD ** -0.5).then_inc(t_out, 1)
                elif u < 6:
                    for h in range(NKV):
                        hs = slice(h * HD, (h + 1) * HD)
                        last = act.copy(k.KT[hs, u - 4, h, :], ps[hs, u, :])
                    last.then_inc(t_out, 1)
                else:
                    act.copy(k.XT[:, :, u - 6, 0:SEQ // 2], ps[:, u, :].rearrange("p (h t) -> p h t", h=2)).then_inc(t_out, 1)
            act.wait_ge(t_done, 9)
            for h in range(NKV):
                hs = slice(h * HD, (h + 1) * HD)
                for i in range(GQA):
                    act.activation(k.qsT[hs, h, :, i, :], ps[hs, 0, i * NS:(i + 1) * NS].rearrange("p (b t) -> p b t", b=B),
                                   ACT.Copy, scale=HD ** -0.5)
            act.wait_ge(t_done, 10)
            act.copy(k.KTs[:, :, :], ps[:, 1, 0:2 * NS].rearrange("p (u t) -> p u t", u=2))

        @block.vector
        def _(dve):
            def rope(base, n, step):
                def half(o):
                    return k.z[:, :, base:base + n * HD].rearrange("p i (h d) -> p i h d", d=HD)[:, :, :, o:o + 8]
                cos = k.c["cos"].rearrange("p (i d) -> p i d", i=NTT).unsqueeze(2).broadcast_to([128, NTT, n, 8])
                sin = k.c["sin"].rearrange("p (i d) -> p i d", i=NTT).unsqueeze(2).broadcast_to([128, NTT, n, 8])
                t = [rt[:, a, 0:NTT * n * 8].rearrange("p (i h d) -> p i h d", i=NTT, h=n) for a in range(4)]
                dve.tensor_tensor(t[0], half(0), cos, ALU.mult)
                dve.tensor_tensor(t[1], half(8), sin, ALU.mult)
                dve.tensor_tensor(t[2], half(8), cos, ALU.mult)
                k.dve.after(dve.tensor_tensor(t[3], half(0), sin, ALU.mult))
                dve.tensor_tensor(half(0), t[0], t[1], ALU.subtract)
                return dve.tensor_tensor(half(8), t[2], t[3], ALU.add)

            def rest(low, src, high):
                return dve.tensor_tensor(low, src, high.bitcast(F32), ALU.subtract)

            def x_low(q):
                ks = slice(2 * q, 2 * q + 2)
                dve.wait_ge(x_hi, q + 1)
                rest(k.xT_low[:, ks, :], k.xT[:, ks, :], xh[:, ks, :]).then_inc(x_lo, 1)

            def w_low(u):
                dve.wait_ge(w_hi, u + 1)
                rest(wl[:, u % RING, 0:width[u]], w32[:, u % RING, 0:width[u]],
                     wh[:, u % HRING, 0:width[u]]).then_inc(w_lo, 1)
            x_low(0)
            w_low(0)
            x_low(1)
            w_low(1)
            x_low(2)
            x_low(3)
            for u in range(2, NU):
                w_low(u)
                if u == 10:
                    dve.wait_ge(k.const_in, 16)
                    dve.wait_ge(z_out, FIRST[2])
                    rope(Q0, NH, HD).then_inc(roped, 1)
                    dve.wait_ge(roped, 1)
                if u == 14:
                    dve.wait_ge(z_out, FIRST[3])
                    for c in range(3):
                        last = rope(KV0 + 256 * c, NKV, HD)
                        if c < 2:
                            k.dve.after(last)
                    last.then_inc(roped, 1)
            dve.wait_ge(z_out, NRES)
            for i in range(NTT):
                last = dve.bn_stats(st[:, i, :], k.z[:, i, V0:V0 + 256])
            k.dve.after(last)
            for i in range(NTT):
                last = dve.bn_aggr(mv[:, i, :], st[:, i, :])
            last.then_inc(stat_ready, 1)
            dve.wait_ge(rstd_ready, 1)
            for i in range(NTT):
                last = dve.tensor_scalar(k.vn[:, i, :], k.z[:, i, V0:V0 + 256], mv[:, i, 0:1], rs[:, i:i + 1],
                                         ALU.subtract, ALU.mult)
            k.dve.after(last)
            dve.wait_ge(small_in, 32)
            k.dve.after(dve.tensor_tensor(k.vn[:, :, :], k.vn[:, :, :],
                                          k.s["vg"].unsqueeze(1).broadcast_to([128, NTT, 256]), ALU.mult))
            dve.tensor_tensor(k.vn[:, :, :], k.vn[:, :, :],
                              k.s["vb"].unsqueeze(1).broadcast_to([128, NTT, 256]), ALU.add).then_inc(vn_ready, 1)
            dve.wait_ge(gate_tanh, 1)
            dve.tensor_scalar(k.gates[:, :, :], k.gates[:, :, :], 0.5, 0.5, ALU.mult, ALU.add)


def mixers(k):
    nc, io, l, ps, c = k.nc, k.io, k.layer, k.ps, k.c
    sem = k.sem
    w1_in, masked = sem("w1_in"), sem("gmlp_masked")
    d_done, d_out, mix_done, mix_out, y_done = (sem("pool_d_done"), sem("pool_d_out"), sem("mix_done"),
                                                sem("mix_out"), sem("pool_y_done"))
    u_done, u1_out, x_ready, th_ready, hid_ready = (sem("cmp_u_done"), sem("cmp_u1_out"), sem("cmp_x_ready"),
                                                    sem("cmp_tanh_ready"), sem("cmp_hid_ready"))
    gr_done, kc_done = sem("gate_rows_done"), sem("kc_done")
    with ExitStack() as ctx:
        def sb(name, shape):
            return ctx.enter_context(nc.sbuf_tensor(name, shape, F32))
        w1 = sb("w1", [128, 2, CS, HID])
        dT = k.oT[:, 0:2, :]
        wmT = sb("wmT", [128, 4, 128])
        wmsT = sb("wmsT", [128, 4, NS])
        u1 = sb("u1", [128, 4, UW])
        bias = sb("cmp_bias", [128, 4])
        spare = k.oT[:, 4:8, :].rearrange("p a t -> p (a t)")
        xh, th, hid = (spare[:, n * 4 * NB:(n + 1) * 4 * NB].rearrange("p (n m) -> p n m", n=4) for n in range(3))
        hrep = spare[:, 12 * NB:12 * NB + NKV * 4 * 32].rearrange("p (h i c) -> p h i c", h=NKV, i=4)
        gt = sb("gate_tmp", [128, 2, NKV, 3, 4])
        block = ctx.enter_context(nc.Block())
        BANK = [[0, 1], [6, 7]]

        @block.sync
        def _(sp):
            sp.dma_start(w1[:, :, :, :], io["w1"][l]).then_inc(w1_in, 16)

        @block.tensor
        def _(pe):
            for g in range(4):
                p, half = g // 2, slice(64 * (g % 2), 64 * (g % 2) + 64)
                col = slice(A0 + 64 * g, A0 + 64 * g + 64)
                for i in range(NT):
                    out = ps[half, p, i * 128:(i + 1) * 128]
                    cur = c["bcur0" if i == 0 else "bcur"][:, g * 128:(g + 1) * 128]
                    pe.matmul(out, k.z[:, i, col], cur, start=True, stop=(i == 0))
                    if i:
                        pe.matmul(out, k.z[:, i - 1, col], c["bprev"][:, g * 128:(g + 1) * 128], start=False, stop=True)
                out = ps[half, 2, p * 64:p * 64 + 64]
                pe.matmul(out, k.spool[0:B * KEEP, 64 * g:64 * g + 64], c["bst"][0:B * KEEP, g * 64:g * 64 + 64],
                          start=True, stop=False)
                last = pe.matmul(out, k.z[0:NS, NT, col], c["bnew"][0:NS, g * 64:g * 64 + 64], start=False, stop=True)
            last.then_inc(d_done, 1)
            pe.wait_ge(masked, 1)
            for g in range(4):
                p, half = g // 2, slice(64 * (g % 2), 64 * (g % 2) + 64)
                for i in range(NT):
                    pe.matmul(ps[half, 3 + p, i * 128:(i + 1) * 128], k.vn[:, i, 64 * g:64 * g + 64], wmT[:, g, :],
                              start=True, stop=True)
                last = pe.matmul(ps[half, 5, p * 64:p * 64 + 64], k.vn[0:NS, NT, 64 * g:64 * g + 64],
                                 wmsT[0:NS, g, :], start=True, stop=True)
            last.then_inc(mix_done, 1)
            pe.wait_ge(d_out, 1)
            pe.wait_ge(w1_in, 16)
            pe.wait_ge(k.pages_in, 16 * (B * PAST // PAGE + NKV))
            for kv in range(2):
                for a in range(2):
                    for j in range(CS // 2):
                        last = pe.matmul(ps[:, BANK[kv][a], 0:2 * UW].rearrange("p (h m) -> p h m", h=2),
                                         w1[:, kv, a * CS // 2 + j, :], k.XT[:, :, kv, j:HC:CS // 2],
                                         start=(j == 0), stop=(j == CS // 2 - 1))
                last.then_inc(u_done, 1)
            pe.wait_ge(mix_out, 1)
            for p in range(2):
                w = k.s["poolw"][:, p * 128:(p + 1) * 128]
                pe.matmul(ps[:, 3 + p, :], w, dT[:, p, 0:SEQ], start=True, stop=True)
                last = pe.matmul(ps[:, 2, 128 + p * 64:192 + p * 64], w, dT[:, p, SEQ:TOK], start=True, stop=True)
            last.then_inc(y_done, 1)
            for g in range(2):
                last = pe.matmul(ps[:, 5, 256 + 24 * g:280 + 24 * g], c["gsel"][0:NS, g * 128:(g + 1) * 128],
                                 k.gates[0:NS, NT, :], start=True, stop=True)
            last.then_inc(gr_done, 1)
            pe.wait_ge(hid_ready, 1)
            for h in range(NKV):
                pe.matmul(ps[h * HD:(h + 1) * HD, 6, 0:NB], k.s["w2"][:, 0:64], hid[:, h, :], start=True, stop=True)
            pe.wait_ge(hid_ready, 2)
            for h in range(NKV):
                pe.matmul(ps[:, 7, h * HD:(h + 1) * HD], hrep[:, h, :, :].rearrange("p i c -> p (i c)"),
                          k.s["w2"][:, 64:128], start=True, stop=True)
                last = pe.matmul(ps[:, 7, 128 + h * HD:192 + h * HD], hid[:, 2 + h, 32:NB], k.s["w2"][:, 64:128],
                                 start=True, stop=True)
            last.then_inc(kc_done, 1)

        @block.scalar
        def _(act):
            for kv in range(2):
                act.wait_ge(u_done, kv + 1)
                act.copy(u1[:, 2 * kv:2 * kv + 2, :], ps[:, BANK[kv][1], 0:2 * UW].rearrange("p (h m) -> p h m", h=2)
                         ).then_inc(u1_out, 1)
            act.wait_ge(x_ready, 1)
            act.activation(th[:, :, :], hid[:, :, :], ACT.Tanh, scale=0.7978845608028654).then_inc(th_ready, 1)
            act.wait_ge(kc_done, 1)
            for h in range(NKV):
                hs = slice(h * HD, (h + 1) * HD)
                act.activation(k.kcT[hs, h, :], ps[hs, 6, 0:32], ACT.Copy, scale=0.5)
            act.activation(k.kcsT[:, :], ps[:, 6, 32:NB], ACT.Copy, scale=0.5)

        @block.vector
        def _(dve):
            step = k.dve.after
            s = k.s
            dve.tensor_tensor(wmT[:, :, :], s["wsT"].rearrange("p (g t) -> p g t", g=4),
                              c["gm"].unsqueeze(1).broadcast_to([128, 4, 128]), ALU.mult)
            dve.tensor_tensor(wmsT[0:NS, :, :].rearrange("p g (b t) -> p g b t", b=B),
                              s["wss"][0:NS].rearrange("p (g t) -> p g t", g=4).unsqueeze(2).broadcast_to([NS, 4, B, TS]),
                              c["gms"][0:NS].rearrange("p (b t) -> p b t", b=B).unsqueeze(1).broadcast_to([NS, 4, B, TS]),
                              ALU.mult).then_inc(masked, 1)
            dve.tensor_copy(k.mk[:, 0:128], k.ident)
            dve.tensor_copy(k.mk[:, 128:256], c["diag"])
            dve.tensor_copy(k.mk[:, 256:512], c["scneg"])
            dve.tensor_copy(k.mk[:, 512:640], c["newneg"])
            dve.wait_ge(d_done, 1)
            dve.tensor_copy(dT[:, :, 0:SEQ], ps[:, 0:2, :])
            dve.tensor_copy(dT[:, :, SEQ:TOK], ps[:, 2, 0:128].rearrange("p (a t) -> p a t", a=2)).then_inc(d_out, 1)
            dve.wait_ge(mix_done, 1)
            bs = s["bsT"].rearrange("p (a t) -> p a t", a=2)
            for p in range(2):
                dve.tensor_tensor(k.oT[:, 2 + p, 0:SEQ].rearrange("p (i t) -> p i t", i=NT),
                                  ps[:, 3 + p, :].rearrange("p (i t) -> p i t", i=NT),
                                  bs[:, p, :].unsqueeze(1).broadcast_to([128, NT, 128]), ALU.add)
            for p in range(2):
                last = dve.tensor_tensor(k.oT[:, 2 + p, SEQ:TOK].rearrange("p (b t) -> p b t", b=B),
                                         ps[:, 5, 64 * p:64 * p + 64].rearrange("p (b t) -> p b t", b=B),
                                         bs[:, p, 0:TS].unsqueeze(1).broadcast_to([128, B, TS]), ALU.add)
            last.then_inc(mix_out, 1)
            dve.wait_ge(mix_out, 1)
            dve.tensor_tensor(k.oT[:, 2:4, :], k.oT[:, 2:4, :], k.uT[:, :, :], ALU.mult)

            for n in range(4):
                kv, h = n // 2, n % 2
                dve.wait_ge(u1_out, kv + 1)
                U = ps[:, BANK[kv][0], h * UW:(h + 1) * UW]
                step(dve.scalar_tensor_tensor(bias[:, n:n + 1], U[:, NB:NB + 1], s["b1"][:, kv:kv + 1],
                                              u1[:, n, NB + 1:NB + 2], ALU.add, ALU.add))
                last = dve.scalar_tensor_tensor(xh[:, n, :], U[:, 0:NB], bias[:, n:n + 1], u1[:, n, 1:NB + 1],
                                                ALU.add, ALU.add)
            step(last)
            step(dve.tensor_tensor(th[:, :, :], xh[:, :, :], xh[:, :, :], ALU.mult))
            step(dve.tensor_scalar(th[:, :, :], th[:, :, :], 0.044715, 1.0, ALU.mult, ALU.add))
            dve.tensor_tensor(hid[:, :, :], th[:, :, :], xh[:, :, :], ALU.mult).then_inc(x_ready, 1)
            dve.wait_ge(th_ready, 1)
            dve.scalar_tensor_tensor(hid[:, :, :], th[:, :, :], 1.0, xh[:, :, :], ALU.add, ALU.mult).then_inc(hid_ready, 1)
            dve.wait_ge(hid_ready, 1)
            dve.tensor_copy(hrep[:, :, :, :], hid[:, 2:4, 0:32].unsqueeze(2).broadcast_to([128, NKV, 4, 32])).then_inc(hid_ready, 1)
            dve.wait_ge(y_done, 1)
            for p in range(2):
                sc = s["pscale"][:, p:p + 1]
                dve.tensor_scalar(k.oT[:, p, 0:SEQ], ps[:, 3 + p, :], sc, None, ALU.mult)
                dve.tensor_scalar(k.oT[:, p, SEQ:TOK], ps[:, 2, 128 + 64 * p:192 + 64 * p], sc, None, ALU.mult)
            dve.wait_ge(gr_done, 1)
            for g in range(2):
                for h in range(NKV):
                    rows = ps[:, 5, 256 + 24 * g + 12 * h:268 + 24 * g + 12 * h].rearrange("p (i c) -> p c i", i=4)
                    last = dve.tensor_tensor(gt[:, g, h, :, :], rows, c["rowhead"].unsqueeze(1).broadcast_to([128, 3, 4]),
                                             ALU.mult)
            step(last)
            dve.tensor_reduce(k.gsr[:, :, :, :].rearrange("p g h c -> p (g h c)"),
                              gt[:, :, :, :, :].rearrange("p g h c i -> p (g h c) i"), AX.X, ALU.add)
            dve.wait_ge(kc_done, 1)
            dve.tensor_scalar(k.vcs[:, :, :], ps[:, 7, 128:256].rearrange("p (h d) -> p h d", h=2), 0.5, None, ALU.mult)
            for h in range(NKV):
                dve.scalar_tensor_tensor(k.vblk[:, h, :, :],
                                         ps[:, 7, h * HD:(h + 1) * HD].unsqueeze(1).broadcast_to([128, 4, HD]), 0.5,
                                         c["blk"].unsqueeze(2).broadcast_to([128, 4, HD]), ALU.mult, ALU.mult)


def attention(k):
    nc, io, l, ps, c = k.nc, k.io, k.layer, k.ps, k.c
    sem = k.sem
    LAG_T, LAG_V = 2, 3
    units = []
    for t in range(NT):
        units += [("kv", t, kvh, i, br) for kvh in range(NKV) for i in range(GQA) for br in range(2)]
        units.append(("cmp", t, 0, 0, 0))
    for g in range(2):
        for kvh in range(NKV):
            units.append(("scmp", g, kvh, 0, 0))
            units += [("skv", g, kvh, 0, br) for br in range(2)]
    NU = len(units)
    group = [u[1] + (NT if u[0][0] == "s" else 0) for u in units]
    scored = [n for n in range(NU) if units[n][0] != "cmp"]
    order = {n: m for m, n in enumerate(scored)}
    last_of = [max(n for n in range(NU) if group[n] == gr) for gr in range(NT + 2)]

    def on_act(n):
        return n % 2 == 1

    def copied(eng, n):
        if on_act(n):
            eng.wait_ge(pt_by_act, len([m for m in range(n + 1) if on_act(m)]))
        else:
            eng.wait_ge(pt_by_dve, len([m for m in range(n + 1) if not on_act(m)]))

    sel_in, win_in = sem("sel_pages_in"), sem("win_rows_in")
    k.rows_cleared = sem("expert_rows_cleared")
    s_done, masked, p_ready = sem("score_done"), sem("score_masked"), sem("prob_ready")
    cs_done, cs_taken, cs_ready, cp_exp, cp_ready = (sem("cmp_score_done"), sem("cmp_score_taken"), sem("cmp_score_ready"),
                                                     sem("cmp_exp_done"), sem("cmp_prob_ready"))
    weighed = sem("branches_weighed")
    pt_done, pt_by_act, pt_by_dve, av_done = sem("pt_done"), sem("pt_by_act"), sem("pt_by_dve"), sem("av_done")
    o_out, ot_done = sem("o_out"), sem("ot_done")
    with ExitStack() as ctx:
        def sb(name, shape):
            return ctx.enter_context(nc.sbuf_tensor(name, shape, F32))
        sel = sb("sel_pages", [128, B, 2, 256])
        win = sb("win_rows", [128, B, 2, 256])
        P = sb("probs", [128, 3, 512])
        PT = sb("probsT", [128, 2, 512])
        cp = sb("cmp_probs", [128, NT, NH, 32])
        cpf = cp[:, :, :, :].rearrange("p t h c -> p t (h c)")
        mx = sb("row_max", [128, 3])
        mxc = sb("cmp_max", [128, NT, NH])
        cden = sb("cmp_den", [128, NT, NH])
        den = sb("den", [128, 2, 3, 8])
        wgt = sb("wgt", [128, 2, 3, 8])
        acc = sb("acc", [128, 3, 512])
        otm = sb("otm", [128, NT, 512])
        osm = sb("osm", [128, 2, 128])
        block = ctx.enter_context(nc.Block())
        past = (sel, win)

        def vcol(br, kvh):
            return slice(KV0 + 256 * (br + 1) + 128 + kvh * HD, KV0 + 256 * (br + 1) + 128 + (kvh + 1) * HD)

        @block.sync
        def _(sp):
            for j in range(B * PAST // PAGE):
                page = sp.value_load(k.pt[0:1, j:j + 1], min_val=0, max_val=N_POOL - 1)
                sp.dma_start(sel[:, j // 2, j % 2, :], io["sel_pages"][l, page]).then_inc(sel_in, 16)
            sp.dma_start(win[:, :, :, :], io["win_rows"][l]).then_inc(win_in, 16)
            with sp.Fori(0, l * (MAXCH // 2 - 1) + 1):
                sp.sem_inc(k.rows_cleared, 16)
            with sp.Fori(l * (MAXCH // 2 - 1), MAXCH // 2) as p:
                sp.dma_start(io["ys"][bass.ds(p * 256, 256), :].rearrange("(p c) (q e) -> p (c q) e", p=128, e=256),
                             k.zrow[:, :].unsqueeze(1).broadcast_to([128, 8, 256])).then_inc(k.rows_cleared, 16)

        @block.tensor
        def _(pe):
            def scores(n):
                kind, t, kvh, i, br = units[n]
                if kind == "cmp":
                    return
                m = order[n]
                bank = m % 3
                if m >= 3:
                    pe.wait_ge(p_ready, m - 2)
                lo, hi, mcol = {"kv": (t * 128, (t + 1) * 128, 128), "scmp": (0, 128, 256 + 128 * t),
                             "skv": (256, 320, 512 + 64 * t)}[kind]
                pe.matmul(ps[:, bank, lo:hi], k.mk[:, 0:128], k.mk[:, mcol:mcol + hi - lo], start=True,
                          stop=False, skip_group_check=True)
                if kind == "kv":
                    last = pe.matmul(ps[:, bank, 0:(t + 1) * 128], k.qT[:, i, t * 128:(t + 1) * 128],
                                     k.KT[:, br, kvh, 0:(t + 1) * 128], start=False, stop=True,
                                     skip_group_check=True)
                elif kind == "scmp":
                    q = k.qsT[:, kvh, 4 * t:4 * t + 4, :, :].rearrange("p b i t -> p (b i t)")
                    last = pe.matmul(ps[:, bank, 0:128], q, k.kcsT[:, :], start=False, stop=True,
                                     skip_group_check=True)
                else:
                    pe.wait_ge((sel_in, win_in)[br], 16 * (B * PAST // PAGE, 1)[br])
                    q = k.qsT[:, kvh, 4 * t:4 * t + 4, :, :].rearrange("p b i t -> p (b i t)")
                    pe.matmul(ps[:, bank, 256:320], q, k.KTs[:, br, :], start=False, stop=True,
                              skip_group_check=True)
                    for b in range(4):
                        q = k.qsT[:, kvh, 4 * t + b, :, :].rearrange("p i t -> p (i t)")
                        last = pe.matmul(ps[32 * b:32 * b + 32, bank, 0:256].rearrange("p (a t) -> p a t", a=2), q,
                                         past[br][:, 4 * t + b, :, 0:128], start=True, stop=True)
                last.then_inc(s_done, 1)

            def transposes(n):
                kind, t, kvh, i, br = units[n]
                bank = 3 + n % 2
                if kind == "cmp":
                    pe.wait_ge(cp_ready, 1)
                    src = cpf[:, t, :]
                else:
                    pe.wait_ge(p_ready, order[n] + 1)
                    src = P[:, order[n] % 3, :]
                if n >= 2:
                    copied(pe, n - 2)
                w = {"cmp": 2, "kv": t + 1, "scmp": 1, "skv": 2}[kind]
                for a in range(w):
                    last = pe.transpose(ps[:, bank, a * 128:(a + 1) * 128], src[:, a * 128:(a + 1) * 128], k.ident)
                if kind == "skv":
                    last = pe.transpose(ps[0:64, bank, 256:384], src[:, 256:320], k.ident)
                last.then_inc(pt_done, 1)

            def values(n):
                kind, t, kvh, i, br = units[n]
                copied(pe, n)
                if group[n] and (n == 0 or group[n] != group[n - 1]):
                    pe.wait_ge(weighed, 3 * group[n])
                if n == 0:
                    pe.wait_ge(cs_taken, 1)
                pt = PT[:, n % 2, :]
                if kind == "cmp":
                    for h in range(NKV):
                        last = pe.matmul(ps[:, 5, h * 256:(h + 1) * 256], pt[:, h * 128:(h + 1) * 128],
                                         k.vblk[:, h, :, :].rearrange("p i d -> p (i d)"), start=True, stop=True)
                elif kind == "kv":
                    out = ps[:, 6 + br, (kvh * 4 + i) * HD:(kvh * 4 + i + 1) * HD]
                    for a in range(t + 1):
                        last = pe.matmul(out, pt[:, a * 128:(a + 1) * 128], k.z[:, a, vcol(br, kvh)],
                                         start=(a == 0), stop=(a == t))
                elif kind == "scmp":
                    last = pe.matmul(ps[:, 5, kvh * HD:(kvh + 1) * HD], pt[:, 0:128], k.vcs[:, kvh, :],
                                     start=True, stop=True)
                else:
                    pe.matmul(ps[:, 6 + br, kvh * HD:(kvh + 1) * HD], pt[0:NS, 256:384], k.z[0:NS, NT, vcol(br, kvh)],
                              start=True, stop=False, skip_group_check=True)
                    for b in range(4):
                        for a in range(2):
                            last = pe.matmul(ps[32 * b:32 * b + 32, 6 + br, kvh * HD:(kvh + 1) * HD],
                                             pt[:, a * 128 + 32 * b:a * 128 + 32 * b + 32],
                                             past[br][:, 4 * t + b, a, 128 + kvh * HD:128 + (kvh + 1) * HD],
                                             start=False, stop=(a == 1), skip_group_check=True)
                last.then_inc(av_done, 1)

            for t in range(NT):
                out = ps[:, 6 + t // 2, t % 2 * 256:t % 2 * 256 + 256].rearrange("p (h i c) -> p i h c", h=NKV, i=GQA)
                for i in range(GQA):
                    last = pe.matmul(out[:, i, :, :], k.qT[:, i, t * 128:(t + 1) * 128], k.kcT[:, :, :],
                                     start=True, stop=True)
            last.then_inc(cs_done, 1)
            for n in range(NU + LAG_V):
                if n < NU:
                    scores(n)
                if 0 <= n - LAG_T < NU:
                    transposes(n - LAG_T)
                if n >= LAG_V:
                    values(n - LAG_V)
            pe.wait_ge(o_out, NT + 2)
            for i in range(GQA):
                for t in range(NT):
                    last = pe.transpose(ps[:, i, t * 128:(t + 1) * 128], otm[:, t, i * 128:(i + 1) * 128], k.ident)
                last.then_inc(ot_done, 1)
            for g in range(2):
                last = pe.transpose(ps[:, 4, g * 128:(g + 1) * 128], osm[:, g, :], k.ident)
            last.then_inc(ot_done, 1)

        def copy_probs(eng, copy, n, done):
            kind, t, kvh, i, br = units[n]
            eng.wait_ge(pt_done, n + 1)
            if n >= 2:
                eng.wait_ge(av_done, n - 1)
            w = {"cmp": 256, "kv": (t + 1) * 128, "scmp": 128, "skv": 256}[kind]
            last = copy(PT[:, n % 2, 0:w], ps[:, 3 + n % 2, 0:w])
            if kind == "skv":
                last = copy(PT[0:NS, n % 2, 256:384], ps[0:NS, 3 + n % 2, 256:384])
            last.then_inc(done, 1)

        @block.gpsimd
        def _(pool):
            for gr in range(NT + 2):
                n = (NH if gr < NT else NKV) * HD
                a = [acc[:, b, 0:n] for b in range(3)]
                pool.wait_ge(weighed, 3 * gr + 2)
                k.pool.after(pool.tensor_tensor(a[0], a[0], a[1], ALU.add))
                pool.wait_ge(weighed, 3 * gr + 3)
                if gr < NT:
                    a = [x.rearrange("p (h i d) -> p h i d", h=2, i=4) for x in a]
                    dst = otm[:, gr, :].rearrange("p (i h d) -> p h i d", i=4, h=2)
                else:
                    dst = osm[:, gr - NT, :]
                pool.tensor_tensor(dst, a[0], a[2], ALU.add).then_inc(o_out, 1)

        @block.scalar
        def _(act):
            def probs(n):
                kind, t, kvh, i, br = units[n]
                if kind == "cmp":
                    return
                m = order[n]
                act.wait_ge(masked, m + 1)
                if m >= 3:
                    act.wait_ge(pt_done, scored[m - 3] + 1)
                w = {"kv": (t + 1) * 128, "scmp": 128, "skv": 320}[kind]
                g = group[n] % 2
                if kind == "kv":
                    d = den[:, g, br + 1, kvh * 4 + i:kvh * 4 + i + 1]
                else:
                    d = den[:, g, (0 if kind == "scmp" else br + 1), kvh:kvh + 1]
                act.activation(P[:, m % 3, 0:w], ps[:, m % 3, 0:w], ACT.Exp, bias=mx[:, m % 3:m % 3 + 1],
                               accum_out=d).then_inc(p_ready, 1)

            for n in range(NU + 2):
                if n == 3:
                    act.wait_ge(cs_ready, 1)
                    act.activation(cp[:, :, :, :], cp[:, :, :, :], ACT.Exp).then_inc(cp_exp, 1)
                if n < NU:
                    probs(n)
                if n >= 2 and on_act(n - 2):
                    copy_probs(act, act.copy, n - 2, pt_by_act)
            for i in range(GQA):
                act.wait_ge(ot_done, i + 1)
                act.copy(k.oT[:, 4 + i, 0:SEQ], ps[:, i, :])

        @block.vector
        def _(dve):
            step = k.dve.after

            def cmp_softmax(n):
                neg = c["cneg"].rearrange("p (t c) -> p t c", t=NT).unsqueeze(2).broadcast_to([128, NT, NH, 32])
                ok = c["cm"].rearrange("p (t c) -> p t c", t=NT).unsqueeze(2).broadcast_to([128, NT, NH, 32])
                if n == 0:
                    dve.wait_ge(cs_done, 1)
                    dve.tensor_tensor(cp[:, :, :, :], ps[:, 6:8, :].rearrange("p b (t h c) -> p (b t) h c", t=2, h=NH),
                                      neg, ALU.add).then_inc(cs_taken, 1)
                if n == 1:
                    dve.wait_ge(cs_taken, 1)
                    step(dve.tensor_reduce(mxc[:, :, :], cp[:, :, :, :], AX.X, ALU.max))
                    dve.tensor_tensor(cp[:, :, :, :], cp[:, :, :, :], mxc[:, :, :].unsqueeze(3).broadcast_to([128, NT, NH, 32]),
                                      ALU.subtract).then_inc(cs_ready, 1)
                if n == 6:
                    dve.wait_ge(cp_exp, 1)
                    dve.tensor_tensor(cp[:, :, :, :], cp[:, :, :, :], ok, ALU.mult).then_inc(cp_ready, 1)
                if n == 7:
                    dve.wait_ge(cp_ready, 1)
                    step(dve.tensor_reduce(cden[:, :, :], cp[:, :, :, :], AX.X, ALU.add))

            def mask(n):
                kind, t, kvh, i, br = units[n]
                if kind == "cmp":
                    return
                m = order[n]
                dve.wait_ge(s_done, m + 1)
                w = {"kv": (t + 1) * 128, "scmp": 128, "skv": 320}[kind]
                if m >= 3:
                    dve.wait_ge(p_ready, m - 2)
                dve.tensor_reduce(mx[:, m % 3:m % 3 + 1], ps[:, m % 3, 0:w], AX.X, ALU.max, negate=True).then_inc(masked, 1)

            def shapes(gr):
                return (NH, k.gates[:, gr, :].rearrange("p (h c) -> p c h", c=3)) if gr < NT else \
                       (NKV, k.gsr[:, gr - NT, :, :].rearrange("p h c -> p c h"))

            def weights(gr):
                n, gates = shapes(gr)
                dve.wait_ge(p_ready, max(order[m] for m in range(last_of[gr] + 1) if m in order) + 1)
                w = wgt[:, gr % 2, :, 0:n]
                first = 1 if gr < NT else 0
                if gr < NT:
                    step(dve.tensor_scalar(w[:, 0, :], cden[:, gr, :], 1e-30, None, ALU.max))
                step(dve.tensor_scalar(w[:, first:3, :], den[:, gr % 2, first:3, 0:n], 1e-30, None, ALU.max))
                step(dve.reciprocal(w, w))
                step(dve.tensor_tensor(w, w, gates, ALU.mult))

            def weigh(gr):
                dve.wait_ge(av_done, last_of[gr] + 1)
                if gr:
                    dve.wait_ge(o_out, gr)
                n, _ = shapes(gr)
                for b in range(3):
                    dve.tensor_tensor(acc[:, b, 0:n * HD].rearrange("p (h d) -> p h d", d=HD),
                                      ps[:, 5 + b, 0:n * HD].rearrange("p (h d) -> p h d", d=HD),
                                      wgt[:, gr % 2, b, 0:n].unsqueeze(2).broadcast_to([128, n, HD]), ALU.mult
                                      ).then_inc(weighed, 1)

            for n in range(NU + LAG_V + 1):
                cmp_softmax(n)
                if n < NU:
                    mask(n)
                if 2 <= n < NU + 2 and not on_act(n - 2):
                    copy_probs(dve, dve.tensor_copy, n - 2, pt_by_dve)
                for gr in range(NT + 2):
                    if last_of[gr] + LAG_V - 1 == n:
                        weights(gr)
                    if last_of[gr] + LAG_V == n:
                        weigh(gr)
            dve.wait_ge(ot_done, GQA + 1)
            src = ps[:, 4, 0:256].rearrange("p (b i t) -> p b i t", b=B, i=4)
            for i in range(GQA):
                dve.tensor_copy(k.oT[:, 4 + i, SEQ:TOK].rearrange("p (b t) -> p b t", b=B), src[:, :, i, :])


class Norm:

    def __init__(self, k, name, row, eps, ctx, on_pool):
        self.k, self.eps, self.on_pool = k, eps, on_pool
        sem = k.sem
        self.summed, self.rstd_ready = sem(name + "_stats"), sem(name + "_rstd")
        self.scaled = sem(name + "_scaled")
        self.by_pool, self.by_dve = sem(name + "_ready_by_pool"), sem(name + "_ready_by_dve")
        self.t_done, self.t_out, self.vec_in = sem(name + "_t_done"), sem(name + "_t_out"), sem(name + "_vec_in")
        nc = k.nc
        self.vec = ctx.enter_context(nc.sbuf_tensor(name + "_gb", [128, 2, D], F32))
        self.st = ctx.enter_context(nc.sbuf_tensor(name + "_st", [128, NTT, 2, 6], F32))
        self.mv = ctx.enter_context(nc.sbuf_tensor(name + "_mv", [128, NTT, 2], F32))
        self.rs = ctx.enter_context(nc.sbuf_tensor(name + "_rs", [128, NTT], F32))
        self.nb = ctx.enter_context(nc.sbuf_tensor(name + "_shift", [128, NTT], F32))
        self.normed = sem(name + "_normed")
        self.row = row

    def wait_ready(self, eng, i):
        if i < self.on_pool:
            eng.wait_ge(self.by_pool, i + 1)
        else:
            eng.wait_ge(self.by_dve, i - self.on_pool + 1)

    def load(self, eng):
        src = self.k.io["ln"][self.k.layer, self.row:self.row + 2, :].unsqueeze(0).broadcast_to([128, 2, D])
        eng.dma_start(self.vec[:, :, :], src).then_inc(self.vec_in, 16)

    def stats(self, dve, i):
        k, rows = self.k, TILES[i]
        for n in range(2):
            last = dve.bn_stats(self.st[0:rows, i, n, :], k.x[0:rows, i, n * 512:(n + 1) * 512])
        k.dve.after(last)
        dve.bn_aggr(self.mv[0:rows, i, :], self.st[0:rows, i, :, :].rearrange("p a s -> p (a s)")).then_inc(self.summed, 1)

    def rstd(self, pool, i):
        rows = TILES[i]
        pool.wait_ge(self.summed, i + 1)
        r = self.rs[0:rows, i:i + 1]
        self.k.pool.after(pool.tensor_scalar(r, self.mv[0:rows, i, 1:2], self.eps, None, ALU.add))
        self.k.pool.after(pool.tensor_tensor(r, r, self.k.c["mhalf"][0:rows, 0:1], ALU.pow))
        nb = self.nb[0:rows, i:i + 1]
        self.k.pool.after(pool.tensor_tensor(nb, self.mv[0:rows, i, 0:1], r, ALU.mult))
        pool.tensor_scalar(nb, nb, -1.0, None, ALU.mult).then_inc(self.rstd_ready, 1)

    def normalise(self, act, i):
        rows = TILES[i]
        x = self.k.x[0:rows, i, :]
        act.wait_ge(self.rstd_ready, i + 1)
        act.activation(x, x, ACT.Identity, scale=self.rs[0:rows, i:i + 1], bias=self.nb[0:rows, i:i + 1]
                       ).then_inc(self.normed, 1)

    def scale(self, dve, i):
        k, rows = self.k, TILES[i]
        x = k.x[0:rows, i, :]
        if i == 0:
            dve.wait_ge(self.vec_in, 16)
        dve.wait_ge(self.normed, i + 1)
        dve.tensor_tensor(x, x, self.vec[0:rows, 0, :], ALU.mult).then_inc(self.scaled, 1)
        if i >= self.on_pool:
            dve.wait_ge(self.scaled, i + 1)
            dve.tensor_tensor(x, x, self.vec[0:rows, 1, :], ALU.add).then_inc(self.by_dve, 1)

    def shift(self, pool, i):
        k, rows = self.k, TILES[i]
        if i >= self.on_pool:
            return
        x = k.x[0:rows, i, :]
        pool.wait_ge(self.scaled, i + 1)
        pool.tensor_tensor(x, x, self.vec[0:rows, 1, :], ALU.add).then_inc(self.by_pool, 1)

    def transposes(self, pe, i):
        k, rows = self.k, TILES[i]
        self.wait_ready(pe, i)
        if i:
            pe.wait_ge(self.t_out, i)
        for kk in range(KT_D):
            last = pe.transpose(k.ps[:, 6 + kk // 4, kk % 4 * 128:kk % 4 * 128 + rows],
                                k.x[0:rows, i, kk * 128:(kk + 1) * 128], k.ident[0:rows, 0:rows])
        last.then_inc(self.t_done, 1)

    def copies(self, act, i):
        k, rows = self.k, TILES[i]
        act.wait_ge(self.t_done, i + 1)
        for h in range(2):
            last = act.copy(k.xT[:, 4 * h:4 * h + 4, i * 128:i * 128 + rows],
                            k.ps[:, 6 + h, :].rearrange("p (a t) -> p a t", a=4)[:, :, 0:rows])
        last.then_inc(self.t_out, 1)


def merge(k):
    nc, io, l, ps = k.nc, k.io, k.layer, k.ps
    sem = k.sem
    RING, HRING = 4, 3
    HALF = D // 2
    w_in, wo_in = [sem(f"w_in{n}") for n in range(RING)], [sem(f"wo_in{n}") for n in range(4)]
    x_hi, x_lo, w_hi, w_lo = sem("x_high_ready"), sem("x_low_ready"), sem("w_high_ready"), sem("w_low_ready")
    m_hi, m_lo, wo_hi, wo_lo = sem("merged_high"), sem("merged_low"), sem("wo_high"), sem("wo_low")
    unit_done, g_ready, b_out, merged = sem("unit_done"), sem("gate_ready"), sem("branch_out"), sem("merged")
    m_done, m_out, x1_stored = sem("mix_product_done"), sem("mix_product_out"), sem("x1_stored")
    k.x1_stored, k.lg_done = x1_stored, sem("logits_done")
    with ExitStack() as ctx:
        def sb(name, shape, dt=F32):
            return ctx.enter_context(nc.sbuf_tensor(name, shape, dt))
        w32, wl = two_types(nc, ctx, "w_ring", [128, RING, 1536])
        wh = sb("w_high", [128, HRING, 1536], F32R)
        xh = sb("xT_high", [128, KT_D, TOK], F32R)
        oh = sb("oT_high", [128, KT_D, TOK], F32R)
        mT, ml = two_types(nc, ctx, "mergedT", [128, KT_D, TOK])
        mh = sb("mergedT_high", [128, KT_D, TOK], F32R)
        tg = sb("tanh_gate", [128, 2, TOK])
        part = sb("branch_part", [128, TOK])
        wo32 = k.oT[:, :, 0:HALF]
        wol = k.oT_low[:, :, 0:HALF]
        woh = oh[:, :, 0:HALF]
        norm = Norm(k, "ln1", 0, 4 * EPS, ctx, 0)
        block = ctx.enter_context(nc.Block())
        TILE_OF = ((0, 1), (2, 3), (4, 5, 6, 7))
        TH = TOK // 2
        HALVES = (slice(0, TH), slice(TH, TOK))
        UNIT_AT = (0, 1280, 2560, 4096)
        NG_ = KT_D * 3
        NU = NG_ + 4
        width = [UNIT_AT[u % 3 + 1] - UNIT_AT[u % 3] if u < NG_ else 2 * HALF for u in range(NU)]
        X_PARTS = (("x", 0, 4), ("x", 4, 8), ("o", 0, 2), ("o", 2, 4), ("o", 4, 8))

        @block.sync
        def _(sp):
            for u in range(NU):
                if u >= RING:
                    sp.wait_ge(unit_done, u - RING + 1)
                dst = w32[:, u % RING, 0:width[u]]
                if u < NG_:
                    sp.dma_start(dst, io["wm"][l, u // 3, :, UNIT_AT[u % 3]:UNIT_AT[u % 3 + 1]]).then_inc(w_in[u % RING], 16)
                else:
                    kk = 2 * (u - NG_)
                    sp.dma_start(dst.rearrange("p (k n) -> p k n", k=2), io["wo"][l, :, kk:kk + 2, 0:HALF]
                                 ).then_inc(w_in[u % RING], 16)
            sp.wait_ge(unit_done, NG_)
            for q in range(4):
                sp.dma_start(wo32[:, 2 * q:2 * q + 2, :], io["wo"][l, :, 2 * q:2 * q + 2, HALF:D]).then_inc(wo_in[q], 16)
            norm.load(sp)
            for i, rows in enumerate(TILES):
                norm.wait_ready(sp, i)
                sp.dma_start(io["x1"][i * 128:i * 128 + rows, :], k.x[0:rows, i, :]).then_inc(x1_stored, 16)

        @block.tensor
        def _(pe):
            def product(out, w, x, first, last):
                pe.matmul(out, w[0], x[0], start=first, stop=False)
                pe.matmul(out, w[0], x[1], start=False, stop=False)
                return pe.matmul(out, w[1], x[0], start=False, stop=last)

            def parts(x, xl, kk, cols):
                return x[:, kk, cols], xl[:, kk, cols]
            for u in range(NG_):
                b, base = u % 3, 4 * (u % 2)
                pe.wait_ge(w_lo, u + 1)
                if u >= 2:
                    pe.wait_ge(b_out, u - 1)

                def w(kk):
                    return wh[:, u % HRING, kk * 128:(kk + 1) * 128], wl[:, u % RING, kk * 128:(kk + 1) * 128]
                for half, cols in enumerate(HALVES):
                    for kk in range(KT_D):
                        if u == 0 and kk % 4 == 0:
                            pe.wait_ge(x_lo, kk // 4 + 1)
                        product(ps[:, base + half, 0:TH], w(kk), parts(xh, k.xT_low, kk, cols), kk == 0, kk == KT_D - 1)
                ks = TILE_OF[b]
                if u < 3:
                    pe.wait_ge(x_lo, 3 + u)
                for half, cols in enumerate(HALVES):
                    for n, kk in enumerate(ks):
                        last = product(ps[:, base + 2 + half, 0:TH], w(KT_D + n), parts(oh, k.oT_low, kk, cols), n == 0, n == len(ks) - 1)
                last.then_inc(unit_done, 1)
            pe.wait_ge(b_out, NG_)
            for q in range(4):
                u = NG_ + q
                pe.wait_ge(w_lo, u + 1)
                pe.wait_ge(m_lo, 2 * q + 2)
                for i, rows in enumerate(TILES):
                    for a in range(2):
                        kk, cols = 2 * q + a, slice(i * 128, i * 128 + rows)
                        wsl = slice(a * HALF, (a + 1) * HALF)
                        last = product(ps[0:rows, i, :], parts(mh, ml, kk, cols), (wh[:, u % HRING, wsl], wl[:, u % RING, wsl]),
                                       kk == 0, kk == KT_D - 1)
                last.then_inc(unit_done, 1)
            def logits(i):
                rows = TILES[i]
                pe.wait_ge(norm.t_out, i + 1)
                if i == 0:
                    pe.wait_ge(m_out, NTT)
                for kk in range(KT_D):
                    last = pe.matmul(ps[0:rows, LOGITS, i * E:(i + 1) * E], k.xT[:, kk, i * 128:i * 128 + rows],
                                     k.wr[:, kk, :], start=(kk == 0), stop=(kk == KT_D - 1))
                last.then_inc(k.lg_done, 1)
            for i in range(NTT + 2):
                if i < NTT:
                    rows = TILES[i]
                    if i:
                        pe.wait_ge(m_out, i)
                    for kk in range(KT_D):
                        if i == 0 and kk % 2 == 0:
                            pe.wait_ge(wo_lo, kk // 2 + 1)
                        last = product(ps[0:rows, (i + 5) % 6, :], parts(mh, ml, kk, slice(i * 128, i * 128 + rows)),
                                       (woh[:, kk, :], wol[:, kk, :]), kk == 0, kk == KT_D - 1)
                    last.then_inc(m_done, 1)
                if i >= 2:
                    norm.transposes(pe, i - 2)
                if i >= 3:
                    logits(i - 3)
            logits(NTT - 1)

        @block.scalar
        def _(act):
            def x_high(n):
                what, lo, hi = X_PARTS[n]
                src, dst = (k.xT, xh) if what == "x" else (k.oT, oh)
                act.copy(dst[:, lo:hi, :], src[:, lo:hi, :]).then_inc(x_hi, 1)

            def w_high(u):
                act.wait_ge(w_in[u % RING], 16 * (u // RING + 1))
                if u >= HRING:
                    act.wait_ge(unit_done, u - HRING + 1)
                act.copy(wh[:, u % HRING, 0:width[u]], w32[:, u % RING, 0:width[u]]).then_inc(w_hi, 1)

            def m_high(m):
                act.wait_ge(merged, m + 1)
                act.copy(mh[:, m, :], mT[:, m, :]).then_inc(m_hi, 1)
            x_high(0)
            w_high(0)
            x_high(1)
            x_high(2)
            w_high(1)
            x_high(3)
            x_high(4)
            for u in range(NG_):
                base = 4 * (u % 2)
                w_high(u + 2)
                act.wait_ge(unit_done, u + 1)
                if u >= 2:
                    act.wait_ge(b_out, u - 1)
                act.activation(tg[:, u % 2, :].rearrange("p (a t) -> p a t", a=2), ps[:, base:base + 2, 0:TH],
                               ACT.Tanh, scale=0.5).then_inc(g_ready, 1)
                if u >= 3 and u % 3 == 0:
                    m_high(u // 3 - 1)
            m_high(KT_D - 1)
            w_high(NG_ + 2)
            w_high(NG_ + 3)
            for q in range(4):
                act.wait_ge(wo_in[q], 16)
                act.copy(woh[:, 2 * q:2 * q + 2, :], wo32[:, 2 * q:2 * q + 2, :]).then_inc(wo_hi, 1)
            for i in range(NTT + 2):
                if i < NTT:
                    norm.normalise(act, i)
                if i >= 2:
                    norm.copies(act, i - 2)

        @block.vector
        def _(dve):
            def rest(low, src, high):
                return dve.tensor_tensor(low, src, high.bitcast(F32), ALU.subtract)

            def x_low(n):
                what, lo, hi = X_PARTS[n]
                low, src, high = (k.xT_low, k.xT, xh) if what == "x" else (k.oT_low, k.oT, oh)
                dve.wait_ge(x_hi, n + 1)
                rest(low[:, lo:hi, :], src[:, lo:hi, :], high[:, lo:hi, :]).then_inc(x_lo, 1)

            def w_low(u):
                dve.wait_ge(w_hi, u + 1)
                rest(wl[:, u % RING, 0:width[u]], w32[:, u % RING, 0:width[u]], wh[:, u % HRING, 0:width[u]]).then_inc(w_lo, 1)

            def m_low(m):
                dve.wait_ge(m_hi, m + 1)
                rest(ml[:, m, :], mT[:, m, :], mh[:, m, :]).then_inc(m_lo, 1)
            x_low(0)
            w_low(0)
            x_low(1)
            x_low(2)
            w_low(1)
            x_low(3)
            x_low(4)
            for u in range(NG_):
                m, b, base = u // 3, u % 3, 4 * (u % 2)
                w_low(u + 2)
                dve.wait_ge(g_ready, u + 1)
                dst = (mT[:, m, :] if b == 0 else part[:, :]).rearrange("p (a t) -> p a t", a=2)
                dve.scalar_tensor_tensor(dst, tg[:, u % 2, :].rearrange("p (a t) -> p a t", a=2), 1.0,
                                         ps[:, base + 2:base + 4, 0:TH], ALU.add, ALU.mult).then_inc(b_out, 1)
                if b:
                    dve.wait_ge(b_out, u + 1)
                    last = dve.tensor_tensor(mT[:, m, :], mT[:, m, :], part[:, :], ALU.add)
                    if b == 1:
                        k.dve.after(last)
                    else:
                        last.then_inc(merged, 1)
                        dve.wait_ge(merged, m + 1)
                if u >= 3 and b == 0:
                    m_low(m - 1)
            m_low(KT_D - 1)
            w_low(NG_ + 2)
            w_low(NG_ + 3)
            for q in range(4):
                dve.wait_ge(wo_hi, q + 1)
                rest(wol[:, 2 * q:2 * q + 2, :], wo32[:, 2 * q:2 * q + 2, :], woh[:, 2 * q:2 * q + 2, :]).then_inc(wo_lo, 1)
            dve.wait_ge(k.x_in, 32)
            dve.wait_ge(unit_done, NU)
            for i, rows in enumerate(TILES):
                xs = k.x[0:rows, i, 0:HALF]
                dve.scalar_tensor_tensor(xs, xs, 2 * ALPHA, ps[0:rows, i, :], ALU.mult, ALU.add).then_inc(m_out, 1)
            for i in range(NTT + 1):
                if i < NTT:
                    rows = TILES[i]
                    dve.wait_ge(m_done, i + 1)
                    xs = k.x[0:rows, i, HALF:D]
                    dve.scalar_tensor_tensor(xs, xs, 2 * ALPHA, ps[0:rows, (i + 5) % 6, :], ALU.mult, ALU.add).then_inc(m_out, 1)
                    dve.wait_ge(m_out, NTT + i + 1)
                    norm.stats(dve, i)
                if i:
                    norm.scale(dve, i - 1)

        @block.gpsimd
        def _(pool):
            for i in range(NTT + 1):
                if i < NTT:
                    norm.rstd(pool, i)
                if i:
                    norm.shift(pool, i - 1)


def experts(k):
    nc, io, l, ps, c = k.nc, k.io, k.layer, k.ps, k.c
    sem = k.sem
    ex_ready, sel_ready, rank_done = sem("exp_ready"), sem("choice_ready"), sem("rank_done")
    plan_ready, ex_clear = sem("plan_ready"), sem("exp_cleared")
    lanes_ready, table_done, table_ready = sem("lanes_ready"), sem("slot_table_done"), sem("slot_table_ready")
    gu_in = [sem("gate_up_in_a"), sem("gate_up_in_b")]
    dw_in = [sem("down_in_a"), sem("down_in_b")]
    idx_ready, x_in = sem("idx_ready"), [sem("rows_in_a"), sem("rows_in_b")]
    xt_done, xt_act, xt_dve = sem("rowsT_done"), sem("rowsT_by_act"), sem("rowsT_by_dve")
    gu_done, act_ready = sem("gate_up_done"), sem("hidden_ready")
    tanh_ready2 = [sem("silu_ready_a"), sem("silu_ready_b")]
    tanh_ready, at_done, at_out = sem("gate_tanh_ready"), sem("hiddenT_done"), sem("hiddenT_out")
    dn_done = [sem("down_done_a"), sem("down_done_b")]
    y_act, y_dve, y_stored = sem("y_by_act"), sem("y_by_dve"), [sem("y_stored_a"), sem("y_stored_b")]
    x_stored = sem("layer_output_stored")
    all_stored = sem("all_expert_rows_stored")
    yg_in, y_added = [sem(f"y_rows_in{i}") for i in range(NTT)], sem("y_rows_added")

    with ExitStack() as outer:
        def so(name, shape, dt=F32):
            return outer.enter_context(nc.sbuf_tensor(name, shape, dt))
        norm = Norm(k, "ln2", 2, EPS, outer, NTT - 1)
        slot = so("slot", [128, 2, NTT], I32)
        wt = so("pair_weight", [128, 2, NTT])
        plan = so("plan", [1, 34], I32)
        with ExitStack() as ctx:
            def sb(name, shape, dt=F32):
                return ctx.enter_context(nc.sbuf_tensor(name, shape, dt))
            S3 = [128, NTT, E]
            ex, aff, score, ms, t1 = sb("ex", S3), sb("aff", S3), sb("score", S3), sb("ms", S3), sb("rt1", S3)
            oh = sb("onehot", [128, 2, NTT, E])
            both = sb("both", S3)
            g = sb("grp", [128, 8, NTT, EG])
            v = sb("rv", [128, 4, NTT])
            cnt, nch, cum, basev = sb("cnt", [128, E]), sb("nch", [128, E]), sb("cum", [128, E]), sb("base", [128, E])
            big = sb("cmpbuf", [128, 32, E])
            pf = sb("plan_f", [1, 34])
            slotf = sb("slot_f", [128, 2, NTT])
            gu = [sb("gate_up_a", [128, 4096]), sb("gate_up_b", [128, 4096])]
            dw = [sb("down_a", [128, 2048]), sb("down_b", [128, 2048])]
            ge = sb("slot_ge", [128, 2 * NTT, MAXCH + 3])
            C = sb("slot_chunk", [128, 2 * NTT, MAXCH + 2])
            R = sb("slot_lane", [128, 2 * NTT, 128])
            lane = sb("lane", [128, 2, NTT])
            table = sb("slot_table", [128, MAXCH + 2], I32)
            idx = [sb("idx_a", [128, 1], I32), sb("idx_b", [128, 1], I32)]
            xg = [sb("rows_a", [128, D]), sb("rows_b", [128, D])]
            xgT = [sb("rowsT_a", [128, KT_D, 128]), sb("rowsT_b", [128, KT_D, 128])]
            tgt = [sb("gtanh_a", [128, FE]), sb("gtanh_b", [128, FE])]
            h1 = [sb("hid_a", [128, FE]), sb("hid_b", [128, FE])]
            hT = [sb("hidT_a", [128, 2, 128]), sb("hidT_b", [128, 2, 128])]
            y = [sb("y_a", [128, D]), sb("y_b", [128, D])]
            block = ctx.enter_context(nc.Block())
            XB, GB, YB = [0, 2], [4, 5], [6, 0]

            def pairs(eng):
                eng.wait_ge(plan_ready, 1)
                return eng.value_load(plan[0:1, 32:33], min_val=1, max_val=MAXCH // 2)

            @block.sync
            def _(sp):
                norm.load(sp)
                with sp.Fori(0, pairs(sp)) as p:
                    e = [sp.value_load(plan[0:1, bass.ds(2 * p + a, 1)], min_val=0, max_val=E - 1) for a in range(2)]
                    for a in range(2):
                        sp.wait_ge(gu_done, 2 * p + a + 1)
                        sp.dma_start(gu[a][:, :], io["we"][l, e[a], :, 0:4096]).then_inc(gu_in[a], 16)
                    for a in range(2):
                        sp.wait_ge(dn_done[a], p + 1)
                        sp.dma_start(dw[a][:, :], io["we"][l, e[a], :, 4096:6144]).then_inc(dw_in[a], 16)

            @block.tensor
            def _(pe):
                pe.wait_ge(sel_ready, 1)
                flat = both[:, :, :].rearrange("p i e -> p (i e)")
                pe.matmul(ps[:, 1, 0:NTT * E], c["tri"], flat, start=True, stop=False, skip_group_check=True)
                for d in range(1, NTT):
                    pe.matmul(ps[:, 1, d * E:NTT * E], c["ones"], flat[:, 0:(NTT - d) * E], start=False,
                              stop=(d == NTT - 1), skip_group_check=True)
                for j, rows in enumerate(TILES):
                    last = pe.matmul(ps[:, 1, NTT * E:(NTT + 1) * E], c["ones"][0:rows, :], both[0:rows, j, :],
                                     start=(j == 0), stop=(j == NTT - 1), skip_group_check=True)
                last.then_inc(rank_done, 1)
                pe.wait_ge(lanes_ready, 1)
                for n in range(2 * NTT):
                    rows = TILES[n % NTT]
                    last = pe.matmul(ps[:, 6, 0:MAXCH + 2], R[0:rows, n, :], C[0:rows, n, :],
                                     start=(n == 0), stop=(n == 2 * NTT - 1))
                last.then_inc(table_done, 1)
                for s in (dn_done[0], dn_done[1]):
                    pe.sem_inc(s, 1)
                for s in (xt_done, gu_done):
                    pe.sem_inc(s, 2)

                def rows_t(a):
                    for kk in range(KT_D):
                        last = pe.transpose(ps[:, XB[a] + kk // 4, kk % 4 * 128:(kk % 4 + 1) * 128],
                                            xg[a][:, kk * 128:(kk + 1) * 128], k.ident)
                    last.then_inc(xt_done, 1)
                for a in range(2):
                    pe.wait_ge(x_in[a], 16)
                    rows_t(a)
                with pe.Fori(0, pairs(pe)) as p:
                    for a in range(2):
                        pe.wait_ge(gu_in[a], 16 * p + 16)
                        pe.wait_ge(xt_act, 2 * p + a + 1)
                        pe.wait_ge(xt_dve, 2 * p + a + 1)
                        for kk in range(KT_D):
                            last = pe.matmul(ps[:, GB[a], :], xgT[a][:, kk, :], gu[a][:, kk * 512:(kk + 1) * 512],
                                             start=(kk == 0), stop=(kk == KT_D - 1))
                        last.then_inc(gu_done, 1)
                    for a in range(2):
                        pe.wait_ge(act_ready, 2 * p + a + 1)
                        for f in range(2):
                            last = pe.transpose(ps[:, GB[a], f * 128:(f + 1) * 128], h1[a][:, f * 128:(f + 1) * 128], k.ident)
                        last.then_inc(at_done, 1)
                        pe.wait_ge(x_in[a], 16 * p + 32)
                        if a == 0:
                            pe.wait_ge(y_act, 2 * p + 1)
                            pe.wait_ge(y_dve, 2 * p + 1)
                        rows_t(a)
                        pe.wait_ge(at_out, 2 * p + a + 1)
                        pe.wait_ge(dw_in[a], 16 * p + 16)
                        if a == 1:
                            pe.wait_ge(xt_act, 2 * p + 3)
                            pe.wait_ge(xt_dve, 2 * p + 3)
                        for n in range(2):
                            for f in range(2):
                                last = pe.matmul(ps[:, YB[a] + n, :], hT[a][:, f, :],
                                                 dw[a][:, f * D + n * 512:f * D + (n + 1) * 512],
                                                 start=(f == 0), stop=(f == 1))
                        last.then_inc(dn_done[a], 1)

            @block.scalar
            def _(act):
                act.wait_ge(k.lg_done, NTT)
                act.wait_ge(ex_clear, 1)
                act.activation(ex[:, 0:NT, :], ps[:, LOGITS, 0:NT * E].rearrange("p (i e) -> p i e", i=NT), ACT.Exp, scale=-1.0)
                act.activation(ex[0:NS, NT, :], ps[0:NS, LOGITS, NT * E:NTT * E], ACT.Exp, scale=-1.0).then_inc(ex_ready, 1)
                act.sem_inc(y_act, 1)
                for s in y_stored:
                    act.sem_inc(s, 16)
                act.wait_ge(k.rows_cleared, 16 * (MAXCH // 2 + 1))

                def rows_copy(a):
                    act.copy(xgT[a][:, 0:4, :], ps[:, XB[a], :].rearrange("p (a t) -> p a t", a=4)).then_inc(xt_act, 1)
                for a in range(2):
                    act.wait_ge(xt_done, 2 + a + 1)
                    rows_copy(a)
                with act.Fori(0, pairs(act)) as p:
                    for a in range(2):
                        act.wait_ge(gu_done, 2 * p + a + 3)
                        act.activation(tgt[a][:, :], ps[:, GB[a], 0:FE], ACT.Tanh, scale=0.5).then_inc(tanh_ready, 1)

                    def hidden_copy(a):
                        act.wait_ge(at_done, 2 * p + a + 1)
                        act.copy(hT[a][:, :, :], ps[:, GB[a], 0:256].rearrange("p (a t) -> p a t", a=2)).then_inc(at_out, 1)

                    def next_rows_copy(a):
                        act.wait_ge(xt_done, 2 * p + a + 5)
                        rows_copy(a)

                    def output_copy(a):
                        act.wait_ge(dn_done[a], p + 2)
                        act.wait_ge(y_stored[a], 16 * p + 16)
                        act.copy(y[a][:, 0:512], ps[:, YB[a], :]).then_inc(y_act, 1)

                    def store(a):
                        act.wait_ge(y_act, 2 * p + a + 2)
                        act.wait_ge(y_dve, 2 * p + a + 2)
                        act.dma_start(io["ys"][bass.ds((2 * p + a) * 128, 128), :], y[a][:, :]).then_inc(y_stored[a], 16)
                    hidden_copy(0)
                    next_rows_copy(0)
                    hidden_copy(1)
                    output_copy(0)
                    next_rows_copy(1)
                    store(0)
                    output_copy(1)
                    store(1)

            @block.gpsimd
            def _(pool):
                pool.wait_ge(k.x1_stored, 16 * NTT)
                for i, rows in enumerate(TILES):
                    k.pool.after(pool.tensor_scalar(k.x[0:rows, i, :], k.x[0:rows, i, :], ALPHA, None, ALU.mult))
                pool.wait_ge(table_ready, 1)

                def gather(a, chunk):
                    pool.tensor_copy(idx[a][:, :], table[:, chunk]).then_inc(idx_ready, 1)
                    pool.wait_ge(idx_ready, 1)
                    pool.sem_clear(idx_ready)
                    pool.indirect_dma_start(xg[a][:, :], None, io["x1"], bass.IndirectOffsetOnAxis(idx[a][:, 0:1], 0)
                                            ).then_inc(x_in[a], 16)
                for a in range(2):
                    gather(a, slice(a, a + 1))
                with pool.Fori(0, pairs(pool)) as p:
                    for a in range(2):
                        pool.wait_ge(xt_done, 2 * p + a + 3)
                        gather(a, bass.ds(2 * p + a + 2, 1))

            @block.vector
            def _(dve):
                step = k.dve.after
                dve.memset(ex[:, :, :], 1.0).then_inc(ex_clear, 1)
                dve.memset(g[:, :, :, :], 0.0)
                dve.wait_ge(ex_ready, 1)
                step(dve.tensor_scalar(aff[:, :, :], ex[:, :, :], 1.0, None, ALU.add))
                step(dve.reciprocal(aff[:, :, :], aff[:, :, :]))
                step(dve.tensor_tensor(score[:, :, :], aff[:, :, :], k.br[:, :].unsqueeze(1).broadcast_to(S3), ALU.add))
                s4 = score[:, :, :].rearrange("p i (g e) -> p i g e", g=EG)
                G = [g[:, n, :, :] for n in range(8)]
                step(dve.tensor_tensor(G[0], s4[:, :, :, 0], s4[:, :, :, 1], ALU.max))
                step(dve.tensor_tensor(G[1], s4[:, :, :, 0], s4[:, :, :, 1], ALU.min))
                step(dve.tensor_tensor(G[2], s4[:, :, :, 2], s4[:, :, :, 3], ALU.max))
                step(dve.tensor_tensor(G[3], s4[:, :, :, 2], s4[:, :, :, 3], ALU.min))
                step(dve.tensor_tensor(G[4], G[0], G[2], ALU.max))
                step(dve.tensor_tensor(G[5], G[0], G[2], ALU.min))
                step(dve.tensor_tensor(G[6], G[1], G[3], ALU.max))
                step(dve.tensor_tensor(G[5], G[5], G[6], ALU.max))
                step(dve.tensor_tensor(G[4], G[4], G[5], ALU.add))

                def first_best(val, out, order, width, tmp):
                    shape = [128, NTT, width]
                    step(dve.tensor_reduce(v[:, 0, :], val, AX.X, ALU.max))
                    step(dve.tensor_tensor(tmp, val, v[:, 0, :].unsqueeze(2).broadcast_to(shape), ALU.is_equal))
                    step(dve.tensor_tensor(tmp, tmp, order.unsqueeze(1).broadcast_to(shape), ALU.mult))
                    step(dve.tensor_reduce(v[:, 1, :], tmp, AX.X, ALU.max))
                    step(dve.tensor_tensor(out, tmp, v[:, 1, :].unsqueeze(2).broadcast_to(shape), ALU.is_equal))

                first_best(G[4], G[0], c["g4"], EG, G[1])
                step(dve.tensor_scalar(G[1], G[0], 1.0, -NEG, ALU.subtract, ALU.mult))
                ms4 = ms[:, :, :].rearrange("p i (g e) -> p i g e", g=EG)
                S4 = [128, NTT, EG, E // EG]
                step(dve.tensor_tensor(ms4, s4, G[0].unsqueeze(3).broadcast_to(S4), ALU.mult))
                step(dve.tensor_tensor(ms4, ms4, G[1].unsqueeze(3).broadcast_to(S4), ALU.add))
                first_best(ms[:, :, :], oh[:, 0, :, :], c["e16"], E, t1[:, :, :])
                step(dve.tensor_scalar(t1[:, :, :], oh[:, 0, :, :], 3 * NEG, None, ALU.mult))
                step(dve.tensor_tensor(ms[:, :, :], ms[:, :, :], t1[:, :, :], ALU.add))
                first_best(ms[:, :, :], oh[:, 1, :, :], c["e16"], E, t1[:, :, :])
                dve.tensor_tensor(both[:, :, :], oh[:, 0, :, :], oh[:, 1, :, :], ALU.add).then_inc(sel_ready, 1)
                for a in range(2):
                    step(dve.tensor_tensor(t1[:, :, :], oh[:, a, :, :], aff[:, :, :], ALU.mult))
                    step(dve.tensor_reduce(v[:, a, :], t1[:, :, :], AX.X, ALU.add))
                step(dve.tensor_tensor(v[:, 2, :], v[:, 0, :], v[:, 1, :], ALU.add))
                step(dve.reciprocal(v[:, 2, :], v[:, 2, :]))
                step(dve.tensor_scalar(v[:, 2, :], v[:, 2, :], 0.5, None, ALU.mult))
                step(dve.tensor_tensor(wt[:, :, :], v[:, 0:2, :], v[:, 2, :].unsqueeze(1).broadcast_to([128, 2, NTT]), ALU.mult))
                dve.wait_ge(rank_done, 1)
                step(dve.tensor_copy(cnt[:, :], ps[:, 1, NTT * E:(NTT + 1) * E]))
                step(dve.tensor_tensor(big[:, 0:5, :], cnt[:, :].unsqueeze(1).broadcast_to([128, 5, E]),
                                       c["th"].unsqueeze(2).broadcast_to([128, 5, E]), ALU.is_gt))
                step(dve.tensor_reduce(nch[:, :], big[:, 0:5, :].rearrange("p m e -> p e m"), AX.X, ALU.add))
                step(dve.tensor_tensor_scan(cum[:, :], c["ones"][:, 0:E], nch[:, :], 0.0, ALU.mult, ALU.add))
                step(dve.tensor_tensor(basev[:, :], cum[:, :], nch[:, :], ALU.subtract))
                step(dve.tensor_scalar(basev[:, :], basev[:, :], 128.0, None, ALU.mult))
                step(dve.tensor_copy(t1[:, :, :], basev[:, :].unsqueeze(1).broadcast_to(S3)))
                step(dve.tensor_tensor(t1[:, 0:NT, :], ps[:, 1, 0:NT * E].rearrange("p (i e) -> p i e", i=NT),
                                       t1[:, 0:NT, :], ALU.add))
                step(dve.tensor_tensor(t1[0:NS, NT, :], ps[0:NS, 1, NT * E:NTT * E], t1[0:NS, NT, :], ALU.add))
                for a in range(2):
                    step(dve.tensor_tensor(ms[:, :, :], t1[:, :, :], oh[:, a, :, :], ALU.mult))
                    step(dve.tensor_reduce(slotf[:, a, :], ms[:, :, :], AX.X, ALU.add))
                dve.tensor_copy(slot[:, :, :], slotf[:, :, :])
                n2 = 2 * NTT
                s2 = slotf[:, :, :].rearrange("p a i -> p (a i)")
                ln = lane[:, :, :].rearrange("p a i -> p (a i)")
                step(dve.tensor_scalar(ln, s2, 1 / 128, None, ALU.mult))
                step(dve.tensor_tensor(ge[:, :, :], ln.unsqueeze(2).broadcast_to([128, n2, MAXCH + 3]),
                                       c["chunk"][:, 0:MAXCH + 3].unsqueeze(1).broadcast_to([128, n2, MAXCH + 3]), ALU.is_ge))
                step(dve.tensor_reduce(ln, ge[:, :, 1:MAXCH + 3], AX.X, ALU.add))
                step(dve.scalar_tensor_tensor(ln, ln, -128.0, s2, ALU.mult, ALU.add))
                dve.tensor_tensor(R[:, :, :], ln.unsqueeze(2).broadcast_to([128, n2, 128]),
                                  c["lane"].unsqueeze(1).broadcast_to([128, n2, 128]), ALU.is_equal)
                step(dve.tensor_tensor(C[:, :, :], ge[:, :, 0:MAXCH + 2], ge[:, :, 1:MAXCH + 3], ALU.subtract))
                c4 = C[:, :, :].rearrange("p (a i) c -> p a i c", a=2)
                for a in range(2):
                    last = dve.tensor_tensor(c4[:, a, :, :], c4[:, a, :, :],
                                             c["tok"].unsqueeze(2).broadcast_to([128, NTT, MAXCH + 2]), ALU.mult)
                last.then_inc(lanes_ready, 1)
                chunk = c["chunk"][0:1, :]
                step(dve.tensor_tensor(big[0:1, :, :], cum[0:1, :].unsqueeze(1).broadcast_to([1, 32, E]),
                                       chunk.unsqueeze(2).broadcast_to([1, 32, E]), ALU.is_le))
                step(dve.tensor_reduce(pf[:, 0:32], big[0:1, :, :], AX.X, ALU.add))
                step(dve.tensor_scalar(pf[:, 0:32], pf[:, 0:32], float(E - 1), None, ALU.min))
                dve.wait_ge(table_done, 1)
                dve.tensor_copy(table[:, :], ps[:, 6, 0:MAXCH + 2]).then_inc(table_ready, 1)
                step(dve.tensor_scalar(cum[0:1, 0:1], cum[0:1, E - 1:E], 0.5, None, ALU.mult))
                step(dve.tensor_tensor(big[0:1, :, 0], chunk, cum[0:1, 0:1].broadcast_to([1, 32]), ALU.is_lt))
                step(dve.tensor_reduce(pf[:, 32:33], big[0:1, :, 0], AX.X, ALU.add))
                step(dve.memset(pf[:, 33:34], 0.0))
                dve.tensor_copy(plan[:, :], pf[:, :]).then_inc(plan_ready, 1)
                dve.sem_inc(y_dve, 1)

                def rows_copy(a):
                    dve.tensor_copy(xgT[a][:, 4:8, :], ps[:, XB[a] + 1, :].rearrange("p (a t) -> p a t", a=4)).then_inc(xt_dve, 1)
                for a in range(2):
                    dve.wait_ge(xt_done, 2 + a + 1)
                    rows_copy(a)
                with dve.Fori(0, pairs(dve)) as p:
                    for a in range(2):
                        dve.wait_ge(tanh_ready, 2 * p + a + 1)
                        dve.scalar_tensor_tensor(tgt[a][:, :], tgt[a][:, :], 1.0, ps[:, GB[a], 0:FE],
                                                 ALU.add, ALU.mult).then_inc(tanh_ready2[a], 1)
                        dve.wait_ge(tanh_ready2[a], p + 1)
                        dve.tensor_tensor(h1[a][:, :], tgt[a][:, :], ps[:, GB[a], FE:2 * FE], ALU.mult).then_inc(act_ready, 1)
                    for a in range(2):
                        dve.wait_ge(xt_done, 2 * p + a + 5)
                        rows_copy(a)
                        dve.wait_ge(dn_done[a], p + 2)
                        dve.wait_ge(y_stored[a], 16 * p + 16)
                        dve.tensor_copy(y[a][:, 512:1024], ps[:, YB[a] + 1, :]).then_inc(y_dve, 1)

        with ExitStack() as ctx:
            yg = ctx.enter_context(nc.sbuf_tensor("y_rows", [128, NTT, 2, D], F32))
            block = ctx.enter_context(nc.Block())

            @block.gpsimd
            def _(pool):
                pool.wait_ge(all_stored, 1)

                def gather(i):
                    rows = TILES[i]
                    for a in range(2):
                        pool.indirect_dma_start(yg[0:rows, i, a, :], None, io["ys"],
                                                bass.IndirectOffsetOnAxis(slot[0:rows, a, i:i + 1], 0)).then_inc(yg_in[i], 16)
                AHEAD = 3
                for i in range(AHEAD):
                    gather(i)
                for i in range(NTT + 1):
                    if i < NTT:
                        norm.rstd(pool, i)
                    if i:
                        norm.shift(pool, i - 1)
                    if i + AHEAD < NTT:
                        gather(i + AHEAD)
                n = pool.value_load(plan[0:1, 32:33], min_val=1, max_val=MAXCH // 2)
                for a in range(2):
                    pool.wait_ge(x_in[a], 16 * n + 16)
                for i in range(NTT):
                    pool.wait_ge(yg_in[i], 32)
                pool.wait_ge(k.stored, 16 * k.n_stored)

            @block.vector
            def _(dve):
                for i in range(NTT + 1):
                    if i < NTT:
                        rows = TILES[i]
                        x = k.x[0:rows, i, :]
                        dve.wait_ge(yg_in[i], 32)
                        for a in range(2):
                            dve.scalar_tensor_tensor(x, yg[0:rows, i, a, :], wt[0:rows, a, i:i + 1], x,
                                                     ALU.mult, ALU.add).then_inc(y_added, 1)
                            dve.wait_ge(y_added, 2 * i + a + 1)
                        norm.stats(dve, i)
                    if i:
                        norm.scale(dve, i - 1)

            @block.tensor
            def _(pe):
                for i in range(NTT):
                    norm.transposes(pe, i)

            @block.scalar
            def _(act):
                for i in range(NTT + 2):
                    if i < NTT:
                        norm.normalise(act, i)
                    if i >= 2:
                        norm.copies(act, i - 2)

            @block.sync
            def _(sp):
                n = sp.value_load(plan[0:1, 32:33], min_val=1, max_val=MAXCH // 2)
                for a in range(2):
                    sp.wait_ge(y_stored[a], 16 * n + 16)
                sp.sem_inc(all_stored, 1)
                for i, rows in enumerate(TILES):
                    norm.wait_ready(sp, i)
                    out = io["y_p"][i * 128:(i + 1) * 128, :] if i < NT else io["y_s"]
                    sp.dma_start(out, k.x[0:rows, i, :]).then_inc(x_stored, 16)
                sp.wait_ge(x_stored, 16 * NTT)
                sp.wait_ge(k.stored, 16 * k.n_stored)



def layouts(inp):
    a = {n: np.asarray(v) for n, v in inp.items()}
    c = np.ascontiguousarray
    out = {}
    xp, xs = a["x_prompt"].reshape(SEQ, D), a["x_sample"].reshape(NS, D)
    out["xp"], out["xs"] = xp, xs
    out["x0T"] = c(np.concatenate([xp, xs], 0).T.reshape(KT_D, 128, TOK).transpose(1, 0, 2))
    out["consts"] = constants()
    out["page_table"] = a["page_table"].reshape(1, -1).astype(np.int32)
    out["w_router"] = a["w_router"]
    out["br"] = c(np.broadcast_to(a["b_router"], (128, E)))
    w = a["w_in"]
    pa, pu, pv, pq, pkv, pg, pm = (w[:, :, s:e] for s, e in ((0, 256), (256, 512), (512, 768), (768, 1280),
                                                             (1280, 2048), (2048, 2072), (2072, 5144)))
    pq = pq.reshape(L, D, NKV, GQA, HD).transpose(0, 1, 3, 2, 4).reshape(L, D, 512)
    tm = np.concatenate([pq, pkv, pa, pv, pg], 2)
    out["wtm"] = c(tm.reshape(L, KT_D, 128, NCH, CW).transpose(0, 3, 2, 1, 4))
    out["wu"] = c(pu.reshape(L, KT_D, 128, 256).transpose(0, 2, 1, 3))
    g = pm.reshape(L, KT_D, 128, 3, KT_D, 128).transpose(0, 4, 2, 3, 1, 5).reshape(L, KT_D, 128, 3, 1024)
    heads = a["w_branch_nsa"].reshape(L, NKV, GQA, HD, D).transpose(0, 2, 1, 3, 4).reshape(L, 4, 128, D)
    parts = []
    for b, br in enumerate((a["w_branch_pool"].reshape(L, 2, 128, D), a["w_branch_gmlp"].reshape(L, 2, 128, D), heads)):
        br = br.reshape(L, -1, 128, KT_D, 128).transpose(0, 3, 2, 1, 4).reshape(L, KT_D, 128, -1)
        parts += [g[:, :, :, b], br]
    out["wm"] = c(np.concatenate(parts, 3))
    out["wo"] = c(a["w_out"].reshape(L, KT_D, 128, D).transpose(0, 2, 1, 3))
    gu = np.concatenate([a["w_gate"], a["w_up"]], 3).reshape(L, E, KT_D, 128, 512).transpose(0, 1, 3, 2, 4)
    dn = a["w_down"].reshape(L, E, 2, 128, D).transpose(0, 1, 3, 2, 4)
    out["we"] = c(np.concatenate([gu.reshape(L, E, 128, 4096), dn.reshape(L, E, 128, 2048)], 3))
    out["w1"] = c(a["cmp_w1"].reshape(L, 2, CS, 2, HD, HID).transpose(0, 3, 4, 1, 2, 5).reshape(L, 128, 2, CS, HID))
    out["peT"] = c(a["cmp_pe"].reshape(L, 2, CS, 2, HD).transpose(0, 3, 4, 1, 2).reshape(L, 128, 2, CS))
    out["ln"] = c(np.stack([a["ln1_g"], a["ln1_b"], a["ln2_g"], a["ln2_b"]], 1))
    kv = a["cache_cmp_kv"].reshape(L, N_POOL, PAGE // 2, 2, 2, NKV, HD).transpose(0, 1, 3, 6, 5, 4, 2)
    out["cmp_pages"] = c(kv.reshape(L, N_POOL, 128, NKV, 2, PAGE // 2))

    def keys_and_values(rows):
        lead = rows.shape[:-4]
        kt = np.moveaxis(rows[..., 0, :, :], -3, -1).reshape(*lead, 128, 128)
        return np.concatenate([kt, rows[..., 1, :, :].reshape(*lead, 128, 128)], -1)
    out["sel_pages"] = c(keys_and_values(a["cache_sel_kv"]))
    win = a["state_win_kv"]
    out["win_rows"] = c(keys_and_values(win.reshape(L, B, 2, 128, 2, NKV, HD)).transpose(0, 3, 1, 2, 4))
    out["state_win"] = win.reshape(L, B, PAST, 256)
    out["state_pool"] = a["state_pool"]
    out["state_pool2"] = a["state_pool"].reshape(L, B * KEEP, 256)
    s = np.zeros((L, 128, NSMALL), np.float32)

    def put(name, v):
        lo, hi = _S[name]
        s[:, :v.shape[1], lo:hi] = v.reshape(L, v.shape[1], hi - lo)
    put("w2", a["cmp_w2"].transpose(0, 2, 1, 3))
    pw = np.zeros((L, 2, 2, 64, 2, 64), np.float32)
    for h in range(2):
        pw[:, :, h, :, h, :] = a["pool_w"].reshape(L, 2, 2, 64, 64)[:, :, h]
    put("poolw", pw.reshape(L, 2, 128, 128).transpose(0, 2, 1, 3))
    put("wsT", a["gmlp_ws"].transpose(0, 3, 1, 2))
    put("bsT", np.repeat(a["gmlp_bs"], 64, 1).reshape(L, 2, 128, 128).transpose(0, 2, 1, 3))
    put("pscale", a["pool_scale"].reshape(L, 2, 128).transpose(0, 2, 1))
    put("b1", a["cmp_b1"].transpose(0, 2, 1))
    put("wss", np.tile(a["gmlp_ws"][:, :, :TS, :TS].transpose(0, 3, 1, 2), (1, B, 1, 1)))
    put("vg", np.broadcast_to(a["gmlp_ln_g"][:, None], (L, 128, 256)))
    put("vb", np.broadcast_to(a["gmlp_ln_b"][:, None], (L, 128, 256)))
    out["small"] = s
    return out


_OUTS = [("y_p", (SEQ, D)), ("y_s", (NS, D)),
         ("o_cmp_p", (L, SEQ, 256)), ("o_sel_p", (L, SEQ, 256)), ("o_win_p", (L, SEQ, 256)), ("o_pool_p", (L, KEEP, 256)),
         ("o_cmp_s", (L, NS, 256)), ("o_sel_s", (L, NS, 256)), ("o_win_s", (L, B, PAST, 256)),
         ("o_pool_s", (L, B, KEEP, 256)), ("o_gmlp_s", (L, NS, 256))]


def kernel(**inputs):
    import concourse.bacc as _bacc
    from concourse.bass_utils import run_bass_kernel_spmd as _run

    arrays = layouts(inputs)
    nc = _bacc.Bacc("TRN2", target_bir_lowering=False, num_devices=1)
    io = {n: nc.dram_tensor("in_" + n, v.shape, mybir.dt.from_np(v.dtype), kind="ExternalInput").ap() for n, v in arrays.items()}
    for n, shape in _OUTS:
        io[n] = nc.dram_tensor("out_" + n, shape, F32, kind="ExternalOutput").ap()
    io["x1"] = nc.dram_tensor("x1_rows", (TOK, D), F32).ap()
    io["ys"] = nc.dram_tensor("expert_rows", (SLOTS, D), F32).ap()
    build(nc, io)
    r = _run(nc, [{"in_" + n: v for n, v in arrays.items()}], core_ids=[0]).results[0]
    r = {n: r["out_" + n] for n, _ in _OUTS}
    kv = (2, NKV, HD)
    return (r["y_p"].reshape(1, SEQ, D), r["y_s"].reshape(B, TS, D),
            r["o_cmp_p"].reshape(L, 1, SEQ, *kv), r["o_sel_p"].reshape(L, 1, SEQ, *kv), r["o_win_p"].reshape(L, 1, SEQ, *kv),
            r["o_pool_p"].reshape(L, 1, KEEP, 256),
            r["o_cmp_s"].reshape(L, B, TS, *kv), r["o_sel_s"].reshape(L, B, TS, *kv), r["o_win_s"].reshape(L, B, PAST, *kv),
            r["o_pool_s"], r["o_gmlp_s"].reshape(L, B, TS, 256))
```
